# Optimizing a Trainium2 kernel written in Bass

```python
import jax, jax.numpy as jnp
from jax import lax
import numpy as np

D_MODEL = 1024
BATCH = 1
SEQ = 512
DEPTH = 2

N_MIXERS = 2
EXPAND = 2
D_INNER = EXPAND * D_MODEL
HEAD_SIZE = 64
N_HEADS = D_INNER // HEAD_SIZE
LORA_DECAY = 64
LORA_A = 64
LORA_V = 32
N_LERP = 6
CONV_WIDTH = 3
N_RWKV = (DEPTH + 1) // 2
N_CONV = DEPTH // 2
RMS_EPS = 1e-6
GN_EPS = 64e-5
L2_EPS = 1e-12


def rms_norm(x, g):
    x32 = x.astype(jnp.float32)
    y = x32 * lax.rsqrt(jnp.mean(x32 * x32, axis=-1, keepdims=True) + RMS_EPS)
    return (y * g.astype(jnp.float32)).astype(x.dtype)

def token_shift(h):
    return jnp.pad(h, ((0, 0), (1, 0), (0, 0)))[:, :-1]

def head_group_norm(y, w, b):
    mu = jnp.mean(y, axis=-1, keepdims=True)
    var = jnp.mean(jnp.square(y - mu), axis=-1, keepdims=True)
    yn = (y - mu) * lax.rsqrt(var + GN_EPS)
    bsz, t = y.shape[0], y.shape[1]
    return yn.reshape(bsz, t, D_INNER) * w + b

def wkv7_scan(r, decay, k, v, kk, kka):
    bsz, _, nh, n = r.shape

    def step(S, inp):
        r_t, w_t, k_t, v_t, kk_t, kka_t = inp
        sa = jnp.einsum('bhvk,bhk->bhv', S, kk_t)
        S = (S * w_t[:, :, None, :]
             - sa[..., None] * kka_t[:, :, None, :]
             + v_t[..., None] * k_t[:, :, None, :])
        y_t = jnp.einsum('bhvk,bhk->bhv', S, r_t)
        return S, y_t

    seq_first = lambda z: jnp.moveaxis(z, 1, 0)
    S0 = jnp.zeros((bsz, nh, n, n), jnp.float32)
    _, ys = lax.scan(step, S0, (seq_first(r), seq_first(decay), seq_first(k),
                                seq_first(v), seq_first(kk), seq_first(kka)))
    return jnp.moveaxis(ys, 0, 1)

def rwkv7_time_mix(h, v_first, mu, w_in, w0, w1, w2, a0, a1, a2, k_k, k_a, r_k,
                   lnx_w, lnx_b, w_out, v_res):
    bsz, t, _ = h.shape
    f32 = jnp.float32
    xx = token_shift(h) - h
    lerp = lambda j: h + xx * mu[j]
    xr, xw, xk, xv, xa, xg = (lerp(j) for j in range(N_LERP))
    r = xr @ w_in[0]
    k = xk @ w_in[1]
    v = xv @ w_in[2]
    g = xg @ w_in[3]
    w_log = -jax.nn.softplus(-(w0 + jnp.tanh(xw @ w1) @ w2).astype(f32)) - 0.5
    decay = jnp.exp(-jnp.exp(w_log))
    a = jax.nn.sigmoid((a0 + (xa @ a1) @ a2).astype(f32))
    if v_res is None:
        v_first = v
    else:
        v0, v1, v2 = v_res
        v = v + (v_first - v) * jax.nn.sigmoid(v0 + (xv @ v1) @ v2)
    heads = lambda z: z.astype(f32).reshape(bsz, t, N_HEADS, HEAD_SIZE)
    kk = heads(k * k_k)
    kk = kk / jnp.maximum(jnp.linalg.norm(kk, axis=-1, keepdims=True), L2_EPS)
    k = k.astype(f32) * (1.0 + (a - 1.0) * k_a.astype(f32))
    rh, kh, vh, ah = heads(r), heads(k), heads(v), heads(a)
    y = wkv7_scan(rh, heads(decay), kh, vh, kk, kk * ah)
    y = head_group_norm(y, lnx_w.astype(f32), lnx_b.astype(f32))
    bonus = (jnp.sum(rh * kh * r_k.astype(f32), axis=-1, keepdims=True) * vh)
    y = (y + bonus.reshape(bsz, t, D_INNER)) * jax.nn.silu(g.astype(f32))
    return y.astype(h.dtype) @ w_out, v_first

def short_conv_mix(h, w_in, conv_w, w_out):
    z = h @ w_in
    c, b, u, g = jnp.split(z, 4, axis=-1)
    cu = c * u
    conv = lax.conv_general_dilated(
        cu, conv_w[:, None, :].astype(cu.dtype), window_strides=(1,),
        padding=[(CONV_WIDTH - 1, 0)], dimension_numbers=('NWC', 'WIO', 'NWC'),
        feature_group_count=D_INNER)
    y = b * conv * jax.nn.silu(g)
    return y @ w_out

def first_inputs(seed: int = 0) -> dict:
    key = jax.random.key(seed)
    ks = jax.random.split(key, 32)
    nrm = lambda i, shape, s: s * jax.random.normal(ks[i], shape, jnp.float32)
    uni = lambda i, shape, lo, hi: jax.random.uniform(ks[i], shape, jnp.float32, lo, hi)
    D, DI, NA, NB, NV = D_MODEL, D_INNER, N_RWKV, N_CONV, max(N_RWKV - 1, 0)
    return {
        "x": nrm(0, (BATCH, SEQ, D), 1.0),
        "a_norm": 1.0 + nrm(1, (NA, D), 0.02),
        "a_mu": uni(2, (NA, N_LERP, D), 0.0, 1.0),
        "a_w_in": nrm(3, (NA, 4, D, DI), D ** -0.5),
        "a_w0": uni(4, (NA, DI), -6.0, -1.0),
        "a_w1": nrm(5, (NA, D, LORA_DECAY), D ** -0.5),
        "a_w2": nrm(6, (NA, LORA_DECAY, DI), 0.5 * LORA_DECAY ** -0.5),
        "a_a0": nrm(7, (NA, DI), 0.1),
        "a_a1": nrm(8, (NA, D, LORA_A), D ** -0.5),
        "a_a2": nrm(9, (NA, LORA_A, DI), 0.5 * LORA_A ** -0.5),
        "a_kk": 0.85 + nrm(10, (NA, DI), 0.05),
        "a_ka": 1.0 + nrm(11, (NA, DI), 0.05),
        "a_rk": nrm(12, (NA, N_HEADS, HEAD_SIZE), 0.1),
        "a_lnw": 1.0 + nrm(13, (NA, DI), 0.02),
        "a_lnb": nrm(14, (NA, DI), 0.02),
        "a_w_out": nrm(15, (NA, DI, D), DI ** -0.5),
        "a_v0": 1.0 + nrm(16, (NV, DI), 0.1),
        "a_v1": nrm(17, (NV, D, LORA_V), D ** -0.5),
        "a_v2": nrm(18, (NV, LORA_V, DI), 0.5 * LORA_V ** -0.5),
        "b_norm": 1.0 + nrm(19, (NB, D), 0.02),
        "b_w_in": nrm(20, (NB, D, 4 * DI), D ** -0.5),
        "b_conv": nrm(21, (NB, CONV_WIDTH, DI), CONV_WIDTH ** -0.5),
        "b_w_out": nrm(22, (NB, DI, D), DI ** -0.5),
        "final_norm": 1.0 + nrm(23, (D,), 0.02),
    }

def first_block(x, a_norm, a_mu, a_w_in, a_w0, a_w1, a_w2, a_a0, a_a1, a_a2, a_kk, a_ka,
              a_rk, a_lnw, a_lnb, a_w_out, a_v0, a_v1, a_v2, b_norm, b_w_in, b_conv,
              b_w_out, final_norm):
    v_first = None
    for i in range(DEPTH):
        j = i // N_MIXERS
        if i % N_MIXERS == 0:
            h = rms_norm(x, a_norm[j])
            v_res = None if j == 0 else (a_v0[j - 1], a_v1[j - 1], a_v2[j - 1])
            out, v_first = rwkv7_time_mix(
                h, v_first, a_mu[j], a_w_in[j], a_w0[j], a_w1[j], a_w2[j],
                a_a0[j], a_a1[j], a_a2[j], a_kk[j], a_ka[j], a_rk[j],
                a_lnw[j], a_lnb[j], a_w_out[j], v_res)
        else:
            h = rms_norm(x, b_norm[j])
            out = short_conv_mix(h, b_w_in[j], b_conv[j], b_w_out[j])
        x = x + out
    return rms_norm(x, final_norm)


DEPTH_2 = 1

CHUNK = 64
Q_BLOCK = 128
MIX = D_MODEL
W_LRU = MIX // 2
LRU_BLOCKS = 8
LRU_BW = W_LRU // LRU_BLOCKS
LRU_C = 8.0
CONV_A = 4
SB_HEADS = 4
SB_DH = MIX // 4 // SB_HEADS
SB_W = SB_HEADS * SB_DH
DF_HEADS = 4
DF_DV = MIX // 4 // DF_HEADS
DF_DQK = DF_DV // 2
DF_W = DF_HEADS * DF_DV
D_FF = ((8 * D_MODEL // 3 + 255) // 256) * 256
CONV_FF = 3
EPS = 1e-6
IN_SIZES = [W_LRU, W_LRU, SB_W, SB_W, SB_W, DF_W, DF_W, DF_W]
P_IN = sum(IN_SIZES)


def rmsnorm(x, g):
    xf = x.astype(jnp.float32)
    y = xf * lax.rsqrt(jnp.mean(xf * xf, axis=-1, keepdims=True) + EPS)
    return (y * g.astype(jnp.float32)).astype(x.dtype)

def causal_dwconv(x, w, b):
    k = w.shape[0]
    y = lax.conv_general_dilated(
        x, w[:, None, :], window_strides=(1,), padding=[(k - 1, 0)],
        dimension_numbers=('NWC', 'WIO', 'NWC'), feature_group_count=x.shape[-1])
    return y + b

def rg_lru(xa, w_r, b_r, w_i, b_i, lam):
    bn, s, c = xa.shape
    xb = xa.reshape(bn, s, LRU_BLOCKS, LRU_BW)
    r = jax.nn.sigmoid((jnp.einsum('bsnc,ncd->bsnd', xb, w_r).reshape(bn, s, c) + b_r).astype(jnp.float32))
    i = jax.nn.sigmoid((jnp.einsum('bsnc,ncd->bsnd', xb, w_i).reshape(bn, s, c) + b_i).astype(jnp.float32))
    log_a = -LRU_C * r * jax.nn.softplus(-lam.astype(jnp.float32))
    a = jnp.exp(log_a)
    u = jnp.sqrt(-jnp.expm1(2.0 * log_a)) * (i * xa.astype(jnp.float32))

    def combine(left, right):
        a1, b1 = left
        a2, b2 = right
        return a1 * a2, a2 * b1 + b2

    _, h = lax.associative_scan(combine, (a, u), axis=1)
    return h.astype(xa.dtype)

def to_heads(t, n_heads):
    bn, s, w = t.shape
    return t.reshape(bn, s, n_heads, w // n_heads).transpose(0, 2, 1, 3)

def from_blocks(o):
    nb, bn, h, qb, dh = o.shape
    return o.transpose(1, 0, 3, 2, 4).reshape(bn, nb * qb, h, dh)

def stick_breaking(q, k, v):
    s_len = q.shape[2]
    scale = SB_DH ** -0.5
    spos = jnp.arange(s_len)

    def block(start):
        qb = lax.dynamic_slice_in_dim(q, start, Q_BLOCK, axis=2)
        tpos = start + jnp.arange(Q_BLOCK)
        earlier = spos[None, :] < tpos[:, None]
        z = jnp.einsum('bhqd,bhkd->bhqk', qb, k).astype(jnp.float32) * scale
        log_1m = jnp.where(earlier, jax.nn.log_sigmoid(-z), 0.0)
        tail = lax.cumsum(log_1m, axis=3, reverse=True) - log_1m
        wts = jnp.where(earlier, jnp.exp(jax.nn.log_sigmoid(z) + tail), 0.0)
        return jnp.einsum('bhqk,bhkd->bhqd', wts.astype(v.dtype), v)

    starts = jnp.arange(s_len // Q_BLOCK, dtype=jnp.int32) * Q_BLOCK
    o = from_blocks(lax.map(block, starts))
    return o.reshape(o.shape[0], s_len, SB_W)

def diff_attention(q, k, v, lam, lam_init, g_sub):
    s_len = q.shape[2]
    scale = DF_DQK ** -0.5
    q1, q2 = q[..., :DF_DQK], q[..., DF_DQK:]
    k1, k2 = k[..., :DF_DQK], k[..., DF_DQK:]
    slopes = 2.0 ** (-8.0 * (jnp.arange(DF_HEADS, dtype=jnp.float32) + 1.0) / DF_HEADS)
    spos = jnp.arange(s_len)

    def block(start):
        qb1 = lax.dynamic_slice_in_dim(q1, start, Q_BLOCK, axis=2)
        qb2 = lax.dynamic_slice_in_dim(q2, start, Q_BLOCK, axis=2)
        tpos = start + jnp.arange(Q_BLOCK)
        allowed = (spos[None, :] // CHUNK) <= (tpos[:, None] // CHUNK)
        dist = jnp.abs(tpos[:, None] - spos[None, :]).astype(jnp.float32)
        bias = -slopes[:, None, None] * dist

        def probs(qb, kk):
            sc = jnp.einsum('bhqd,bhkd->bhqk', qb, kk).astype(jnp.float32) * scale + bias
            return jax.nn.softmax(jnp.where(allowed, sc, -jnp.inf), axis=-1)

        p = probs(qb1, k1) - lam * probs(qb2, k2)
        return jnp.einsum('bhqk,bhkd->bhqd', p.astype(v.dtype), v)

    starts = jnp.arange(s_len // Q_BLOCK, dtype=jnp.int32) * Q_BLOCK
    o = from_blocks(lax.map(block, starts))
    o = rmsnorm(o, g_sub) * (1.0 - lam_init)
    return o.reshape(o.shape[0], s_len, DF_W)

def second_inputs(seed: int = 0) -> dict:
    key = jax.random.key(seed)
    ks = jax.random.split(key, 24)
    f32 = jnp.float32

    def nrm(k, shape, fan_in):
        return jax.random.normal(k, shape, f32) * (fan_in ** -0.5)

    def gain(k, shape):
        return 1.0 + 0.02 * jax.random.normal(k, shape, f32)

    def small(k, shape):
        return 0.01 * jax.random.normal(k, shape, f32)

    a_c = jax.random.uniform(ks[8], (DEPTH_2, W_LRU), f32, minval=0.9, maxval=0.999)
    a_base = a_c ** (1.0 / LRU_C)
    return {
        'x': jax.random.normal(ks[0], (BATCH, SEQ, D_MODEL), f32),
        'norm1_g': gain(ks[1], (DEPTH_2, D_MODEL)),
        'w_in': nrm(ks[2], (DEPTH_2, D_MODEL, P_IN), D_MODEL),
        'conv_a_w': nrm(ks[3], (DEPTH_2, CONV_A, W_LRU), CONV_A),
        'conv_a_b': small(ks[4], (DEPTH_2, W_LRU)),
        'w_rgate': nrm(ks[5], (DEPTH_2, LRU_BLOCKS, LRU_BW, LRU_BW), LRU_BW),
        'b_rgate': small(ks[6], (DEPTH_2, W_LRU)),
        'w_igate': nrm(ks[7], (DEPTH_2, LRU_BLOCKS, LRU_BW, LRU_BW), LRU_BW),
        'b_igate': small(ks[9], (DEPTH_2, W_LRU)),
        'lru_lambda': jnp.log(a_base) - jnp.log1p(-a_base),
        'lam_q1': 0.1 * jax.random.normal(ks[10], (DEPTH_2, DF_DQK), f32),
        'lam_k1': 0.1 * jax.random.normal(ks[11], (DEPTH_2, DF_DQK), f32),
        'lam_q2': 0.1 * jax.random.normal(ks[12], (DEPTH_2, DF_DQK), f32),
        'lam_k2': 0.1 * jax.random.normal(ks[13], (DEPTH_2, DF_DQK), f32),
        'subln_g': gain(ks[14], (DEPTH_2, DF_DV)),
        'w_out': nrm(ks[15], (DEPTH_2, MIX, D_MODEL), MIX),
        'norm2_g': gain(ks[16], (DEPTH_2, D_MODEL)),
        'w_ff_up': nrm(ks[17], (DEPTH_2, D_MODEL, 2 * D_FF), D_MODEL),
        'conv_ff_w': nrm(ks[18], (DEPTH_2, CONV_FF, 2 * D_FF), CONV_FF),
        'conv_ff_b': small(ks[19], (DEPTH_2, 2 * D_FF)),
        'w_ff_down': nrm(ks[20], (DEPTH_2, D_FF, D_MODEL), D_FF),
        'final_g': gain(ks[21], (D_MODEL,)),
    }

def second_block(x, norm1_g, w_in, conv_a_w, conv_a_b, w_rgate, b_rgate, w_igate, b_igate,
              lru_lambda, lam_q1, lam_k1, lam_q2, lam_k2, subln_g, w_out, norm2_g,
              w_ff_up, conv_ff_w, conv_ff_b, w_ff_down, final_g):
    split_at = np.cumsum(IN_SIZES)[:-1].tolist()
    for l in range(DEPTH_2):
        h = rmsnorm(x, norm1_g[l])
        proj = h @ w_in[l]
        xa, ya, sq, sk, sv, dq, dk, dv = jnp.split(proj, split_at, axis=-1)

        xa = causal_dwconv(xa, conv_a_w[l], conv_a_b[l])
        out_a = rg_lru(xa, w_rgate[l], b_rgate[l], w_igate[l], b_igate[l], lru_lambda[l]) * jax.nn.gelu(ya)

        out_b = stick_breaking(to_heads(sq, SB_HEADS), to_heads(sk, SB_HEADS), to_heads(sv, SB_HEADS))

        lam_init = 0.8 - 0.6 * float(np.exp(-0.3 * l))
        lam = (jnp.exp(jnp.sum(lam_q1[l] * lam_k1[l]).astype(jnp.float32))
               - jnp.exp(jnp.sum(lam_q2[l] * lam_k2[l]).astype(jnp.float32)) + lam_init)
        out_c = diff_attention(to_heads(dq, DF_HEADS), to_heads(dk, DF_HEADS), to_heads(dv, DF_HEADS),
                               lam, lam_init, subln_g[l])

        mixed = jnp.concatenate([out_a, out_b.astype(out_a.dtype), out_c.astype(out_a.dtype)], axis=-1)
        x = x + mixed @ w_out[l]

        h2 = rmsnorm(x, norm2_g[l])
        u = causal_dwconv(h2 @ w_ff_up[l], conv_ff_w[l], conv_ff_b[l])
        gate, val = jnp.split(u, 2, axis=-1)
        x = x + (jax.nn.silu(gate) * val) @ w_ff_down[l]
    return rmsnorm(x, final_g)


def setup_inputs(seed=0):
    out = dict(first_inputs(seed))
    for name, value in second_inputs(seed + 1).items():
        if name != "x":
            out[name + "_2"] = value
    return out


def reference(
    x, a_norm, a_mu, a_w_in, a_w0, a_w1, a_w2, a_a0, a_a1, a_a2, a_kk, a_ka, a_rk, a_lnw, a_lnb,
    a_w_out, a_v0, a_v1, a_v2, b_norm, b_w_in, b_conv, b_w_out, final_norm, norm1_g_2, w_in_2,
    conv_a_w_2, conv_a_b_2, w_rgate_2, b_rgate_2, w_igate_2, b_igate_2, lru_lambda_2, lam_q1_2,
    lam_k1_2, lam_q2_2, lam_k2_2, subln_g_2, w_out_2, norm2_g_2, w_ff_up_2, conv_ff_w_2,
    conv_ff_b_2, w_ff_down_2, final_g_2,
):
    x = first_block(
        x, a_norm, a_mu, a_w_in, a_w0, a_w1, a_w2, a_a0, a_a1, a_a2, a_kk, a_ka, a_rk, a_lnw,
        a_lnb, a_w_out, a_v0, a_v1, a_v2, b_norm, b_w_in, b_conv, b_w_out, final_norm,
    )
    return second_block(
        x, norm1_g_2, w_in_2, conv_a_w_2, conv_a_b_2, w_rgate_2, b_rgate_2, w_igate_2,
        b_igate_2, lru_lambda_2, lam_q1_2, lam_k1_2, lam_q2_2, lam_k2_2, subln_g_2, w_out_2,
        norm2_g_2, w_ff_up_2, conv_ff_w_2, conv_ff_b_2, w_ff_down_2, final_g_2,
    )


_drawn_inputs = setup_inputs


def setup_inputs(seed=0):
    import zlib

    import numpy as np

    out = dict(_drawn_inputs(seed))
    spreads = {}
    factors = {'a_w1': 3.423,
     'a_w2': 3.43,
     'a_lnw': 3.863,
     'a_lnb': 3.524,
     'norm1_g_2': 3.2,
     'conv_a_b_2': 8.134,
     'b_rgate_2': 34.947,
     'b_igate_2': 32.836,
     'lam_k1_2': 8.0,
     'subln_g_2': 27.882,
     'norm2_g_2': 11.216,
     'conv_ff_b_2': 23.057,
     'final_g_2': 22.881}
    for name, (base, spread) in spreads.items():
        noise = np.random.default_rng([zlib.crc32(name.encode()), seed]).standard_normal(out[name].shape)
        drawn = base * np.exp(spread * noise) if base else spread * noise
        out[name] = __import__('jax').numpy.asarray(drawn.astype(out[name].dtype))
    for name, factor in factors.items():
        out[name] = (out[name] * factor).astype(out[name].dtype)
    return out
```

```python
from contextlib import ExitStack

import numpy as np
import concourse.bass as bass
from concourse import mybir

ALU = mybir.AluOpType
ACT = mybir.ActivationFunctionType
AX_X = mybir.AxisListType.X
F32 = mybir.dt.float32

P = 128
T = 512
D = 1024
DC = D // P
DI = 2048
IC = DI // P
HD = 64
NCH = T // HD
TB = T // P
LORA = 64
RMS_EPS = 1e-6
GN_EPS = 64e-5
EXP_HALF = 0.6065306597126334
LRU = 512
DFF = 2816
FC = DFF // P
PIN = 2560
IN_ORDER = np.r_[0:1536, 1792:2304, 1536:1792, 2304:2560]
LVL = 6
FAR = 1e30
DIST = [0, 1 * P, 3 * P, 6 * P, 10 * P]
LN2 = 0.6931471805599453

PARAMS = [("a_norm", D), ("a_mu", 6 * D), ("a_w0", DI), ("a_a0", DI), ("a_kk", DI), ("a_ka", DI), ("a_rk", DI),
          ("a_lnw", DI), ("a_lnb", DI), ("b_norm", D), ("b_conv", 3 * DI), ("final_norm", D), ("norm1_g_2", D),
          ("conv_a_w_2", 4 * LRU), ("conv_a_b_2", LRU), ("b_rgate_2", LRU), ("b_igate_2", LRU), ("lru_lambda_2", LRU),
          ("subln_g_2", P),
          ("norm2_g_2", D), ("conv_ff_w_2", 6 * DFF), ("conv_ff_b_2", 2 * DFF), ("final_g_2", D)]
PCOL = {}
_at = 0
for _name, _len in PARAMS:
    PCOL[_name] = _at
    _at += _len // P
NPAR = _at

CONSTS = [("ident", P), ("head_sum", P), ("head_mean", P), ("row_mean", P), ("score_mask", 2 * P),
          ("level_first", P), ("level_mask", 5 * P), ("scan_keep", T), ("eye", 6 * HD),
          ("minus_after", P), ("minus_all", P), ("before", P)]
CCOL = {}
_at = 0
for _name, _len in CONSTS:
    CCOL[_name] = _at
    _at += _len
NCON = _at


def constants():
    c = np.zeros((P, NCON), np.float32)
    i, j = np.meshgrid(np.arange(P), np.arange(P), indexing="ij")
    same = (i // HD) == (j // HD)

    def put(name, a):
        c[:, CCOL[name]:CCOL[name] + a.shape[1]] = a

    put("ident", i == j)
    put("head_sum", same)
    put("head_mean", same / HD)
    put("row_mean", np.full((P, P), 1.0 / D))
    put("score_mask", np.concatenate([-1.0 * (same & (j > i)), 1.0 * (same & (j >= i))], 1))
    below = lambda n: (i // (2 * n) == j // (2 * n)) & (i % (2 * n) >= n) & (j % (2 * n) < n)
    put("level_first", below(1).T)
    put("level_mask", np.concatenate([below(1 << k) for k in range(1, LVL)], 1))
    put("scan_keep", np.tile((np.arange(T) % HD != 0), (P, 1)))
    put("eye", np.tile(np.eye(HD), (2, 6)))
    put("minus_after", -1.0 * (i > j))
    put("minus_all", -np.ones((P, P)))
    put("before", i < j)
    return c


def distances():
    d = np.zeros((P, DIST[-1]), np.float32)
    for b in range(TB):
        t, s = np.meshgrid(b * P + np.arange(P), np.arange((b + 1) * P), indexing="ij")
        d[:, DIST[b]:DIST[b + 1]] = np.where(s // HD <= t // HD, np.abs(t - s), FAR)
    return d


def need(eng, sem, n):
    if isinstance(n, int) and n <= 0:
        return
    eng.wait_ge(sem, n)


def apart(eng):
    eng.nop(nofuse=True)


class Sems:

    def __init__(self, nc, ctx, phase):
        self.nc, self.ctx, self.phase, self.have = nc, ctx, phase, {}
        ctx.callback(self.clear)

    def __call__(self, name):
        if name not in self.have:
            self.have[name] = self.ctx.enter_context(self.nc.semaphore(f"{self.phase}_{name}"))
        return self.have[name]

    def clear(self):
        numbers = sorted(s.num for s in self.have.values())
        first = 0
        for n in range(1, len(numbers) + 1):
            if n == len(numbers) or numbers[n] != numbers[n - 1] + 1:
                self.nc.gpsimd.sem_clear(range(numbers[first], numbers[n - 1] + 1))
                first = n
        self.nc.all_engine_barrier()


def norm_scalar(act, S, tag, x, sq, bank, lnv, rstd, eps, ready):
    for j in range(DC):
        ready(j)
        need(act, S(tag + "_sum"), j - 1)
        act.activation(sq[:, j % 2, :], x[:, j, :], ACT.Square).then_inc(S(tag + "_sq"), 1)
    act.wait_ge(S(tag + "_sum"), DC)
    act.activation(lnv, bank, ACT.Ln, bias=eps).then_inc(S(tag + "_ln"), 1)
    act.wait_ge(S(tag + "_ln"), 1)
    act.activation(rstd, lnv, ACT.Exp, scale=-0.5).then_inc(S(tag + "_rstd"), 1)


def norm_tensor(pe, S, tag, row_mean, sq, bank):
    for j in range(DC):
        pe.wait_ge(S(tag + "_sq"), j + 1)
        pe.matmul(bank, row_mean, sq[:, j % 2, :], start=(j == 0), stop=(j == DC - 1)).then_inc(S(tag + "_sum"), 1)


def norm_vector(dve, S, tag, x, g, rstd, out):
    dve.wait_ge(S(tag + "_rstd"), 1)
    for j in range(DC):
        dve.scalar_tensor_tensor(out=out[:, j, :], in0=x[:, j, :], scalar=g[:, j:j + 1], in1=rstd,
                                 op0=ALU.mult, op1=ALU.mult).then_inc(S(tag + "_out"), 1)


def program(nc, ins, out, stop_after=None):
    with ExitStack() as top:
        def sbt(ctx, name, shape, dt=F32):
            return ctx.enter_context(nc.sbuf_tensor(name, shape, dt))

        bank = [top.enter_context(nc.psum_tensor(f"bank{i}", [P, T], F32)) for i in range(8)]
        con = sbt(top, "con", [P, NCON])
        par = sbt(top, "par", [P, NPAR])
        eps = sbt(top, "eps", [P, 3])
        C = {n: con[:, CCOL[n]:CCOL[n] + k] for n, k in CONSTS}
        V = {n: par[:, PCOL[n]:PCOL[n] + k // P] for n, k in PARAMS}
        K = dict(nc=nc, ins=ins, out=out, bank=bank, C=C, V=V, eps=eps, con=con, par=par, sbt=sbt)
        with ExitStack() as mem:
            gate = K["gate"] = sbt(mem, "gate", [P, IC, T])
            with ExitStack() as mix:
                K["lerp"] = {n: sbt(mix, f"lerp_{n}", [P, DC, T]) for n in "rkv"}
                K["hidden"] = sbt(mix, "hidden", [P, T])
                K["mixpar"] = sbt(mix, "mixpar", [P, IC, 8])
                lerp_phase(K)
                rwkv_phase(K)
            if stop_after == "rwkv":
                return
            x = K["x"] = sbt(mem, "x", [P, DC, T])
            h = K["h"] = sbt(mem, "h", [P, DC, T])
            project_phase(K, "out1", gate, IC, "w_out1", [("norm", "b_norm", h)], load_x=True)
            conv_phase(K)
            project_phase(K, "out2", gate, IC, "w_out2", [("norm", "final_norm", x), ("norm2", "norm1_g_2", h)])
            if stop_after == "x3":
                return
            K["proj"] = gate
            mixed = K["mixed"] = h
            with ExitStack() as mix:
                K["vals"] = sbt(mix, "vals", [P, TB, 4 * P])
                input_phase(K)
                mixer_phase(K)
            if stop_after == "mixed":
                return
            project_phase(K, "out3", mixed, DC, "w_out3", [("norm", "norm2_g_2", h)])
            ff = K["ff"] = sbt(mem, "ff", [P, FC, T])
            up_phase(K)
            project_phase(K, "down", ff, FC, "w_down", [("norm", "final_g_2", x)], store=True)


def lerp_phase(K):
    nc, ins, bank, C, V = (K[n] for n in ("nc", "ins", "bank", "C", "V"))
    eps, gate, lerp, hidden, mixpar = (K[n] for n in ("eps", "gate", "lerp", "hidden", "mixpar"))
    RING = 4
    with ExitStack() as ctx:
        S = Sems(nc, ctx, "lerp")
        x = K["sbt"](ctx, "x_in", [P, DC, T])
        xx = K["sbt"](ctx, "xx", [P, DC, T])
        tmp = [gate[:, 0:DC, :], x]
        h = gate[:, DC:2 * DC, :]
        xg = K["sbt"](ctx, "xg", [P, DC, T])
        ring = K["sbt"](ctx, "g_ring", [P, RING, DC * P])
        wl = K["sbt"](ctx, "lora_w1", [P, DC, P])
        sq = K["sbt"](ctx, "sq", [P, 2, T])
        lnv = K["sbt"](ctx, "lnv", [P, T])
        rstd = K["sbt"](ctx, "rstd", [P, T])
        thg = K["sbt"](ctx, "thg", [P, 2, T])
        block = ctx.enter_context(nc.Block())
        mu = V["a_mu"].rearrange("p (j c) -> p j c", j=6)
        ORDER = ["w", "a", "g", "r", "k", "v"]
        MU = {"r": 0, "w": 1, "k": 2, "v": 3, "a": 4, "g": 5}
        dst = {"w": tmp[0], "a": tmp[1], "g": xg, **lerp}

        @block.sync
        def _(sp):
            sp.dma_start(K["con"][:, :], ins["consts"]).then_inc(S("const"), 16)
            sp.dma_start(x[:, :, :], ins["x"]).then_inc(S("x"), 16)
            sp.dma_start(K["par"][:, :], ins["params"]).then_inc(S("param"), 16)
            sp.dma_start(wl[:, :, :], ins["lora1"]).then_inc(S("wl"), 16)

            def load(i, s):
                need(sp, S("g_mm"), RING * (i - 1) + s + 1)
                sp.dma_start(ring[:, s, :], ins["w_g"][RING * i + s]).then_inc(S(f"w{s}"), 16)

            for s in range(RING):
                load(0, s)
            with sp.Fori(1, IC // RING) as i:
                for s in range(RING):
                    load(i, s)

        @block.gpsimd
        def _(pool):
            for n, v in enumerate((RMS_EPS, GN_EPS, 10 * LN2)):
                pool.memset(eps[:, n:n + 1], v).then_inc(S("eps"), 1)
            pool.wait_ge(S("param"), 16)
            for n, (name, a, b) in enumerate((("a_w0", 0.5, 0.0), ("a_a0", 0.5, 0.0), ("a_ka", 0.5, 0.0),
                                              ("a_ka", -0.5, 1.0), ("a_kk", 1.0, 0.0), ("a_rk", 1.0, 0.0),
                                              ("a_lnw", 1.0, 0.0), ("a_lnb", 1.0, 0.0))):
                pool.tensor_scalar(mixpar[:, :, n], V[name], a, b, ALU.mult, ALU.add).then_inc(S("mixpar"), 1)

        @block.scalar
        def _(act):
            act.wait_ge(S("eps"), 3)
            norm_scalar(act, S, "norm", x, sq, bank[0][:, :], lnv[:, :], rstd[:, :], eps[:, 0:1],
                        lambda j: act.wait_ge(S("x"), 16) if j == 0 else None)
            act.wait_ge(S("hid_mm"), 1)
            act.activation(hidden[0:LORA, :], bank[1][0:LORA, :], ACT.Tanh).then_inc(S("hid"), 1)
            act.wait_ge(S("hid_mm"), 2)
            act.activation(hidden[LORA:P, :], bank[1][LORA:P, :], ACT.Copy).then_inc(S("hid"), 1)

            def job(i, s):
                n = RING * i + s
                act.wait_ge(S("g_mm"), n + 1)
                need(act, S("gate"), n - 1)
                act.activation(thg[:, s % 2, :], bank[2 + s][:, :], ACT.Tanh, scale=0.5).then_inc(S("thg"), 1)

            for s in range(RING):
                job(0, s)
            with act.Fori(1, IC // RING) as i:
                for s in range(RING):
                    job(i, s)

        @block.tensor
        def _(pe):
            pe.wait_ge(S("const"), 16)
            norm_tensor(pe, S, "norm", C["row_mean"], sq, bank[0][:, :])
            pe.wait_ge(S("wl"), 16)
            for n, (lo, hi) in enumerate(((0, LORA), (LORA, P))):
                for j in range(DC):
                    pe.wait_ge(S("lerp"), DC * n + j + 1)
                    m = pe.matmul(bank[1][lo:hi, :], wl[:, j, lo:hi], tmp[n][:, j, :], start=(j == 0),
                                  stop=(j == DC - 1))
                m.then_inc(S("hid_mm"), 1)

            def job(i, s):
                pe.wait_ge(S(f"w{s}"), 16 * i + 16)
                need(pe, S("gate"), RING * (i - 1) + s + 1)
                if isinstance(i, int) and s == 0:
                    pe.wait_ge(S("lerp"), DC * 3)
                for j in range(DC):
                    m = pe.matmul(bank[2 + s][:, :], ring[:, s, j * P:(j + 1) * P], xg[:, j, :],
                                  start=(j == 0), stop=(j == DC - 1))
                m.then_inc(S("g_mm"), 1)

            for s in range(RING):
                job(0, s)
            with pe.Fori(1, IC // RING) as i:
                for s in range(RING):
                    job(i, s)

        @block.vector
        def _(dve):
            dve.wait_ge(S("param"), 16)
            norm_vector(dve, S, "norm", x, V["a_norm"], rstd[:, :], h)
            for j in range(DC):
                dve.wait_ge(S("norm_out"), j + 1)
                dve.tensor_tensor(xx[:, j, 1:T], h[:, j, 0:T - 1], h[:, j, 1:T], ALU.subtract).then_inc(S("xx"), 1)
                dve.tensor_scalar(xx[:, j, 0:1], h[:, j, 0:1], -1.0, None, ALU.mult).then_inc(S("xx"), 1)
            dve.wait_ge(S("xx"), 2 * DC)

            def lerps(name):
                for j in range(DC):
                    dve.scalar_tensor_tensor(out=dst[name][:, j, :], in0=xx[:, j, :],
                                             scalar=mu[:, MU[name], j:j + 1], in1=h[:, j, :],
                                             op0=ALU.mult, op1=ALU.add).then_inc(S("lerp"), 1)

            for name in ORDER:
                lerps(name)
            dve.wait_ge(S("lerp"), DC * len(ORDER))
            dve.wait_ge(S("hid_mm"), 2)

            def job(i, s):
                n = RING * i + s
                dve.wait_ge(S("thg"), n + 1)
                dve.scalar_tensor_tensor(out=gate[:, n, :], in0=thg[:, s % 2, :], scalar=1.0,
                                         in1=bank[2 + s][:, :], op0=ALU.add, op1=ALU.mult).then_inc(S("gate"), 1)

            for s in range(RING):
                job(0, s)
            with dve.Fori(1, IC // RING) as i:
                for s in range(RING):
                    job(i, s)


def rwkv_phase(K):
    nc, ins, bank, C, V = (K[n] for n in ("nc", "ins", "bank", "C", "V"))
    eps, gate, lerp, hidden, mixpar, sbt = (K[n] for n in ("eps", "gate", "lerp", "hidden", "mixpar", "sbt"))
    with ExitStack() as ctx:
        S = Sems(nc, ctx, "mix")
        ring = {n: sbt(ctx, f"w_{n}", [P, DC * P]) for n in "krv"}
        lora = sbt(ctx, "w_lora2", [P, P])
        kap, bet, kd, ke, be, vT = (sbt(ctx, n, [P, T]) for n in ("kap", "bet", "kd", "ke", "be", "vT"))
        rt, bonus = sbt(ctx, "rt", [P, 2, T]), sbt(ctx, "bonus", [P, 2, T])
        dend = sbt(ctx, "dend", [P, 2, 6 * HD])
        ld, cum, e1, tha, kp, kraw, kk, nn, rraw, bon = (
            sbt(ctx, n, [P, T]) for n in ("ld", "cum", "e1", "tha", "kp", "kraw", "kk", "nn", "rraw", "bon"))
        LA = sbt(ctx, "LA", [P, 2, TB, 2 * P])
        MK = sbt(ctx, "MK", [P, 2, TB, 2 * P])
        XK = sbt(ctx, "XK", [P, 2, TB, P])
        NTG = sbt(ctx, "NTG", [P, 2, TB, P])
        tok = {n: sbt(ctx, f"{n}_tok", [P, TB, P]) for n in ("ke", "be", "v")}
        inv, invT, low = (sbt(ctx, n, [P, 2, TB, P]) for n in ("inv", "invT", "low"))
        rh = sbt(ctx, "rh", [P, T])
        phi = sbt(ctx, "phi", [P, 6 * HD])
        st = sbt(ctx, "st", [P, NCH, HD])
        y = sbt(ctx, "y", [P, T])
        yc, yv = sbt(ctx, "yc", [P, T]), sbt(ctx, "yv", [P, T])
        chan = sbt(ctx, "chan", [P, 2, 6])
        affine = sbt(ctx, "affine", [P, 2])
        block = ctx.enter_context(nc.Block())

        G, YB, ROT = bank[0:2], bank[2], bank[4:8]
        SB = (bank[3], ROT[2])
        PH = (ROT[3], ROT[0])
        MEANB, VARB, NNB, BONB = 0, 1, 2, 3
        MVB, TKGB, RHB = 0, (1, 2), 1
        chunks = lambda ap: ap.rearrange("p (n t) -> p n t", t=HD)
        blocks = lambda ap: ap.rearrange("p (b t) -> p b t", t=P)
        pairs = lambda ap: ap.rearrange("p (b t) -> p b t", t=2 * P)
        over = lambda ap, n: ap.rearrange("p (o k) -> p o k", o=1).broadcast_to([P, n, ap.shape[1]])
        ends = lambda ap: chunks(ap)[:, :, HD - 1:HD].broadcast_to([P, NCH, HD])
        rows = (slice(0, HD), slice(HD, P))
        JOBS = ["w", "a", "k", "r", "v"]
        NJ = len(JOBS)

        def run(step):
            def loop(eng):
                step(0)
                step(1)
                with eng.Fori(1, IC // 2 - 1) as i:
                    step(2 * i, 0)
                    step(2 * i + 1, 1)
                step(IC - 2)
                step(IC - 1)
            return loop

        @block.sync
        def _(sp):
            def load(c, p=None):
                for n, name in enumerate("krv"):
                    need(sp, S("gemm"), NJ * (c - 1) + 3 + n)
                    sp.dma_start(ring[name][:, :], ins["w_" + name][c]).then_inc(S("w_" + name), 16)
                    if n == 0:
                        sp.dma_start(lora[:, :], ins["lora2"][c]).then_inc(S("w_lora"), 16)

            load(0)
            load(1)
            with sp.Fori(2, IC) as c:
                load(c)

        @block.gpsimd
        def _(pool):
            def prepare(n, p):
                pool.wait_ge(S("tanh"), 2 * n + 1)
                apart(pool)
                pool.tensor_scalar(ld[:, :], ld[:, :], -EXP_HALF / 2, -EXP_HALF / 2, ALU.mult, ALU.add)\
                    .then_inc(S("ld"), 1)
                pool.wait_ge(S("tanh"), 2 * n + 2)
                need(pool, S("bon"), n)
                apart(pool)
                pool.tensor_scalar(kp[:, :], tha[:, :], chan[:, p, 2:3], chan[:, p, 3:4], ALU.mult, ALU.add)\
                    .then_inc(S("kfac"), 1)
                pool.wait_ge(S("kfac"), n + 1)
                apart(pool)
                pool.tensor_scalar(tha[:, :], tha[:, :], 0.5, 0.5, ALU.mult, ALU.add).then_inc(S("a"), 1)

            def prepare_keys(n, p):
                pool.wait_ge(S("evac"), 3 * n + 1)
                need(pool, S("kap"), 2 * n)
                apart(pool)
                pool.tensor_scalar(kk[:, :], kraw[:, :], chan[:, p, 4:5], None, ALU.mult).then_inc(S("kk0"), 1)
                pool.wait_ge(S("exp"), 2 * n + 1)
                need(pool, S("phi"), 2 * (n - 1))
                pool.tensor_tensor(dend[:, p, :].rearrange("p (n t) -> p n t", t=HD),
                                   C["eye"].rearrange("p (n t) -> p n t", t=HD),
                                   chunks(e1[:, :])[:, 1:7, HD - 1:HD].broadcast_to([P, 6, HD]), ALU.mult)\
                    .then_inc(S("dend"), 1)
                pool.wait_ge(S("kk"), n + 1)
                pool.wait_ge(S("a"), n + 1)
                pool.tensor_tensor(tha[:, :], tha[:, :], kk[:, :], ALU.mult).then_inc(S("b"), 1)
                need(pool, S("score_mm"), 8 * n)
                pool.tensor_tensor(chunks(kap[:, :])[:, :, 1:HD], chunks(kk[:, :])[:, :, 1:HD],
                                   chunks(e1[:, :])[:, :, 0:HD - 1], ALU.mult).then_inc(S("kap"), 1)
                apart(pool)
                pool.tensor_scalar(chunks(kap[:, :])[:, :, 0:1], chunks(kk[:, :])[:, :, 0:1], 1.0, None, ALU.mult)\
                    .then_inc(S("kap"), 1)

            def finish(c, p):
                pool.wait_ge(S("yn"), c + 1)
                pool.wait_ge(S("aff"), c + 1)
                apart(pool)
                pool.tensor_scalar(yv[:, :], yc[:, :], affine[:, 0:1], affine[:, 1:2], ALU.mult, ALU.add)\
                    .then_inc(S("affine"), 1)
                pool.wait_ge(S("affine"), c + 1)
                pool.wait_ge(S("bonus"), c + 1)
                pool.tensor_tensor(yv[:, :], yv[:, :], bonus[:, p, :], ALU.add).then_inc(S("plus"), 1)

            def step(c, p=None):
                q = c % 2 if p is None else p
                last = isinstance(c, int) and c == IC - 1
                if not last:
                    prepare(c + 1, 1 - q)
                if not (isinstance(c, int) and c == 0):
                    finish(c - 1, 1 - q)
                if not last:
                    prepare_keys(c + 1, 1 - q)

            prepare(0, 0)
            prepare_keys(0, 0)
            run(step)(pool)
            finish(IC - 1, 1)

        @block.scalar
        def _(act):
            def tanhs(n, q):
                act.wait_ge(S("gemm"), NJ * n + 1)
                act.wait_ge(S("chan"), n + 1)
                need(act, S("cum"), n)
                act.activation(ld[:, :], G[(q + 0) % 2][:, :], ACT.Tanh, bias=chan[:, q, 0:1], scale=0.5)\
                    .then_inc(S("tanh"), 1)
                act.wait_ge(S("gemm"), NJ * n + 2)
                need(act, S("bet"), n)
                act.activation(tha[:, :], G[(q + 1) % 2][:, :], ACT.Tanh, bias=chan[:, q, 1:2], scale=0.5)\
                    .then_inc(S("tanh"), 1)

            def evacuate(n, q, k, dst, readers):
                act.wait_ge(S("gemm"), NJ * n + 3 + k)
                for name, count in readers:
                    need(act, S(name), count)
                act.activation(dst, G[(q + k) % 2][:, :], ACT.Copy).then_inc(S("evac"), 1)

            def exps(n):
                act.wait_ge(S("cum"), n + 1)
                need(act, S("rt"), n)
                need(act, S("kap"), 2 * n)
                act.activation(e1[:, :], cum[:, :], ACT.Exp).then_inc(S("exp"), 1)
                act.wait_ge(S("exp"), 2 * n + 1)
                act.activation(cum[:, :], cum[:, :], ACT.Exp, scale=-1.0).then_inc(S("exp"), 1)

            def key_square(n):
                act.wait_ge(S("kk0"), n + 1)
                need(act, S("kk"), n)
                act.activation(nn[:, :], kk[:, :], ACT.Square).then_inc(S("nsq"), 1)

            def key_norm(n):
                act.wait_ge(S("nclamp"), n + 1)
                act.activation(nn[:, :], nn[:, :], ACT.Ln, scale=float(2 ** 20)).then_inc(S("nln"), 1)
                act.wait_ge(S("nln"), n + 1)
                act.activation(nn[:, :], nn[:, :], ACT.Exp, scale=-0.5, bias=eps[:, 2:3]).then_inc(S("nrs"), 1)

            def center_square(c):
                act.wait_ge(S("yc"), c + 1)
                need(act, S("gated"), c)
                act.activation(yv[:, :], yc[:, :], ACT.Square).then_inc(S("ysq"), 1)

            def group_norm(c):
                act.wait_ge(S("var_mm"), c + 1)
                act.activation(yv[:, :], ROT[VARB][:, :], ACT.Ln, bias=eps[:, 1:2]).then_inc(S("yln"), 1)
                act.wait_ge(S("yln"), c + 1)
                act.activation(yv[:, :], yv[:, :], ACT.Exp, scale=-0.5).then_inc(S("yrs"), 1)

            def step(c, p=None):
                last = isinstance(c, int) and c == IC - 1
                first = isinstance(c, int) and c == 0
                q = c % 2 if p is None else p
                for k in range(4):
                    act.wait_ge(S("turn_mm"), 4 * c + k + 1)
                    src = blocks(ROT[k][:, :])
                    if k == 0:
                        src = src.rearrange("p b (h k) -> p h b k", h=2)
                        for h in range(2):
                            act.activation(XK[:, h, :, 0:HD], src[:, h], ACT.Copy).then_inc(S("turned"), 1)
                    else:
                        act.activation(tok[("ke", "be", "v")[k - 1]][:, :, :], src, ACT.Copy)\
                            .then_inc(S("turned"), 1)
                if not first:
                    center_square(c - 1)
                if not last:
                    tanhs(c + 1, 1 - q)
                if not first:
                    group_norm(c - 1)
                if not last:
                    exps(c + 1)
                    evacuate(c + 1, 1 - q, 0, kraw[:, :], [("kp", c + 1)])
                    key_square(c + 1)
                    key_norm(c + 1)
                    evacuate(c + 1, 1 - q, 1, rraw[:, :], [("bon", c + 1), ("rt", c + 1)])
                act.wait_ge(S("mv_mm"), c + 1)
                for h in range(2):
                    act.activation(XK[:, h, :, HD:P],
                                   ROT[MVB][:, :].rearrange("p (b h k) -> p h b k", h=2, k=HD)[:, h],
                                   ACT.Copy, scale=-1.0).then_inc(S("mv"), 1)
                for h in range(2):
                    act.wait_ge(S("tkg_mm"), 2 * c + h + 1)
                    act.activation(NTG[:, h, :, :], blocks(ROT[TKGB[h]][:, :]), ACT.Copy, scale=-1.0)\
                        .then_inc(S("tkg"), 1)
                if not last:
                    evacuate(c + 1, 1 - q, 2, vT[:, :], [("bonus", c + 1), ("turn_mm", 4 * (c + 1))])
                act.wait_ge(S("y_mm"), c + 1)
                need(act, S("yc"), c)
                act.activation(y[:, :], YB[:, :], ACT.Copy).then_inc(S("y"), 1)

            tanhs(0, 0)
            exps(0)
            evacuate(0, 0, 0, kraw[:, :], [])
            key_square(0)
            key_norm(0)
            evacuate(0, 0, 1, rraw[:, :], [])
            evacuate(0, 0, 2, vT[:, :], [])
            run(step)(act)
            center_square(IC - 1)
            group_norm(IC - 1)

        @block.tensor
        def _(pe):
            def gemm(n, q):
                for k, name in enumerate("krv"):
                    for j in range(DC):
                        if j == 0:
                            pe.wait_ge(S("w_" + name), 16 * (n + 1))
                            bank_free(n, 2 + k)
                        m = pe.matmul(G[(q + k) % 2][:, :], ring[name][:, j * P:(j + 1) * P],
                                      lerp[name][:, j, :], start=(j == 0), stop=(j == DC - 1))
                        if j == DC - 1:
                            m.then_inc(S("gemm"), 1)
                        yield

            def bank_free(n, j):
                if j == 0:
                    need(pe, S("evac"), 3 * n - 1)
                elif j == 1:
                    need(pe, S("evac"), 3 * n)
                elif j < 4:
                    need(pe, S("tanh"), 2 * n + j - 1)
                else:
                    need(pe, S("evac"), 3 * n + 1)

            def loras(n, q):
                pe.wait_ge(S("w_lora"), 16 * (n + 1))
                for j in range(2):
                    bank_free(n, j)
                    pe.matmul(G[(q + j) % 2][:, :], lora[rows[j], :], hidden[rows[j], :], start=True, stop=True)\
                        .then_inc(S("gemm"), 1)

            def stat(weights, src, b, sem):
                pe.matmul(ROT[b][:, :], weights, src, start=True, stop=True).then_inc(sem, 1)

            def means(c):
                pe.wait_ge(S("y"), c + 1)
                stat(C["head_mean"], y[:, :], MEANB, S("mean_mm"))

            def variances(c):
                pe.wait_ge(S("ysq"), c + 1)
                stat(C["head_mean"], yv[:, :], VARB, S("var_mm"))

            def key_sums(n):
                pe.wait_ge(S("nsq"), n + 1)
                stat(C["head_sum"], nn[:, :], NNB, S("nn_mm"))

            def bonus_sums(n):
                pe.wait_ge(S("bon"), n + 1)
                stat(C["head_sum"], bon[:, :], BONB, S("bsum_mm"))

            def step(c, p=None):
                q = c % 2 if p is None else p
                last = isinstance(c, int) and c == IC - 1
                first = isinstance(c, int) and c == 0
                more = iter(()) if last else gemm(c + 1, 1 - q)

                def fill(k):
                    for _ in range(k):
                        next(more, None)

                pe.wait_ge(S("be"), c + 1)
                pe.wait_ge(S("kap"), 2 * (c + 1))
                pe.wait_ge(S("evac"), 3 * (c + 1))
                for k, src in enumerate((kap, ke, be, vT)):
                    if k == 0:
                        need(pe, S("phi"), 2 * c)
                    if k == 1:
                        need(pe, S("rh"), c)
                    if k == 2:
                        need(pe, S("st"), 7 * c)
                    if k == 3:
                        need(pe, S("bonus"), c + 1)
                    for b in range(TB):
                        m = pe.transpose(ROT[k][:, b * P:(b + 1) * P], src[:, b * P:(b + 1) * P], C["ident"])
                    m.then_inc(S("turn_mm"), 1)
                for h in range(2):
                    for k in range(4):
                        if h == 0:
                            pe.wait_ge(S("turned"), 5 * c + k + 2)
                        else:
                            pe.wait_ge(S("score"), 8 * c + k + 1)
                        lhs = (bet, kd)[k // 2]
                        for b in range(2):
                            blk = 2 * (k % 2) + b
                            tk = slice(blk * P, (blk + 1) * P)
                            pe.matmul(ROT[k][:, 2 * b * P:(2 * b + 1) * P], lhs[rows[h], tk], kap[rows[h], tk],
                                      start=True, stop=True)
                            m = pe.matmul(ROT[k][:, (2 * b + 1) * P:(2 * b + 2) * P], lhs[rows[h], tk],
                                          rt[rows[h], q, tk], start=True, stop=True)
                        m.then_inc(S("score_mm"), 1)
                if not last:
                    loras(c + 1, 1 - q)
                if not first:
                    pe.wait_ge(S("score"), 8 * c + 5)
                    means(c - 1)
                fill(2)
                if not first:
                    pe.wait_ge(S("score"), 8 * c + 6)
                    variances(c - 1)
                fill(2)
                for lv in range(5):
                    for h in range(2):
                        if lv == 0 and h == 0 and not first:
                            pe.wait_ge(S("yc"), c)
                        if lv == 0:
                            pe.wait_ge(S("score"), 8 * c + 8)
                        if lv > 0:
                            pe.wait_ge(S("low"), 10 * c + 2 * (lv - 1) + h + 1)
                        if lv == 2 and h == 1 and not last:
                            pe.wait_ge(S("nclamp"), c + 2)
                        pe.wait_ge(S("inv"), INV(c, h, lv))
                        for b in range(TB):
                            m = pe.matmul(ROT[2 * h][:, b * P:(b + 1) * P], LA[:, h, b, 0:P], inv[:, h, b, :],
                                          start=True, stop=True)
                        m.then_inc(S("low_mm"), 1)
                    fill(1)
                    for h in range(2):
                        if lv == 0 and h == 0 and not first:
                            pe.wait_ge(S("yln"), c)
                        pe.wait_ge(S("low"), 10 * c + 2 * lv + h + 1)
                        lhs, rhs = (invT, low) if lv < 4 else (low, invT)
                        for b in range(TB):
                            m = pe.matmul(ROT[2 * h + 1][:, b * P:(b + 1) * P], lhs[:, h, b, :], rhs[:, h, b, :],
                                          start=True, stop=True)
                        m.then_inc(S("up_mm"), 1)
                    fill(2)
                    if lv == 1 and not last:
                        pe.wait_ge(S("low"), 10 * c + 4)
                        key_sums(c + 1)
                pe.wait_ge(S("low"), 10 * c + 9)
                for h in range(2):
                    for b in range(TB):
                        m = pe.matmul(ROT[MVB][:, (2 * b + h) * HD:(2 * b + h + 1) * HD], MK[:, h, b, 0:P],
                                      tok["v"][:, b, rows[h]], start=True, stop=True)
                m.then_inc(S("mv_mm"), 1)
                need(pe, S("y"), c)
                for h in range(2):
                    for b in range(TB):
                        pe.matmul(YB[rows[h], b * P:(b + 1) * P], tok["v"][:, b, rows[h]], MK[:, h, b, P:2 * P],
                                  start=(b == 0), stop=False, skip_group_check=True)
                pe.wait_ge(S("mv"), 2 * c + 2)
                for h in range(2):
                    pe.wait_ge(S("inv"), INV(c, h, 5))
                    if h == 0:
                        pe.wait_ge(S("low"), 10 * c + 10)
                    for b in range(TB):
                        m = pe.matmul(ROT[TKGB[h]][:, b * P:(b + 1) * P], invT[:, h, b, :], XK[:, h, b, :],
                                      start=True, stop=True)
                    m.then_inc(S("tkg_mm"), 1)
                fill(2)
                pe.wait_ge(S("tkg"), 2 * c + 2)
                apart(pe)
                for i in range(1, NCH - 1):
                    r = rows[i % 2]
                    for h in range(2):
                        m = pe.matmul(PH[i % 2][rows[h], (i - 1) * HD:i * HD], NTG[r, h, i // 2, 0:HD],
                                      tok["be"][r, i // 2, rows[h]], start=True, stop=True)
                m.then_inc(S("phi_mm"), 1)
                need(pe, S("st"), 7 * c)
                apart(pe)
                for i in range(NCH - 1):
                    r = rows[i % 2]
                    for h in range(2):
                        pe.matmul(SB[i % 2][rows[h], i * HD:(i + 1) * HD], tok["ke"][r, i // 2, rows[h]],
                                  tok["v"][r, i // 2, rows[h]], start=(i < 2), stop=False, skip_group_check=True)
                        m = pe.matmul(SB[i % 2][rows[h], i * HD:(i + 1) * HD], tok["be"][r, i // 2, rows[h]],
                                      NTG[r, h, i // 2, HD:P], start=False, stop=False, skip_group_check=True)
                m.then_inc(S("st_mm"), 1)
                for h in range(2):
                    for b in range(TB):
                        m = pe.matmul(ROT[RHB][rows[h], b * P:(b + 1) * P], NTG[:, h, b, 0:HD],
                                      LA[:, h, b, P:2 * P], start=True, stop=True)
                m.then_inc(S("rh_mm"), 1)
                for h in range(2):
                    for b in range(TB):
                        pe.matmul(YB[rows[h], b * P:(b + 1) * P], NTG[:, h, b, HD:P], LA[:, h, b, P:2 * P],
                                  start=False, stop=False, skip_group_check=True)
                pe.wait_ge(S("phi"), 2 * (c + 1))
                for i in range(1, NCH):
                    pe.wait_ge(S("st"), 7 * c + i)
                    apart(pe)
                    if i < NCH - 1:
                        for h in range(2):
                            m = pe.matmul(SB[i % 2][rows[h], i * HD:(i + 1) * HD], phi[rows[h], (i - 1) * HD:i * HD],
                                          st[rows[h], i, :], start=False, stop=True, skip_group_check=True)
                        m.then_inc(S("st_mm"), 1)
                    if i == 1:
                        pe.wait_ge(S("rh"), c + 1)
                        apart(pe)
                    for h in range(2):
                        m = pe.matmul(YB[rows[h], i * HD:(i + 1) * HD], st[rows[h], i, :],
                                      rh[rows[h], i * HD:(i + 1) * HD], start=False, stop=True,
                                      skip_group_check=True)
                    fill(1)
                m.then_inc(S("y_mm"), 1)
                fill(24)
                if not last:
                    pe.wait_ge(S("phi"), 2 * (c + 1))
                    bonus_sums(c + 1)

            loras(0, 0)
            for _ in gemm(0, 0):
                pass
            key_sums(0)
            bonus_sums(0)
            run(step)(pe)
            means(IC - 1)
            variances(IC - 1)

        @block.vector
        def _(dve):
            def channels(n, q):
                for name, k in (("kk0", 1), ("tanh", 2), ("bon", 1)):
                    need(dve, S(name), k * (n - 1))
                dve.tensor_copy(chan[:, q, :], mixpar[:, n, 0:6]).then_inc(S("chan"), 1)

            def affines(c):
                need(dve, S("affine"), c)
                dve.tensor_copy(affine[:, :], mixpar[:, c, 6:8]).then_inc(S("aff"), 1)

            def decay(n):
                dve.wait_ge(S("ld"), n + 1)
                need(dve, S("bet"), n)
                dve.tensor_tensor_scan(cum[:, :], C["scan_keep"], ld[:, :], 0.0, ALU.mult, ALU.add)\
                    .then_inc(S("cum"), 1)

            def keys(n):
                dve.wait_ge(S("kfac"), n + 1)
                dve.wait_ge(S("evac"), 3 * n + 1)
                dve.wait_ge(S("kk0"), n + 1)
                dve.tensor_tensor(kp[:, :], kraw[:, :], kp[:, :], ALU.mult).then_inc(S("kp"), 1)
                dve.wait_ge(S("kp"), n + 1)
                dve.wait_ge(S("exp"), 2 * n + 2)
                need(dve, S("score_mm"), 8 * n)
                dve.tensor_tensor(kd[:, :], kp[:, :], cum[:, :], ALU.mult).then_inc(S("kd"), 1)
                dve.wait_ge(S("kd"), n + 1)
                dve.tensor_tensor(chunks(ke[:, :]), chunks(kd[:, :]), ends(e1[:, :]), ALU.mult).then_inc(S("ke"), 1)

            def clamp(n):
                dve.wait_ge(S("nn_mm"), n + 1)
                dve.tensor_scalar(nn[:, :], ROT[NNB][:, :], 1e-24, None, ALU.max).then_inc(S("nclamp"), 1)

            def normed(n):
                dve.wait_ge(S("nrs"), n + 1)
                dve.tensor_tensor(kk[:, :], kk[:, :], nn[:, :], ALU.mult).then_inc(S("kk"), 1)

            def reads(n, p):
                dve.wait_ge(S("evac"), 3 * n + 2)
                dve.tensor_tensor(rt[:, p, :], rraw[:, :], e1[:, :], ALU.mult).then_inc(S("rt"), 1)
                need(dve, S("bsum_mm"), n)
                dve.scalar_tensor_tensor(out=bon[:, :], in0=rraw[:, :], scalar=chan[:, p, 5:6], in1=kp[:, :],
                                         op0=ALU.mult, op1=ALU.mult).then_inc(S("bon"), 1)

            def removals(n):
                dve.wait_ge(S("b"), n + 1)
                dve.tensor_tensor(bet[:, :], tha[:, :], cum[:, :], ALU.mult).then_inc(S("bet"), 1)
                dve.wait_ge(S("bet"), n + 1)
                dve.tensor_tensor(chunks(be[:, :]), chunks(bet[:, :]), ends(e1[:, :]), ALU.mult).then_inc(S("be"), 1)

            def bonuses(n, p):
                dve.wait_ge(S("bsum_mm"), n + 1)
                dve.wait_ge(S("evac"), 3 * n + 3)
                need(dve, S("plus"), n - 1)
                dve.tensor_tensor(bonus[:, p, :], ROT[BONB][:, :], vT[:, :], ALU.mult).then_inc(S("bonus"), 1)

            def center(c):
                dve.wait_ge(S("mean_mm"), c + 1)
                need(dve, S("affine"), c)
                dve.tensor_tensor(yc[:, :], y[:, :], ROT[MEANB][:, :], ALU.subtract).then_inc(S("yc"), 1)

            def scaled(c):
                dve.wait_ge(S("yrs"), c + 1)
                dve.tensor_tensor(yc[:, :], yc[:, :], yv[:, :], ALU.mult).then_inc(S("yn"), 1)

            def gated(c):
                dve.wait_ge(S("plus"), c + 1)
                dve.scalar_tensor_tensor(out=gate[:, c, :], in0=yv[:, :], scalar=0.5, in1=gate[:, c, :],
                                         op0=ALU.mult, op1=ALU.mult).then_inc(S("gated"), 1)

            def step(c, p=None):
                q = c % 2 if p is None else p
                last = isinstance(c, int) and c == IC - 1
                first = isinstance(c, int) and c == 0
                if not last:
                    channels(c + 1, 1 - q)
                if not first:
                    affines(c - 1)
                for h in range(2):
                    for k in range(4):
                        dve.wait_ge(S("score_mm"), 8 * c + 4 * h + k + 1)
                        dst = (LA, MK)[k // 2]
                        b = 2 * (k % 2)
                        dve.tensor_tensor(dst[:, h, b:b + 2, :], pairs(ROT[k][:, :]), over(C["score_mask"], 2),
                                          ALU.mult).then_inc(S("score"), 1)
                    dve.wait_ge(S("score"), 8 * c + 4 * h + 2)
                    dve.tensor_tensor(invT[:, h], LA[:, h, :, 0:P], over(C["level_first"], TB), ALU.mult)\
                        .then_inc(S("inv0"), 1)
                    dve.wait_ge(S("inv0"), 4 * c + 2 * h + 1)
                    dve.tensor_tensor(invT[:, h], invT[:, h], over(C["ident"], TB), ALU.add).then_inc(S("inv0"), 1)
                    dve.wait_ge(S("inv0"), 4 * c + 2 * h + 2)
                    dve.transpose(inv[:, h].rearrange("p b t -> p (b t)"), invT[:, h].rearrange("p b t -> p (b t)"))\
                        .then_inc(S("inv"), 1)
                if not first:
                    center(c - 1)
                for lv in range(5):
                    for h in range(2):
                        dve.wait_ge(S("low_mm"), 10 * c + 2 * lv + h + 1)
                        dve.tensor_tensor(low[:, h], blocks(ROT[2 * h][:, :]),
                                          over(C["level_mask"][:, lv * P:(lv + 1) * P], TB), ALU.mult)\
                            .then_inc(S("low"), 1)
                    if not last:
                        if lv == 0:
                            decay(c + 1)
                        if lv == 2:
                            keys(c + 1)
                        if lv == 3:
                            normed(c + 1)
                            removals(c + 1)
                    for h in range(2):
                        dve.wait_ge(S("up_mm"), 10 * c + 2 * lv + h + 1)
                        src = blocks(ROT[2 * h + 1][:, :])
                        if lv < 4:
                            dve.tensor_tensor(inv[:, h], inv[:, h], src, ALU.add).then_inc(S("inv_up"), 1)
                            dve.wait_ge(S("inv_up"), 8 * c + 2 * lv + h + 1)
                            dve.transpose(invT[:, h].rearrange("p b t -> p (b t)"),
                                          inv[:, h].rearrange("p b t -> p (b t)")).then_inc(S("inv"), 1)
                        else:
                            dve.tensor_tensor(invT[:, h], invT[:, h], src, ALU.add).then_inc(S("inv"), 1)
                    if lv == 0 and not first:
                        scaled(c - 1)
                    if lv == 1 and not last:
                        clamp(c + 1)
                    if lv == 2 and not first:
                        gated(c - 1)
                    if lv == 4 and not last:
                        reads(c + 1, 1 - q)
                dve.wait_ge(S("phi_mm"), c + 1)
                dve.wait_ge(S("dend"), c + 1)
                for i in range(2):
                    half = lambda ap: ap.rearrange("p (n t) -> p n t", t=2 * HD)[:, :, i * HD:(i + 1) * HD]
                    dve.tensor_tensor(half(phi[:, :]), half(PH[1 - i][:, 0:6 * HD]), half(dend[:, q, :]), ALU.add)\
                        .then_inc(S("phi"), 1)
                for i in range(1, NCH):
                    dve.wait_ge(S("st_mm"), 7 * c + i)
                    dve.tensor_copy(st[:, i, :], SB[(i - 1) % 2][:, (i - 1) * HD:i * HD]).then_inc(S("st"), 1)
                    if i == 1:
                        dve.wait_ge(S("rh_mm"), c + 1)
                        dve.tensor_tensor(rh[:, :], ROT[RHB][:, :], rt[:, q, :], ALU.add).then_inc(S("rh"), 1)
                if not last:
                    bonuses(c + 1, 1 - q)

            channels(0, 0)
            decay(0)
            keys(0)
            clamp(0)
            normed(0)
            removals(0)
            reads(0, 0)
            bonuses(0, 0)
            run(step)(dve)
            affines(IC - 1)
            center(IC - 1)
            scaled(IC - 1)
            gated(IC - 1)


def INV(c, h, lv):
    return 12 * c + 2 * lv + h + 1


def project_phase(K, tag, src, kt, weights, norms, load_x=False, store=False):
    nc, ins, bank, C, V, sbt, x = (K[n] for n in ("nc", "ins", "bank", "C", "V", "sbt", "x"))
    RING = 2
    with ExitStack() as ctx:
        S = Sems(nc, ctx, tag)
        ring = sbt(ctx, tag + "_ring", [P, RING, kt * P])
        sq = sbt(ctx, tag + "_sq", [P, 2, T])
        lnv = sbt(ctx, tag + "_lnv", [P, T])
        rstd = sbt(ctx, tag + "_rstd", [P, T])
        block = ctx.enter_context(nc.Block())

        def loop(eng, job):
            for s in range(RING):
                job(0, s)
            with eng.Fori(1, DC // RING) as i:
                for s in range(RING):
                    job(i, s)

        @block.sync
        def _(sp):
            def load(i, s):
                need(sp, S("mm"), RING * (i - 1) + s + 1)
                sp.dma_start(ring[:, s, :], ins[weights][RING * i + s]).then_inc(S(f"w{s}"), 16)

            if load_x:
                sp.dma_start(x[:, :, :], ins["x"]).then_inc(S("x"), 16)
            loop(sp, load)
            if store:
                for j in range(DC):
                    sp.wait_ge(S(norms[-1][0] + "_out"), j + 1)
                    sp.dma_start(K["out"][:, j, :], x[:, j, :]).then_inc(S("stored"), 16)
                sp.wait_ge(S("stored"), 16 * DC)

        @block.tensor
        def _(pe):
            def job(i, s):
                pe.wait_ge(S(f"w{s}"), 16 * i + 16)
                need(pe, S("added"), RING * (i - 1) + s + 1)
                for k in range(kt):
                    m = pe.matmul(bank[s][:, :], ring[:, s, k * P:(k + 1) * P], src[:, k, :], start=(k == 0),
                                  stop=(k == kt - 1))
                m.then_inc(S("mm"), 1)

            loop(pe, job)
            for n, (name, _, _) in enumerate(norms):
                norm_tensor(pe, S, name, C["row_mean"], sq, bank[4 + n][:, :])

        @block.scalar
        def _(act):
            for n, (name, _, _) in enumerate(norms):
                def ready(j, n=n):
                    if n == 0:
                        act.wait_ge(S("added"), j + 1)
                    else:
                        act.wait_ge(S(norms[n - 1][0] + "_out"), j + 1)
                norm_scalar(act, S, name, x, sq, bank[4 + n][:, :], lnv[:, :], rstd[:, :], K["eps"][:, 0:1], ready)

        @block.vector
        def _(dve):
            if load_x:
                dve.wait_ge(S("x"), 16)

            def add(i, s):
                n = RING * i + s
                dve.wait_ge(S("mm"), n + 1)
                dve.tensor_tensor(x[:, n, :], x[:, n, :], bank[s][:, :], ALU.add).then_inc(S("added"), 1)

            loop(dve, add)
            for name, gain, dst in norms:
                norm_vector(dve, S, name, x, V[gain], rstd[:, :], dst)


def conv_phase(K):
    nc, ins, bank, C, V, sbt, h, gate = (K[n] for n in ("nc", "ins", "bank", "C", "V", "sbt", "h", "gate"))
    JOBS = 4
    with ExitStack() as ctx:
        S = Sems(nc, ctx, "conv")
        ring = sbt(ctx, "conv_ring", [P, JOBS, DC * P])
        u, cu, cv, th, gg = (sbt(ctx, "conv_" + n, [P, T]) for n in ("u", "cu", "cv", "th", "gg"))
        taps = sbt(ctx, "conv_taps", [P, IC, 3])
        tap = sbt(ctx, "conv_tap", [P, 2, 3])
        block = ctx.enter_context(nc.Block())

        def loop(eng, chunk):
            chunk(0, 0)
            chunk(1, 1)
            with eng.Fori(1, IC // 2) as i:
                chunk(2 * i, 0)
                chunk(2 * i + 1, 1)

        @block.sync
        def _(sp):
            def load(n, q=None):
                for j in range(JOBS):
                    need(sp, S("mm"), JOBS * (n - 1) + j + 1)
                    sp.dma_start(ring[:, j, :], ins["w_conv"][n, j]).then_inc(S(f"w{j}"), 16)

            loop(sp, load)

        @block.tensor
        def _(pe):
            def chunk(n, q):
                for j in range(JOBS):
                    pe.wait_ge(S(f"w{j}"), 16 * n + 16)
                    need(pe, S(("u", "cu", "gg", "bg")[j]), n - 1)
                    for k in range(DC):
                        m = pe.matmul(bank[4 * q + j][:, :], ring[:, j, k * P:(k + 1) * P], h[:, k, :],
                                      start=(k == 0), stop=(k == DC - 1))
                    m.then_inc(S("mm"), 1)

            loop(pe, chunk)

        @block.scalar
        def _(act):
            def chunk(n, q):
                act.wait_ge(S("mm"), JOBS * n + 1)
                need(act, S("cu"), n)
                act.activation(u[:, :], bank[4 * q][:, :], ACT.Copy).then_inc(S("u"), 1)
                act.wait_ge(S("cu"), n + 1)
                act.wait_ge(S("tap"), n + 1)
                need(act, S("bg"), n)
                act.activation(cv[:, :], cu[:, :], ACT.Copy, scale=tap[:, q, 2:3]).then_inc(S("tap2"), 1)
                act.wait_ge(S("mm"), JOBS * n + 3)
                need(act, S("gg"), n)
                act.activation(th[:, :], bank[4 * q + 2][:, :], ACT.Tanh, scale=0.5).then_inc(S("th"), 1)

            loop(act, chunk)

        @block.vector
        def _(dve):
            for j in range(3):
                dve.tensor_copy(taps[:, :, j], V["b_conv"][:, j * IC:(j + 1) * IC]).then_inc(S("taps"), 1)
            dve.wait_ge(S("taps"), 3)

            def chunk(n, q):
                need(dve, S("tap2"), n - 1)
                need(dve, S("taps1"), n - 1)
                dve.tensor_copy(tap[:, q, :], taps[:, n, :]).then_inc(S("tap"), 1)
                dve.wait_ge(S("u"), n + 1)
                dve.wait_ge(S("mm"), JOBS * n + 2)
                need(dve, S("taps1"), n)
                dve.tensor_tensor(cu[:, :], bank[4 * q + 1][:, :], u[:, :], ALU.mult).then_inc(S("cu"), 1)
                dve.wait_ge(S("tap2"), n + 1)
                dve.wait_ge(S("tap"), n + 1)
                dve.scalar_tensor_tensor(out=cv[:, 1:T], in0=cu[:, 0:T - 1], scalar=tap[:, q, 1:2], in1=cv[:, 1:T],
                                         op0=ALU.mult, op1=ALU.add).then_inc(S("taps2"), 1)
                dve.wait_ge(S("taps2"), n + 1)
                dve.scalar_tensor_tensor(out=cv[:, 2:T], in0=cu[:, 0:T - 2], scalar=tap[:, q, 0:1], in1=cv[:, 2:T],
                                         op0=ALU.mult, op1=ALU.add).then_inc(S("taps1"), 1)
                dve.wait_ge(S("th"), n + 1)
                need(dve, S("cg"), n)
                dve.scalar_tensor_tensor(out=gg[:, :], in0=th[:, :], scalar=1.0, in1=bank[4 * q + 2][:, :],
                                         op0=ALU.add, op1=ALU.mult).then_inc(S("gg"), 1)
                dve.wait_ge(S("taps1"), n + 1)
                dve.wait_ge(S("gg"), n + 1)
                dve.scalar_tensor_tensor(out=cv[:, :], in0=cv[:, :], scalar=0.5, in1=gg[:, :],
                                         op0=ALU.mult, op1=ALU.mult).then_inc(S("cg"), 1)
                dve.wait_ge(S("mm"), JOBS * n + 4)
                dve.wait_ge(S("cg"), n + 1)
                dve.tensor_tensor(gate[:, n, :], cv[:, :], bank[4 * q + 3][:, :], ALU.mult).then_inc(S("bg"), 1)

            loop(dve, chunk)


def input_phase(K):
    nc, ins, bank, sbt, h, proj, vals = (K[n] for n in ("nc", "ins", "bank", "sbt", "h", "proj", "vals"))
    RING, NCHN, NTOK = 4, 16, 4
    with ExitStack() as ctx:
        S = Sems(nc, ctx, "in2")
        ring = sbt(ctx, "in2_ring", [P, RING, DC * P])
        block = ctx.enter_context(nc.Block())

        def loop(eng, job, last):
            for s in range(RING):
                job(0, s)
            with eng.Fori(1, last) as i:
                for s in range(RING):
                    job(i, s)

        @block.sync
        def _(sp):
            def load(i, s):
                need(sp, S("mm"), RING * (i - 1) + s + 1)
                sp.dma_start(ring[:, s, :], ins["w_in2"][RING * i + s]).then_inc(S(f"w{s}"), 16)

            loop(sp, load, (NCHN + NTOK) // RING)

        @block.tensor
        def _(pe):
            def job(i, s):
                pe.wait_ge(S(f"w{s}"), 16 * i + 16)
                need(pe, S("copied"), RING * (i - 1) + s + 1)
                for k in range(DC):
                    m = pe.matmul(bank[s][:, :], ring[:, s, k * P:(k + 1) * P], h[:, k, :], start=(k == 0),
                                  stop=(k == DC - 1))
                m.then_inc(S("mm"), 1)

            loop(pe, job, NCHN // RING)
            for s in range(NTOK):
                pe.wait_ge(S(f"w{s}"), 16 * (NCHN // RING) + 16)
                pe.wait_ge(S("copied"), NCHN - RING + s + 1)
                for b in range(TB):
                    for k in range(DC):
                        m = pe.matmul(bank[s][:, b * P:(b + 1) * P], h[:, k, b * P:(b + 1) * P],
                                      ring[:, s, k * P:(k + 1) * P], start=(k == 0), stop=(k == DC - 1))
                m.then_inc(S("mm"), 1)

        @block.scalar
        def _(act):
            def job(i, s):
                act.wait_ge(S("mm"), RING * i + s + 1)
                act.activation(proj[:, RING * i + s, :], bank[s][:, :], ACT.Copy).then_inc(S("copied"), 1)

            loop(act, job, NCHN // RING)
            for s in range(NTOK):
                act.wait_ge(S("mm"), NCHN + s + 1)
                act.activation(vals[:, :, s * P:(s + 1) * P], bank[s][:, :].rearrange("p (b t) -> p b t", t=P),
                               ACT.Copy).then_inc(S("copied"), 1)


def mixer_phase(K):
    nc, ins, bank, C, V, sbt, proj, vals, mixed = (K[n] for n in ("nc", "ins", "bank", "C", "V", "sbt", "proj",
                                                                  "vals", "mixed"))
    SB_SCALE, DF_SCALE = 64 ** -0.5, 32 ** -0.5
    LAM_INIT = 0.8 - 0.6 * float(np.exp(0.0))
    SLOPE = [2.0 ** (-8.0 * (n + 1) / 4) for n in range(4)]
    GELU = float(np.sqrt(2.0 / np.pi))
    with ExitStack() as ctx:
        S = Sems(nc, ctx, "mixer")
        t_ = lambda name, shape: sbt(ctx, name, shape)
        wbd = t_("wbd", [P, 2, 4, P])
        lp = t_("lp", [P, 16, 4])
        m4 = lp[:, 7, :]
        xc, rr, ii, la, aa, g1, g2, gl = (t_("lru_" + n, [P, T]) for n in ("xc", "rr", "ii", "la", "aa", "g1", "g2", "gl"))
        za, sp_, ex = (t_("sb_" + n, [P, TB, T]) for n in ("za", "sp", "ex"))
        dist = t_("dist", [P, DIST[-1]])
        bias = t_("bias", [P, DIST[-1]])
        pr = [t_(f"pr{m}", [P, DIST[-1]]) for m in range(2)]
        pT = t_("pT", [P, TB, T])
        ds_ = t_("ds", [P, 5, 2, TB])
        lam = t_("lam", [P, 4, 32])
        lamp = t_("lamp", [P, 2, 32])
        lams = t_("lams", [P, 8])
        gsub = t_("gsub", [P, 1])
        do, dsq = t_("do", [P, T]), t_("dsq", [P, T])
        one = t_("one", [P, 1])
        rows = (slice(0, HD), slice(HD, P))
        block = ctx.enter_context(nc.Block())
        N = lambda i: T - i * P

        @block.sync
        def _(sp):
            sp.wait_ge(S("wbd0"), 1)
            for r in range(2):
                for g in range(2):
                    sp.dma_start(wbd[rows[r], g, :, rows[r]], ins["w_lru"][rows[r], g]).then_inc(S("wbd"), 16)
            sp.dma_start(dist[:, :], ins["distance"]).then_inc(S("dist"), 16)
            sp.dma_start(lam[:, :, :], ins["lam"].rearrange("(o a) b -> o a b", o=1).broadcast_to([P, 4, 32]))\
                .then_inc(S("lam"), 16)

        @block.gpsimd
        def _(pool):
            pool.memset(wbd[:, :, :, :], 0.0).then_inc(S("wbd0"), 1)
            pool.memset(one[:, :], 1.0).then_inc(S("one"), 1)
            pool.wait_ge(S("dist"), 16)
            for n in range(4):
                pool.wait_ge(S("lru_th"), n + 1)
                pool.tensor_scalar(g1[:, :], g1[:, :], -2.0, 1e-18, ALU.mult, ALU.max).then_inc(S("lru_tm"), 1)
                pool.wait_ge(S("ysq"), n + 1)
                pool.tensor_scalar(gl[:, :], gl[:, :], 0.044715, 1.0, ALU.mult, ALU.add).then_inc(S("ycube"), 1)
                pool.wait_ge(S("ycube"), n + 1)
                pool.tensor_tensor(gl[:, :], gl[:, :], proj[:, 4 + n, :], ALU.mult).then_inc(S("yin"), 1)
                for i in range(TB):
                    pool.wait_ge(S("relu"), 4 * n + i + 1)
                    pool.wait_ge(S("sb_ln"), 4 * n + i + 1)
                    pool.tensor_tensor(sp_[:, i, 0:N(i)], sp_[:, i, 0:N(i)], za[:, i, 0:N(i)], ALU.add)\
                        .then_inc(S("sp"), 1)
                need(pool, S("dscore"), 8 * n)
                pool.tensor_scalar(bias[:, :], dist[:, :], -SLOPE[n], None, ALU.mult).then_inc(S("bias"), 1)

        @block.tensor
        def _(pe):
            pe.wait_ge(S("wbd"), 64)
            for n in range(4):
                hp = rows[n % 2]
                pe.wait_ge(S("conv"), 3 * n + 3)
                need(pe, S("din_last"), n)
                for g in range(2):
                    pe.matmul(bank[g][:, :], wbd[:, g, n, :], xc[:, :], start=True, stop=True).then_inc(S("rg_mm"), 1)
                for i in range(TB):
                    pe.matmul(bank[2 + i][:, 0:N(i)], proj[hp, 10 + n // 2, i * P:(i + 1) * P],
                              proj[hp, 8 + n // 2, i * P:T], start=True, stop=True).then_inc(S("z_mm"), 1)
                for i in range(TB - 1, -1, -1):
                    pe.wait_ge(S("spm"), 4 * (n + 1))
                    m = pe.matmul(bank[2 + i][:, 0:N(i)], C["minus_after"], sp_[:, i, 0:N(i)], start=True,
                                  stop=(i == TB - 1), skip_group_check=True)
                    for j in range(i + 1, TB):
                        m = pe.matmul(bank[2 + i][:, (j - i) * P:N(i)], C["minus_all"], sp_[:, j, 0:N(j)],
                                      start=False, stop=(j == TB - 1), skip_group_check=True)
                m.then_inc(S("tail_mm"), 1)
                need(pe, S("sb_out"), n // 2)
                for i in range(TB):
                    pe.wait_ge(S("wm"), 4 * n + i + 1)
                    m = pe.matmul(bank[6][hp, i * P:T], vals[:, i, n * HD:(n + 1) * HD], ex[:, i, 0:N(i)],
                                  start=(i == 0), stop=(i == TB - 1), skip_group_check=True)
                m.then_inc(S("sb_mm"), 1)
                pe.wait_ge(S("wm"), 4 * n + 4)
                for b in range(TB):
                    for m_ in range(2):
                        k = 2 * b + m_
                        need(pe, S("dscore"), 8 * n + k - 3 if k >= 4 else 0)
                        r = slice(hp.start + 32 * m_, hp.start + 32 * m_ + 32)
                        pe.matmul(bank[2 + k % 4][:, 0:(b + 1) * P], proj[r, 12 + n // 2, b * P:(b + 1) * P],
                                  proj[r, 14 + n // 2, 0:(b + 1) * P], start=True, stop=True)\
                            .then_inc(S("d_mm"), 1)
                pe.wait_ge(S("dscore"), 8 * n + 8)
                for b in range(TB):
                    pe.wait_ge(S("dp"), 4 * n + b + 1)
                    for j in range(b + 1):
                        m = pe.transpose(bank[2 + b][:, j * P:(j + 1) * P],
                                         pr[0][:, DIST[b] + j * P:DIST[b] + (j + 1) * P], C["ident"])
                    m.then_inc(S("pT_mm"), 1)
                pe.wait_ge(S("pT"), 4 * n + 4)
                need(pe, S("dln"), n // 2)
                for j in range(TB):
                    m = pe.matmul(bank[7][hp, j * P:T], vals[:, j, 256 + n * HD:256 + (n + 1) * HD], pT[:, j, j * P:T],
                                  start=(j == 0), stop=(j == TB - 1), skip_group_check=True)
                m.then_inc(S("do_mm"), 1)
                if n % 2:
                    pe.wait_ge(S("dsq"), n // 2 + 1)
                    pe.matmul(bank[7][:, :], C["head_mean"], dsq[:, :], start=True, stop=True).then_inc(S("dv_mm"), 1)

        @block.scalar
        def _(act):
            act.wait_ge(S("one"), 1)
            act.activation(lp[:, 0, :], V["lru_lambda_2"], ACT.Abs).then_inc(S("sp_abs"), 1)
            act.wait_ge(S("sp_abs"), 1)
            act.activation(lp[:, 1, :], lp[:, 0, :], ACT.Exp, scale=-1.0).then_inc(S("sp_e"), 1)
            act.wait_ge(S("sp_u"), 1)
            act.activation(lp[:, 3, :], lp[:, 2, :], ACT.Ln).then_inc(S("sp_ln"), 1)
            act.wait_ge(S("lam_sum"), 2)
            act.activation(lams[:, 2:4], lams[:, 0:2], ACT.Exp).then_inc(S("lam_e"), 1)
            for n in range(4):
                act.wait_ge(S("chp"), 1)
                need(act, S("hl"), n)
                act.activation(xc[:, :], proj[:, n, :], ACT.Identity, bias=V["conv_a_b_2"][:, n:n + 1],
                               scale=V["conv_a_w_2"][:, 12 + n:13 + n]).then_inc(S("xc0"), 1)
                for g, dst in enumerate((rr, ii)):
                    act.wait_ge(S("rg_mm"), 2 * n + g + 1)
                    act.activation(dst[:, :], bank[g][:, :], ACT.Tanh, bias=lp[:, 8 + g, n:n + 1], scale=0.5)\
                        .then_inc(S("gate"), 1)
                act.activation(gl[:, :], proj[:, 4 + n, :], ACT.Square).then_inc(S("ysq"), 1)
                act.wait_ge(S("la"), n + 1)
                act.activation(g1[:, :], la[:, :], ACT.Tanh).then_inc(S("lru_th"), 1)
                act.wait_ge(S("yin"), n + 1)
                act.activation(gl[:, :], gl[:, :], ACT.Tanh, scale=GELU).then_inc(S("yth"), 1)
                act.activation(aa[:, :], la[:, :], ACT.Exp).then_inc(S("lru_a"), 1)
                act.wait_ge(S("one_minus"), n + 1)
                act.activation(g2[:, :], g2[:, :], ACT.Ln).then_inc(S("ln2"), 1)
                act.wait_ge(S("lru_tm"), n + 1)
                act.activation(g1[:, :], g1[:, :], ACT.Ln).then_inc(S("ln1"), 1)
                for i in range(TB):
                    act.wait_ge(S("z_mm"), 4 * n + i + 1)
                    need(act, S("sp"), 4 * n)
                    act.activation(za[:, i, 0:N(i)], bank[2 + i][:, 0:N(i)], ACT.Abs, scale=SB_SCALE)\
                        .then_inc(S("zabs"), 1)
                    act.wait_ge(S("zabs"), 4 * n + i + 1)
                    act.activation(za[:, i, 0:N(i)], za[:, i, 0:N(i)], ACT.Exp, scale=-1.0).then_inc(S("sb_e"), 1)
                    act.wait_ge(S("sb_e"), 4 * n + i + 1)
                    act.activation(za[:, i, 0:N(i)], za[:, i, 0:N(i)], ACT.Ln, bias=one[:, 0:1]).then_inc(S("sb_ln"), 1)
                act.wait_ge(S("lndiff"), n + 1)
                act.activation(g1[:, :], g1[:, :], ACT.Exp, scale=0.5).then_inc(S("gam"), 1)
                for i in range(TB):
                    act.wait_ge(S("sum"), 4 * n + i + 1)
                    act.activation(ex[:, i, 0:N(i)], ex[:, i, 0:N(i)], ACT.Exp).then_inc(S("w"), 1)
                if n % 2:
                    act.wait_ge(S("sb_mm"), n + 1)
                    act.activation(mixed[:, 4 + n // 2, :], bank[6][:, :], ACT.Copy).then_inc(S("sb_out"), 1)
                for b in range(TB):
                    for m_ in range(2):
                        act.wait_ge(S("dmax"), 8 * n + 2 * b + m_ + 1)
                        act.activation(pr[m_][:, DIST[b]:DIST[b + 1]], pr[m_][:, DIST[b]:DIST[b + 1]], ACT.Exp,
                                       bias=ds_[:, 0, m_, b:b + 1], accum_out=ds_[:, 1, m_, b:b + 1])\
                            .then_inc(S("dexp"), 1)
                for b in range(TB):
                    act.wait_ge(S("pT_mm"), 4 * n + b + 1)
                    act.activation(pT[:, 0:b + 1, b * P:(b + 1) * P],
                                   bank[2 + b][:, 0:(b + 1) * P].rearrange("p (j t) -> p j t", t=P), ACT.Copy)\
                        .then_inc(S("pT"), 1)
                if n % 2:
                    act.wait_ge(S("do_mm"), n + 1)
                    need(act, S("dout"), n // 2)
                    act.activation(do[:, :], bank[7][:, :], ACT.Copy).then_inc(S("do"), 1)
                    act.activation(dsq[:, :], bank[7][:, :], ACT.Square).then_inc(S("dsq"), 1)
                    act.wait_ge(S("dv_mm"), n // 2 + 1)
                    act.activation(dsq[:, :], bank[7][:, :], ACT.Ln, bias=K["eps"][:, 0:1]).then_inc(S("dln"), 1)
                    act.wait_ge(S("dln"), n // 2 + 1)
                    act.activation(dsq[:, :], dsq[:, :], ACT.Exp, scale=-0.5).then_inc(S("drs"), 1)

        @block.vector
        def _(dve):
            lamb = V["lru_lambda_2"]
            seq = [0]

            def then(ins_):
                seq[0] += 1
                ins_.then_inc(S("small"), 1)
                dve.wait_ge(S("small"), seq[0])

            then(dve.tensor_scalar(lp[:, 8, :], V["b_rgate_2"], 0.5, None, ALU.mult))
            then(dve.tensor_scalar(lp[:, 9, :], V["b_igate_2"], 0.5, None, ALU.mult))
            then(dve.tensor_scalar(gsub[:, :], V["subln_g_2"], 1.0 - LAM_INIT, None, ALU.mult))
            dve.wait_ge(S("sp_e"), 1)
            dve.tensor_scalar(lp[:, 2, :], lp[:, 1, :], 1.0, None, ALU.add).then_inc(S("sp_u"), 1)
            dve.wait_ge(S("sp_u"), 1)
            then(dve.tensor_scalar(lp[:, 4, :], lp[:, 2, :], -1.0, None, ALU.add))
            then(dve.tensor_scalar(lp[:, 5, :], lp[:, 4, :], 0.0, None, ALU.is_equal))
            then(dve.tensor_tensor(lp[:, 4, :], lp[:, 4, :], lp[:, 5, :], ALU.add))
            then(dve.reciprocal(lp[:, 4, :], lp[:, 4, :]))
            dve.wait_ge(S("sp_ln"), 1)
            then(dve.tensor_tensor(lp[:, 4, :], lp[:, 4, :], lp[:, 3, :], ALU.mult))
            then(dve.tensor_tensor(lp[:, 4, :], lp[:, 4, :], lp[:, 5, :], ALU.add))
            then(dve.tensor_tensor(lp[:, 4, :], lp[:, 4, :], lp[:, 1, :], ALU.mult))
            then(dve.tensor_scalar(lp[:, 6, :], lamb, -1.0, 0.0, ALU.mult, ALU.max))
            then(dve.tensor_tensor(lp[:, 4, :], lp[:, 4, :], lp[:, 6, :], ALU.add))
            dve.tensor_scalar(m4, lp[:, 4, :], -4.0, None, ALU.mult).then_inc(S("chp"), 1)
            dve.wait_ge(S("chp"), 1)
            dve.wait_ge(S("lam"), 16)
            for k in range(2):
                then(dve.tensor_tensor(lamp[:, k, :], lam[:, 2 * k, :], lam[:, 2 * k + 1, :], ALU.mult))
                dve.tensor_reduce(lams[:, k:k + 1], lamp[:, k, :], AX_X, ALU.add).then_inc(S("lam_sum"), 1)
            dve.wait_ge(S("lam_e"), 1)
            then(dve.tensor_tensor(lams[:, 4:5], lams[:, 3:4], lams[:, 2:3], ALU.subtract))
            then(dve.tensor_scalar(lams[:, 5:6], lams[:, 4:5], -LAM_INIT, None, ALU.add))
            for n in range(4):
                for k in range(3):
                    if k == 0:
                        dve.wait_ge(S("xc0"), n + 1)
                    else:
                        dve.wait_ge(S("conv"), 3 * n + k)
                    dve.scalar_tensor_tensor(out=xc[:, k + 1:T], in0=proj[:, n, 0:T - k - 1],
                                             scalar=V["conv_a_w_2"][:, 4 * (2 - k) + n:4 * (2 - k) + n + 1],
                                             in1=xc[:, k + 1:T], op0=ALU.mult, op1=ALU.add).then_inc(S("conv"), 1)
                dve.wait_ge(S("gate"), 2 * n + 1)
                dve.tensor_scalar(la[:, :], rr[:, :], m4[:, n:n + 1], m4[:, n:n + 1], ALU.mult, ALU.add)\
                    .then_inc(S("la"), 1)
                dve.wait_ge(S("gate"), 2 * n + 2)
                dve.wait_ge(S("conv"), 3 * n + 3)
                dve.scalar_tensor_tensor(out=ii[:, :], in0=ii[:, :], scalar=1.0, in1=xc[:, :], op0=ALU.add,
                                         op1=ALU.mult).then_inc(S("ix"), 1)
                for i in range(TB):
                    dve.wait_ge(S("z_mm"), 4 * n + i + 1)
                    dve.tensor_scalar(sp_[:, i, 0:N(i)], bank[2 + i][:, 0:N(i)], SB_SCALE, 0.0, ALU.mult,
                                      ALU.max).then_inc(S("relu"), 1)
                dve.wait_ge(S("lru_th"), n + 1)
                need(dve, S("ln2"), n)
                dve.wait_ge(S("lru_tm"), n + 1)
                dve.tensor_scalar(g2[:, :], g1[:, :], 0.5, 1.0, ALU.mult, ALU.add).then_inc(S("one_minus"), 1)
                for i in range(TB):
                    dve.wait_ge(S("sp"), 4 * n + i + 1)
                    dve.scalar_tensor_tensor(out=ex[:, i, 0:N(i)], in0=bank[2 + i][:, 0:N(i)], scalar=SB_SCALE,
                                             in1=sp_[:, i, 0:N(i)], op0=ALU.mult, op1=ALU.subtract)\
                        .then_inc(S("logw"), 1)
                    dve.wait_ge(S("logw"), 4 * n + i + 1)
                    dve.wait_ge(S("zabs"), 4 * n + i + 1)
                    dve.tensor_tensor(sp_[:, i, 0:P], sp_[:, i, 0:P], C["before"], ALU.mult).then_inc(S("spm"), 1)
                dve.wait_ge(S("ln1"), n + 1)
                dve.wait_ge(S("ln2"), n + 1)
                dve.tensor_tensor(g1[:, :], g1[:, :], g2[:, :], ALU.subtract).then_inc(S("lndiff"), 1)
                dve.wait_ge(S("tail_mm"), n + 1)
                for i in range(TB):
                    dve.wait_ge(S("logw"), 4 * n + 4)
                    dve.tensor_tensor(ex[:, i, 0:N(i)], ex[:, i, 0:N(i)], bank[2 + i][:, 0:N(i)], ALU.add)\
                        .then_inc(S("sum"), 1)
                dve.wait_ge(S("gam"), n + 1)
                dve.wait_ge(S("ix"), n + 1)
                dve.scalar_tensor_tensor(out=ii[:, :], in0=ii[:, :], scalar=0.5, in1=g1[:, :], op0=ALU.mult,
                                         op1=ALU.mult).then_inc(S("u"), 1)
                dve.wait_ge(S("u"), n + 1)
                dve.wait_ge(S("lru_a"), n + 1)
                dve.tensor_tensor_scan(rr[:, :], aa[:, :], ii[:, :], 0.0, ALU.mult, ALU.add).then_inc(S("hl"), 1)
                dve.wait_ge(S("yth"), n + 1)
                dve.scalar_tensor_tensor(out=gl[:, :], in0=gl[:, :], scalar=1.0, in1=proj[:, 4 + n, :], op0=ALU.add,
                                         op1=ALU.mult).then_inc(S("gelu"), 1)
                dve.wait_ge(S("gelu"), n + 1)
                dve.wait_ge(S("hl"), n + 1)
                dve.scalar_tensor_tensor(out=mixed[:, n, :], in0=rr[:, :], scalar=0.5, in1=gl[:, :], op0=ALU.mult,
                                         op1=ALU.mult).then_inc(S("din_last"), 1)
                for i in range(TB):
                    dve.wait_ge(S("w"), 4 * n + i + 1)
                    dve.tensor_tensor(ex[:, i, 0:P], ex[:, i, 0:P], C["before"], ALU.mult).then_inc(S("wm"), 1)
                dve.wait_ge(S("bias"), n + 1)
                for b in range(TB):
                    for m_ in range(2):
                        k = 8 * n + 2 * b + m_ + 1
                        w_ = (b + 1) * P
                        part = pr[m_][:, DIST[b]:DIST[b + 1]]
                        dve.wait_ge(S("d_mm"), k)
                        dve.scalar_tensor_tensor(out=part, in0=bank[2 + (2 * b + m_) % 4][:, 0:w_], scalar=DF_SCALE,
                                                 in1=bias[:, DIST[b]:DIST[b + 1]], op0=ALU.mult, op1=ALU.add)\
                            .then_inc(S("dscore"), 1)
                        dve.wait_ge(S("dscore"), k)
                        dve.tensor_reduce(ds_[:, 2, m_, b:b + 1], part, AX_X, ALU.max).then_inc(S("dm"), 1)
                        dve.wait_ge(S("dm"), k)
                        dve.tensor_scalar(ds_[:, 0, m_, b:b + 1], ds_[:, 2, m_, b:b + 1], -1.0, None, ALU.mult)\
                            .then_inc(S("dmax"), 1)
                for b in range(TB):
                    k = 8 * n + 2 * b
                    dve.wait_ge(S("dexp"), k + 2)
                    dve.reciprocal(ds_[:, 3, :, b:b + 1], ds_[:, 1, :, b:b + 1]).then_inc(S("drec"), 1)
                    dve.wait_ge(S("drec"), 4 * n + b + 1)
                    dve.tensor_scalar(ds_[:, 4, 1, b:b + 1], ds_[:, 3, 1, b:b + 1], lams[:, 5:6], None, ALU.mult)\
                        .then_inc(S("dlam"), 1)
                    dve.tensor_scalar(pr[0][:, DIST[b]:DIST[b + 1]], pr[0][:, DIST[b]:DIST[b + 1]],
                                      ds_[:, 3, 0, b:b + 1], None, ALU.mult).then_inc(S("dp0"), 1)
                    dve.wait_ge(S("dp0"), 4 * n + b + 1)
                    dve.wait_ge(S("dlam"), 4 * n + b + 1)
                    dve.scalar_tensor_tensor(out=pr[0][:, DIST[b]:DIST[b + 1]], in0=pr[1][:, DIST[b]:DIST[b + 1]],
                                             scalar=ds_[:, 4, 1, b:b + 1], in1=pr[0][:, DIST[b]:DIST[b + 1]],
                                             op0=ALU.mult, op1=ALU.add).then_inc(S("dp"), 1)
                if n % 2:
                    dve.wait_ge(S("drs"), n // 2 + 1)
                    dve.scalar_tensor_tensor(out=mixed[:, 6 + n // 2, :], in0=do[:, :], scalar=gsub[:, 0:1],
                                             in1=dsq[:, :], op0=ALU.mult, op1=ALU.mult).then_inc(S("dout"), 1)


def up_phase(K):
    nc, ins, bank, V, sbt, h, ff = (K[n] for n in ("nc", "ins", "bank", "V", "sbt", "h", "ff"))
    JOBS = 4
    with ExitStack() as ctx:
        S = Sems(nc, ctx, "up")
        ring = sbt(ctx, "up_ring", [P, JOBS, DC * P])
        z = sbt(ctx, "up_z", [P, 2, T])
        u = sbt(ctx, "up_u", [P, 2, T])
        th = sbt(ctx, "up_th", [P, T])
        cols = sbt(ctx, "up_cols", [P, FC, 8])
        col = sbt(ctx, "up_col", [P, 2, 8])
        block = ctx.enter_context(nc.Block())

        def loop(eng, chunk):
            chunk(0, 0)
            chunk(1, 1)
            with eng.Fori(1, FC // 2) as i:
                chunk(2 * i, 0)
                chunk(2 * i + 1, 1)

        @block.sync
        def _(sp):
            def load(n, q):
                for g in range(2):
                    need(sp, S("mm"), 2 * (n - 2) + g + 1)
                    sp.dma_start(ring[:, 2 * q + g, :], ins["w_up"][n, g]).then_inc(S(f"w{2 * q + g}"), 16)

            loop(sp, load)

        @block.tensor
        def _(pe):
            def chunk(n, q):
                for g in range(2):
                    pe.wait_ge(S(f"w{2 * q + g}"), 8 * n + 16 if q == 0 else 8 * n + 8)
                    need(pe, S("u0"), 2 * (n - 1) + g - 1)
                    for k in range(DC):
                        m = pe.matmul(bank[2 * q + g][:, :], ring[:, 2 * q + g, k * P:(k + 1) * P], h[:, k, :],
                                      start=(k == 0), stop=(k == DC - 1))
                    m.then_inc(S("mm"), 1)

            loop(pe, chunk)

        @block.scalar
        def _(act):
            def chunk(n, q):
                act.wait_ge(S("col"), n + 1)
                for g in range(2):
                    act.wait_ge(S("mm"), 2 * n + g + 1)
                    need(act, S("tap1"), 2 * (n - 1) + g + 1)
                    act.activation(z[:, g, :], bank[2 * q + g][:, :], ACT.Copy).then_inc(S("z"), 1)
                    need(act, S("ff"), n)
                    act.activation(u[:, g, :], bank[2 * q + g][:, :], ACT.Identity, bias=col[:, q, 4 * g + 3:4 * g + 4],
                                   scale=col[:, q, 4 * g + 2:4 * g + 3]).then_inc(S("u0"), 1)
                act.wait_ge(S("tap1"), 2 * n + 1)
                act.activation(th[:, :], u[:, 0, :], ACT.Tanh, scale=0.5).then_inc(S("th"), 1)

            loop(act, chunk)

        @block.vector
        def _(dve):
            for g in range(2):
                for k in range(3):
                    at = 2 * FC * k + FC * g
                    dve.tensor_copy(cols[:, :, 4 * g + k], V["conv_ff_w_2"][:, at:at + FC]).then_inc(S("cols"), 1)
                dve.tensor_copy(cols[:, :, 4 * g + 3], V["conv_ff_b_2"][:, FC * g:FC * (g + 1)]).then_inc(S("cols"), 1)
            dve.wait_ge(S("cols"), 8)

            def chunk(n, q):
                need(dve, S("u0"), 2 * (n - 1))
                need(dve, S("tap1"), 2 * (n - 1))
                dve.tensor_copy(col[:, q, :], cols[:, n, :]).then_inc(S("col"), 1)
                for g in range(2):
                    dve.wait_ge(S("u0"), 2 * n + g + 1)
                    if g == 0:
                        dve.wait_ge(S("col"), n + 1)
                    dve.scalar_tensor_tensor(out=u[:, g, 1:T], in0=z[:, g, 0:T - 1],
                                             scalar=col[:, q, 4 * g + 1:4 * g + 2], in1=u[:, g, 1:T],
                                             op0=ALU.mult, op1=ALU.add).then_inc(S("tap2"), 1)
                    dve.wait_ge(S("tap2"), 2 * n + g + 1)
                    dve.scalar_tensor_tensor(out=u[:, g, 2:T], in0=z[:, g, 0:T - 2],
                                             scalar=col[:, q, 4 * g:4 * g + 1], in1=u[:, g, 2:T],
                                             op0=ALU.mult, op1=ALU.add).then_inc(S("tap1"), 1)
                dve.wait_ge(S("th"), n + 1)
                dve.scalar_tensor_tensor(out=u[:, 0, :], in0=th[:, :], scalar=1.0, in1=u[:, 0, :], op0=ALU.add,
                                         op1=ALU.mult).then_inc(S("silu"), 1)
                dve.wait_ge(S("silu"), n + 1)
                dve.scalar_tensor_tensor(out=ff[:, n, :], in0=u[:, 0, :], scalar=0.5, in1=u[:, 1, :], op0=ALU.mult,
                                         op1=ALU.mult).then_inc(S("ff"), 1)

            loop(dve, chunk)


def tiles(w):
    k, n = w.shape
    return np.ascontiguousarray(w.reshape(k // P, P, n // P, P).transpose(2, 1, 0, 3)).reshape(n // P, P, k)


def layout(inputs):
    a = {k: np.asarray(v) for k, v in inputs.items()}
    o = {"consts": constants(), "distance": distances()}
    a["subln_g_2"] = np.tile(a["subln_g_2"], (1, 2))
    vec = lambda n: a[n].reshape(-1, P).T
    o["params"] = np.ascontiguousarray(np.concatenate([vec(n) for n, _ in PARAMS], 1))
    o["x"] = np.ascontiguousarray(a["x"][0].T.reshape(DC, P, T).transpose(1, 0, 2))
    lora = np.concatenate([a["a_w1"][0], a["a_a1"][0]], 1)
    o["lora1"] = np.ascontiguousarray(lora.reshape(DC, P, P).transpose(1, 0, 2))
    lora = np.concatenate([a["a_w2"][0], a["a_a2"][0]], 0)
    o["lora2"] = np.ascontiguousarray(lora.reshape(P, IC, P).transpose(1, 0, 2))
    for n, name in enumerate("rkvg"):
        o["w_" + name] = tiles(a["a_w_in"][0, n])
    o["w_out1"] = tiles(a["a_w_out"][0])
    cbug = tiles(a["b_w_in"][0]).reshape(4, IC, P, D)
    o["w_conv"] = np.ascontiguousarray(cbug[[2, 0, 3, 1]].transpose(1, 0, 2, 3))
    o["w_out2"] = tiles(a["b_w_out"][0])
    o["w_in2"] = tiles(a["w_in_2"][0][:, IN_ORDER])
    o["w_lru"] = np.ascontiguousarray(np.stack([a["w_rgate_2"][0], a["w_igate_2"][0]]).reshape(2, 4, 2, HD, HD)
                                      .transpose(2, 3, 0, 1, 4)).reshape(P, 2, 4, HD)
    o["lam"] = np.ascontiguousarray(np.stack([a[n][0] for n in ("lam_q1_2", "lam_k1_2", "lam_q2_2", "lam_k2_2")]))
    o["w_out3"] = tiles(a["w_out_2"][0])
    up = tiles(a["w_ff_up_2"][0]).reshape(2, FC, P, D)
    o["w_up"] = np.ascontiguousarray(up.transpose(1, 0, 2, 3))
    o["w_down"] = tiles(a["w_ff_down_2"][0])
    return o


def kernel(**inputs):
    import concourse.bacc as bacc
    from concourse.bass_utils import run_bass_kernel_spmd

    nc = bacc.Bacc("TRN2", target_bir_lowering=False, num_devices=1)
    arrays = layout(inputs)
    ins = {n: nc.dram_tensor(f"in_{n}", a.shape, F32, kind="ExternalInput").ap() for n, a in arrays.items()}
    out = nc.dram_tensor("out_y", (P, DC, T), F32, kind="ExternalOutput").ap()
    program(nc, ins, out)
    r = run_bass_kernel_spmd(nc, [{f"in_{n}": a for n, a in arrays.items()}], core_ids=[0])
    y = r.results[0]["out_y"]
    return np.ascontiguousarray(y.transpose(2, 1, 0).reshape(1, T, D))
```

```python
from contextlib import ExitStack

import numpy as np
import concourse.bass as bass
from concourse import mybir

ALU = mybir.AluOpType
ACT = mybir.ActivationFunctionType
AX_X = mybir.AxisListType.X
F32 = mybir.dt.float32
F32R = mybir.dt.float32r

P = 128
T = 512
D = 1024
DC = D // P
DI = 2048
IC = DI // P
HD = 64
NCH = T // HD
TB = T // P
LORA = 64
RMS_EPS = 1e-6
GN_EPS = 64e-5
EXP_HALF = 0.6065306597126334
LRU = 512
DFF = 2816
FC = DFF // P
PIN = 2560
IN_ORDER = np.r_[0:1536, 1792:2304, 1536:1792, 2304:2560]
LVL = 6
FAR = 1e30
DIST = [0, 1 * P, 3 * P, 6 * P, 10 * P]
LN2 = 0.6931471805599453

PARAMS = [("a_norm", D), ("a_mu", 6 * D), ("a_w0", DI), ("a_a0", DI), ("a_kk", DI), ("a_ka", DI), ("a_rk", DI),
          ("a_lnw", DI), ("a_lnb", DI), ("b_norm", D), ("b_conv", 3 * DI), ("final_norm", D), ("norm1_g_2", D),
          ("conv_a_w_2", 4 * LRU), ("conv_a_b_2", LRU), ("b_rgate_2", LRU), ("b_igate_2", LRU), ("lru_lambda_2", LRU),
          ("subln_g_2", P),
          ("norm2_g_2", D), ("conv_ff_w_2", 6 * DFF), ("conv_ff_b_2", 2 * DFF), ("final_g_2", D)]
PCOL = {}
_at = 0
for _name, _len in PARAMS:
    PCOL[_name] = _at
    _at += _len // P
NPAR = _at

CONSTS = [("ident", P), ("head_sum", P), ("head_mean", P), ("row_mean", P), ("score_mask", 2 * P),
          ("level_first", P), ("level_mask", 5 * P), ("scan_keep", T), ("eye", 6 * HD),
          ("minus_after", P), ("minus_all", P), ("before", P)]
CCOL = {}
_at = 0
for _name, _len in CONSTS:
    CCOL[_name] = _at
    _at += _len
NCON = _at


def constants():
    c = np.zeros((P, NCON), np.float32)
    i, j = np.meshgrid(np.arange(P), np.arange(P), indexing="ij")
    same = (i // HD) == (j // HD)

    def put(name, a):
        c[:, CCOL[name]:CCOL[name] + a.shape[1]] = a

    put("ident", i == j)
    put("head_sum", same)
    put("head_mean", same / HD)
    put("row_mean", np.full((P, P), 1.0 / D))
    put("score_mask", np.concatenate([-1.0 * (same & (j > i)), 1.0 * (same & (j >= i))], 1))
    below = lambda n: (i // (2 * n) == j // (2 * n)) & (i % (2 * n) >= n) & (j % (2 * n) < n)
    put("level_first", below(1).T)
    put("level_mask", np.concatenate([below(1 << k) for k in range(1, LVL)], 1))
    put("scan_keep", np.tile((np.arange(T) % HD != 0), (P, 1)))
    put("eye", np.tile(np.eye(HD), (2, 6)))
    put("minus_after", -1.0 * (i > j))
    put("minus_all", -np.ones((P, P)))
    put("before", i < j)
    return c


def distances():
    d = np.zeros((P, DIST[-1]), np.float32)
    for b in range(TB):
        t, s = np.meshgrid(b * P + np.arange(P), np.arange((b + 1) * P), indexing="ij")
        d[:, DIST[b]:DIST[b + 1]] = np.where(s // HD <= t // HD, np.abs(t - s), FAR)
    return d


def need(eng, sem, n):
    if isinstance(n, int) and n <= 0:
        return
    eng.wait_ge(sem, n)


def apart(eng):
    eng.nop(nofuse=True)


class Sems:

    def __init__(self, nc, ctx, phase):
        self.nc, self.ctx, self.phase, self.have = nc, ctx, phase, {}
        ctx.callback(self.clear)

    def __call__(self, name):
        if name not in self.have:
            self.have[name] = self.ctx.enter_context(self.nc.semaphore(f"{self.phase}_{name}"))
        return self.have[name]

    def clear(self):
        numbers = sorted(s.num for s in self.have.values())
        first = 0
        for n in range(1, len(numbers) + 1):
            if n == len(numbers) or numbers[n] != numbers[n - 1] + 1:
                self.nc.gpsimd.sem_clear(range(numbers[first], numbers[n - 1] + 1))
                first = n
        self.nc.all_engine_barrier()


def products(pe, out, w_hi, w_lo, x_hi, x_lo, ks, first=True, last=True):
    for n, k in enumerate(ks):
        w = slice(n * P, (n + 1) * P)
        pe.matmul(out, w_hi[:, w], x_hi[:, k, :], start=(first and n == 0), stop=False)
        pe.matmul(out, w_hi[:, w], x_lo[:, k, :], start=False, stop=False)
        m = pe.matmul(out, w_lo[:, w], x_hi[:, k, :], start=False, stop=(last and n == len(ks) - 1))
    return m


def split_lo(dve, lo, full, hi):
    return dve.tensor_tensor(lo, full, hi.bitcast(F32), ALU.subtract)


def norm_squares(act, S, tag, x, sq, ready):
    for j in range(DC):
        ready(j)
        need(act, S(tag + "_sum"), j - 1)
        act.activation(sq[:, j % 2, :], x[:, j, :], ACT.Square).then_inc(S(tag + "_sq"), 1)


def norm_tensor(pe, S, tag, row_mean, sq, bank):
    for j in range(DC):
        pe.wait_ge(S(tag + "_sq"), j + 1)
        pe.matmul(bank, row_mean, sq[:, j % 2, :], start=(j == 0), stop=(j == DC - 1)).then_inc(S(tag + "_sum"), 1)


def norm_factor(act, S, tag, bank, rstd, eps):
    act.activation(rstd, bank, ACT.Ln, bias=eps).then_inc(S(tag + "_ln"), 1)
    act.wait_ge(S(tag + "_ln"), 1)
    act.activation(rstd, rstd, ACT.Exp, scale=-0.5).then_inc(S(tag + "_rstd"), 1)


def norm_vector(dve, S, tag, x, g, rstd, out):
    dve.wait_ge(S(tag + "_rstd"), 1)
    for j in range(DC):
        dve.scalar_tensor_tensor(out=out[:, j, :], in0=x[:, j, :], scalar=g[:, j:j + 1], in1=rstd,
                                 op0=ALU.mult, op1=ALU.mult).then_inc(S(tag + "_out"), 1)


NORM_BANK = 4


def head_scalar(act, S, K, rstd, tmp, split):
    norm_factor(act, S, "norm", K["bank"][NORM_BANK][:, :], rstd, K["eps"][:, 0:1])
    split(0)
    split(1)
    for k in range(DC):
        act.wait_ge(S("norm_out"), k + 1)
        act.activation(K["h"][0][:, k, :], tmp[:, k % 2, :], ACT.Copy).then_inc(S("norm_hi"), 1)
        if k in (1, 3):
            split(2 + k // 2)


def head_vector(dve, S, K, gain, rstd, tmp, split):
    hi, lo = K["h"]

    def scaled(k):
        need(dve, S("norm_lo"), k - 1)
        dve.scalar_tensor_tensor(out=tmp[:, k % 2, :], in0=K["x"][:, k, :], scalar=K["V"][gain][:, k:k + 1],
                                 in1=rstd, op0=ALU.mult, op1=ALU.mult).then_inc(S("norm_out"), 1)

    dve.wait_ge(S("norm_rstd"), 1)
    scaled(0)
    scaled(1)
    split(0)
    split(1)
    for k in range(DC):
        dve.wait_ge(S("norm_hi"), k + 1)
        split_lo(dve, lo[:, k, :], tmp[:, k % 2, :], hi[:, k, :]).then_inc(S("norm_lo"), 1)
        if k + 2 < DC:
            scaled(k + 2)
        if k in (1, 3):
            split(2 + k // 2)


def head_tensor(pe, S, K, banks, w_hi, w_lo):
    half = DC // 2
    for first in (0, half):
        for pair in (0, 2):
            for k in range(first, first + half):
                if pair == 0:
                    pe.wait_ge(S("norm_lo"), k + 1)
                for j in (pair, pair + 1):
                    if k == 0:
                        pe.wait_ge(S("wlo"), j + 1)
                    m = products(pe, banks[j][:, :], w_hi[:, j, k * P:], w_lo[:, j, k * P:], *K["h"], [k],
                                 k == 0, k == DC - 1)
                    if k == DC - 1:
                        m.then_inc(S("mm"), 1)


def program(nc, ins, out, stop_after=None):
    with ExitStack() as top:
        def sbt(ctx, name, shape, dt=F32, side="left"):
            return ctx.enter_context(nc.sbuf_tensor(name, shape, dt, side=side))

        def pair(ctx, name, chunks, side="left"):
            return [sbt(ctx, name + part, [P, chunks, T], F32R, side) for part in ("_hi", "_lo")]

        bank = [top.enter_context(nc.psum_tensor(f"bank{i}", [P, T], F32)) for i in range(8)]
        con = sbt(top, "con", [P, NCON])
        par = sbt(top, "par", [P, NPAR])
        eps = sbt(top, "eps", [P, 3])
        C = {n: con[:, CCOL[n]:CCOL[n] + k] for n, k in CONSTS}
        V = {n: par[:, PCOL[n]:PCOL[n] + k // P] for n, k in PARAMS}
        K = dict(nc=nc, ins=ins, out=out, bank=bank, C=C, V=V, eps=eps, con=con, par=par, sbt=sbt, pair=pair)
        with ExitStack() as right:
            gate = K["gate"] = sbt(right, "gate", [P, IC, T], side="right")
            with ExitStack() as left:
                K["lerp"] = {n: sbt(left, f"lerp_{n}", [P, DC, T]) for n in "rkv"}
                K["hidden"] = sbt(left, "hidden", [P, T])
                K["mixpar"] = sbt(left, "mixpar", [P, IC, 8])
                lerp_phase(K)
                rwkv_phase(K)
            if stop_after == "rwkv":
                return
            x = K["x"] = sbt(top, "x", [P, DC, T])
            norms = top.enter_context(ExitStack())
            h = K["h"] = pair(norms, "h", DC)
            with ExitStack() as inner:
                y = K["y"] = pair(inner, "y", IC, "right")
                project_phase(K, "out1", y, IC, "w_out1", load_x=True, full=gate)
                conv_phase(K)
                project_phase(K, "out2", y, IC, "w_out2", norm="final_norm")
            if stop_after == "x3":
                return
            mix = top.enter_context(ExitStack())
            mixed = K["mixed"] = sbt(mix, "mixed", [P, DC, T])
            K["proj"] = gate
            with ExitStack() as left:
                K["vals"] = sbt(left, "vals", [P, TB, 4 * P])
                input_phase(K)
                mixer_phase(K)
            if stop_after == "mixed":
                return
        with ExitStack() as right:
            y = pair(right, "m", DC, "right")
            project_phase(K, "out3", y, DC, "w_out3", full=mixed)
        mix.close()
        with ExitStack() as right:
            ff = K["ff"] = pair(right, "ff", FC, "right")
            up_phase(K)
            norms.close()
            project_phase(K, "down", ff, FC, "w_down", norm="final_g_2", squares=False, store=True)


def lerp_phase(K):
    nc, ins, bank, C, V = (K[n] for n in ("nc", "ins", "bank", "C", "V"))
    eps, gate, lerp, hidden, mixpar = (K[n] for n in ("eps", "gate", "lerp", "hidden", "mixpar"))
    RING = 2
    with ExitStack() as ctx:
        S = Sems(nc, ctx, "lerp")
        x = K["sbt"](ctx, "x_in", [P, DC, T])
        xx = K["sbt"](ctx, "xx", [P, DC, T])
        tmp = [gate[:, 0:DC, :], x]
        h = gate[:, DC:2 * DC, :]
        xg_hi, xg_lo = K["pair"](ctx, "xg", DC)
        raw, w_hi, w_lo = (K["sbt"](ctx, "g_" + n, [P, RING, DC * P], t) for n, t in
                           (("raw", F32), ("hi", F32R), ("lo", F32R)))
        tmp2 = K["sbt"](ctx, "xg_full", [P, 2, T])
        wl = K["sbt"](ctx, "lora_w1", [P, DC, P])
        sq = K["sbt"](ctx, "sq", [P, 2, T])
        rstd = K["sbt"](ctx, "rstd", [P, T])
        thg = K["sbt"](ctx, "thg", [P, 2, T])
        block = ctx.enter_context(nc.Block())
        mu = V["a_mu"].rearrange("p (j c) -> p j c", j=6)
        MU = {"r": 0, "w": 1, "k": 2, "v": 3, "a": 4, "g": 5}
        dst = {"w": tmp[0], "a": tmp[1], **lerp}

        @block.sync
        def _(sp):
            sp.dma_start(K["con"][:, :], ins["consts"]).then_inc(S("const"), 16)
            sp.dma_start(x[:, :, :], ins["x"]).then_inc(S("x"), 16)
            sp.dma_start(K["par"][:, :], ins["params"]).then_inc(S("param"), 16)
            sp.dma_start(wl[:, :, :], ins["lora1"]).then_inc(S("wl"), 16)

            def load(i, s):
                need(sp, S("wlo"), RING * (i - 1) + s + 1)
                sp.dma_start(raw[:, s, :], ins["w_g"][RING * i + s]).then_inc(S(f"w{s}"), 16)

            for s in range(RING):
                load(0, s)
            with sp.Fori(1, IC // RING) as i:
                for s in range(RING):
                    load(i, s)

        @block.gpsimd
        def _(pool):
            for n, v in enumerate((RMS_EPS, GN_EPS, 10 * LN2)):
                pool.memset(eps[:, n:n + 1], v).then_inc(S("eps"), 1)
            pool.wait_ge(S("param"), 16)
            for n, (name, a, b) in enumerate((("a_w0", 0.5, 0.0), ("a_a0", 0.5, 0.0), ("a_ka", 0.5, 0.0),
                                              ("a_ka", -0.5, 1.0), ("a_kk", 1.0, 0.0), ("a_rk", 1.0, 0.0),
                                              ("a_lnw", 1.0, 0.0), ("a_lnb", 1.0, 0.0))):
                pool.tensor_scalar(mixpar[:, :, n], V[name], a, b, ALU.mult, ALU.add).then_inc(S("mixpar"), 1)

        @block.scalar
        def _(act):
            act.wait_ge(S("eps"), 3)
            norm_squares(act, S, "norm", x, sq, lambda j: act.wait_ge(S("x"), 16) if j == 0 else None)
            act.wait_ge(S("norm_sum"), DC)
            norm_factor(act, S, "norm", bank[0][:, :], rstd[:, :], eps[:, 0:1])

            def split(i, s):
                act.wait_ge(S(f"w{s}"), 16 * i + 16)
                need(act, S("g_mm"), RING * (i - 1) + s + 1)
                act.activation(w_hi[:, s, :], raw[:, s, :], ACT.Copy).then_inc(S("whi"), 1)

            for s in range(RING):
                split(0, s)
            for j in range(DC):
                act.wait_ge(S("lerp_g"), j + 1)
                act.activation(xg_hi[:, j, :], tmp2[:, j % 2, :], ACT.Copy).then_inc(S("xg_hi"), 1)
            act.wait_ge(S("hid_mm"), 1)
            act.activation(hidden[0:LORA, :], bank[1][0:LORA, :], ACT.Tanh).then_inc(S("hid"), 1)
            act.wait_ge(S("hid_mm"), 2)
            act.activation(hidden[LORA:P, :], bank[1][LORA:P, :], ACT.Copy).then_inc(S("hid"), 1)

            def job(i, s, more=True):
                n = RING * i + s
                act.wait_ge(S("g_mm"), n + 1)
                if more:
                    split(i + 1, s)
                need(act, S("gate"), n - 1)
                act.activation(thg[:, s % 2, :], bank[2 + s][:, :], ACT.Tanh, scale=0.5).then_inc(S("thg"), 1)

            for s in range(RING):
                job(0, s)
            with act.Fori(1, IC // RING - 1) as i:
                for s in range(RING):
                    job(i, s)
            for s in range(RING):
                job(IC // RING - 1, s, False)

        @block.tensor
        def _(pe):
            pe.wait_ge(S("const"), 16)
            norm_tensor(pe, S, "norm", C["row_mean"], sq, bank[0][:, :])
            pe.wait_ge(S("wl"), 16)
            for n, (lo, hi) in enumerate(((0, LORA), (LORA, P))):
                for j in range(DC):
                    pe.wait_ge(S("lerp"), DC * n + j + 1)
                    m = pe.matmul(bank[1][lo:hi, :], wl[:, j, lo:hi], tmp[n][:, j, :], start=(j == 0),
                                  stop=(j == DC - 1))
                m.then_inc(S("hid_mm"), 1)

            def job(i, s):
                pe.wait_ge(S("wlo"), RING * i + s + 1)
                need(pe, S("gate"), RING * (i - 1) + s + 1)
                if isinstance(i, int) and s == 0:
                    pe.wait_ge(S("xg_lo"), DC)
                products(pe, bank[2 + s][:, :], w_hi[:, s, :], w_lo[:, s, :], xg_hi, xg_lo, range(DC))\
                    .then_inc(S("g_mm"), 1)

            for s in range(RING):
                job(0, s)
            with pe.Fori(1, IC // RING) as i:
                for s in range(RING):
                    job(i, s)

        @block.vector
        def _(dve):
            dve.wait_ge(S("param"), 16)
            norm_vector(dve, S, "norm", x, V["a_norm"], rstd[:, :], h)
            for j in range(DC):
                dve.wait_ge(S("norm_out"), j + 1)
                dve.tensor_tensor(xx[:, j, 1:T], h[:, j, 0:T - 1], h[:, j, 1:T], ALU.subtract).then_inc(S("xx"), 1)
                dve.tensor_scalar(xx[:, j, 0:1], h[:, j, 0:1], -1.0, None, ALU.mult).then_inc(S("xx"), 1)
            dve.wait_ge(S("xx"), 2 * DC)

            def lerps(name):
                for j in range(DC):
                    dve.scalar_tensor_tensor(out=dst[name][:, j, :], in0=xx[:, j, :],
                                             scalar=mu[:, MU[name], j:j + 1], in1=h[:, j, :],
                                             op0=ALU.mult, op1=ALU.add).then_inc(S("lerp"), 1)

            def split(i, s):
                dve.wait_ge(S("whi"), RING * i + s + 1)
                split_lo(dve, w_lo[:, s, :], raw[:, s, :], w_hi[:, s, :]).then_inc(S("wlo"), 1)

            def gate_input():
                def lo(j):
                    dve.wait_ge(S("xg_hi"), j + 1)
                    split_lo(dve, xg_lo[:, j, :], tmp2[:, j % 2, :], xg_hi[:, j, :]).then_inc(S("xg_lo"), 1)

                for j in range(DC):
                    need(dve, S("xg_lo"), j - 1)
                    dve.scalar_tensor_tensor(out=tmp2[:, j % 2, :], in0=xx[:, j, :], scalar=mu[:, MU["g"], j:j + 1],
                                             in1=h[:, j, :], op0=ALU.mult, op1=ALU.add).then_inc(S("lerp_g"), 1)
                    if j:
                        lo(j - 1)
                lo(DC - 1)

            for s in range(RING):
                split(0, s)
            lerps("w")
            lerps("a")
            gate_input()
            for name in "rkv":
                lerps(name)
            dve.wait_ge(S("lerp"), DC * 5)
            dve.wait_ge(S("hid_mm"), 2)

            def job(i, s, more=True):
                n = RING * i + s
                if more:
                    split(i + 1, s)
                dve.wait_ge(S("thg"), n + 1)
                dve.scalar_tensor_tensor(out=gate[:, n, :], in0=thg[:, s % 2, :], scalar=1.0,
                                         in1=bank[2 + s][:, :], op0=ALU.add, op1=ALU.mult).then_inc(S("gate"), 1)

            for s in range(RING):
                job(0, s)
            with dve.Fori(1, IC // RING - 1) as i:
                for s in range(RING):
                    job(i, s)
            for s in range(RING):
                job(IC // RING - 1, s, False)


def rwkv_phase(K):
    nc, ins, bank, C, V = (K[n] for n in ("nc", "ins", "bank", "C", "V"))
    eps, gate, lerp, hidden, mixpar, sbt = (K[n] for n in ("eps", "gate", "lerp", "hidden", "mixpar", "sbt"))
    with ExitStack() as ctx:
        S = Sems(nc, ctx, "mix")
        ring = {n: sbt(ctx, f"w_{n}", [P, DC * P]) for n in "krv"}
        lora = sbt(ctx, "w_lora2", [P, P])
        kap, bet, kd, ke, be, vT = (sbt(ctx, n, [P, T]) for n in ("kap", "bet", "kd", "ke", "be", "vT"))
        rt, bonus = sbt(ctx, "rt", [P, 2, T]), sbt(ctx, "bonus", [P, 2, T])
        dend = sbt(ctx, "dend", [P, 2, 6 * HD])
        ld, cum, e1, tha, kp, kraw, kk, nn, rraw, bon = (
            sbt(ctx, n, [P, T]) for n in ("ld", "cum", "e1", "tha", "kp", "kraw", "kk", "nn", "rraw", "bon"))
        LA = sbt(ctx, "LA", [P, 2, TB, 2 * P])
        MK = sbt(ctx, "MK", [P, 2, TB, 2 * P])
        XK = sbt(ctx, "XK", [P, 2, TB, P])
        NTG = sbt(ctx, "NTG", [P, 2, TB, P])
        tok = {n: sbt(ctx, f"{n}_tok", [P, TB, P]) for n in ("ke", "be", "v")}
        inv, invT, low = (sbt(ctx, n, [P, 2, TB, P]) for n in ("inv", "invT", "low"))
        rh = sbt(ctx, "rh", [P, T])
        phi = sbt(ctx, "phi", [P, 6 * HD])
        st = sbt(ctx, "st", [P, NCH, HD])
        y = sbt(ctx, "y", [P, T])
        yc, yv = sbt(ctx, "yc", [P, T]), sbt(ctx, "yv", [P, T])
        chan = sbt(ctx, "chan", [P, 2, 6])
        affine = sbt(ctx, "affine", [P, 2])
        block = ctx.enter_context(nc.Block())

        G, YB, ROT = bank[0:2], bank[2], bank[4:8]
        SB = (bank[3], ROT[2])
        PH = (ROT[3], ROT[0])
        MEANB, VARB, NNB, BONB = 0, 1, 2, 3
        MVB, TKGB, RHB = 0, (1, 2), 1
        chunks = lambda ap: ap.rearrange("p (n t) -> p n t", t=HD)
        blocks = lambda ap: ap.rearrange("p (b t) -> p b t", t=P)
        pairs = lambda ap: ap.rearrange("p (b t) -> p b t", t=2 * P)
        over = lambda ap, n: ap.rearrange("p (o k) -> p o k", o=1).broadcast_to([P, n, ap.shape[1]])
        ends = lambda ap: chunks(ap)[:, :, HD - 1:HD].broadcast_to([P, NCH, HD])
        rows = (slice(0, HD), slice(HD, P))
        JOBS = ["w", "a", "k", "r", "v"]
        NJ = len(JOBS)

        def run(step):
            def loop(eng):
                step(0)
                step(1)
                with eng.Fori(1, IC // 2 - 1) as i:
                    step(2 * i, 0)
                    step(2 * i + 1, 1)
                step(IC - 2)
                step(IC - 1)
            return loop

        @block.sync
        def _(sp):
            def load(c, p=None):
                for n, name in enumerate("krv"):
                    need(sp, S("gemm"), NJ * (c - 1) + 3 + n)
                    sp.dma_start(ring[name][:, :], ins["w_" + name][c]).then_inc(S("w_" + name), 16)
                    if n == 0:
                        sp.dma_start(lora[:, :], ins["lora2"][c]).then_inc(S("w_lora"), 16)

            load(0)
            load(1)
            with sp.Fori(2, IC) as c:
                load(c)

        @block.gpsimd
        def _(pool):
            def prepare(n, p):
                pool.wait_ge(S("tanh"), 2 * n + 1)
                apart(pool)
                pool.tensor_scalar(ld[:, :], ld[:, :], -EXP_HALF / 2, -EXP_HALF / 2, ALU.mult, ALU.add)\
                    .then_inc(S("ld"), 1)
                pool.wait_ge(S("tanh"), 2 * n + 2)
                need(pool, S("bon"), n)
                apart(pool)
                pool.tensor_scalar(kp[:, :], tha[:, :], chan[:, p, 2:3], chan[:, p, 3:4], ALU.mult, ALU.add)\
                    .then_inc(S("kfac"), 1)
                pool.wait_ge(S("kfac"), n + 1)
                apart(pool)
                pool.tensor_scalar(tha[:, :], tha[:, :], 0.5, 0.5, ALU.mult, ALU.add).then_inc(S("a"), 1)

            def prepare_keys(n, p):
                pool.wait_ge(S("evac"), 3 * n + 1)
                need(pool, S("kap"), 2 * n)
                apart(pool)
                pool.tensor_scalar(kk[:, :], kraw[:, :], chan[:, p, 4:5], None, ALU.mult).then_inc(S("kk0"), 1)
                pool.wait_ge(S("exp"), 2 * n + 1)
                need(pool, S("phi"), 2 * (n - 1))
                pool.tensor_tensor(dend[:, p, :].rearrange("p (n t) -> p n t", t=HD),
                                   C["eye"].rearrange("p (n t) -> p n t", t=HD),
                                   chunks(e1[:, :])[:, 1:7, HD - 1:HD].broadcast_to([P, 6, HD]), ALU.mult)\
                    .then_inc(S("dend"), 1)
                pool.wait_ge(S("kk"), n + 1)
                pool.wait_ge(S("a"), n + 1)
                pool.tensor_tensor(tha[:, :], tha[:, :], kk[:, :], ALU.mult).then_inc(S("b"), 1)
                need(pool, S("score_mm"), 8 * n)
                pool.tensor_tensor(chunks(kap[:, :])[:, :, 1:HD], chunks(kk[:, :])[:, :, 1:HD],
                                   chunks(e1[:, :])[:, :, 0:HD - 1], ALU.mult).then_inc(S("kap"), 1)
                apart(pool)
                pool.tensor_scalar(chunks(kap[:, :])[:, :, 0:1], chunks(kk[:, :])[:, :, 0:1], 1.0, None, ALU.mult)\
                    .then_inc(S("kap"), 1)

            def finish(c, p):
                pool.wait_ge(S("yn"), c + 1)
                pool.wait_ge(S("aff"), c + 1)
                apart(pool)
                pool.tensor_scalar(yv[:, :], yc[:, :], affine[:, 0:1], affine[:, 1:2], ALU.mult, ALU.add)\
                    .then_inc(S("affine"), 1)
                pool.wait_ge(S("affine"), c + 1)
                pool.wait_ge(S("bonus"), c + 1)
                pool.tensor_tensor(yv[:, :], yv[:, :], bonus[:, p, :], ALU.add).then_inc(S("plus"), 1)

            def step(c, p=None):
                q = c % 2 if p is None else p
                last = isinstance(c, int) and c == IC - 1
                if not last:
                    prepare(c + 1, 1 - q)
                if not (isinstance(c, int) and c == 0):
                    finish(c - 1, 1 - q)
                if not last:
                    prepare_keys(c + 1, 1 - q)

            prepare(0, 0)
            prepare_keys(0, 0)
            run(step)(pool)
            finish(IC - 1, 1)

        @block.scalar
        def _(act):
            def tanhs(n, q):
                act.wait_ge(S("gemm"), NJ * n + 1)
                act.wait_ge(S("chan"), n + 1)
                need(act, S("cum"), n)
                act.activation(ld[:, :], G[(q + 0) % 2][:, :], ACT.Tanh, bias=chan[:, q, 0:1], scale=0.5)\
                    .then_inc(S("tanh"), 1)
                act.wait_ge(S("gemm"), NJ * n + 2)
                need(act, S("bet"), n)
                act.activation(tha[:, :], G[(q + 1) % 2][:, :], ACT.Tanh, bias=chan[:, q, 1:2], scale=0.5)\
                    .then_inc(S("tanh"), 1)

            def evacuate(n, q, k, dst, readers):
                act.wait_ge(S("gemm"), NJ * n + 3 + k)
                for name, count in readers:
                    need(act, S(name), count)
                act.activation(dst, G[(q + k) % 2][:, :], ACT.Copy).then_inc(S("evac"), 1)

            def exps(n):
                act.wait_ge(S("cum"), n + 1)
                need(act, S("rt"), n)
                need(act, S("kap"), 2 * n)
                act.activation(e1[:, :], cum[:, :], ACT.Exp).then_inc(S("exp"), 1)
                act.wait_ge(S("exp"), 2 * n + 1)
                act.activation(cum[:, :], cum[:, :], ACT.Exp, scale=-1.0).then_inc(S("exp"), 1)

            def key_square(n):
                act.wait_ge(S("kk0"), n + 1)
                need(act, S("kk"), n)
                act.activation(nn[:, :], kk[:, :], ACT.Square).then_inc(S("nsq"), 1)

            def key_norm(n):
                act.wait_ge(S("nclamp"), n + 1)
                act.activation(nn[:, :], nn[:, :], ACT.Ln, scale=float(2 ** 20)).then_inc(S("nln"), 1)
                act.wait_ge(S("nln"), n + 1)
                act.activation(nn[:, :], nn[:, :], ACT.Exp, scale=-0.5, bias=eps[:, 2:3]).then_inc(S("nrs"), 1)

            def center_square(c):
                act.wait_ge(S("yc"), c + 1)
                need(act, S("gated"), c)
                act.activation(yv[:, :], yc[:, :], ACT.Square).then_inc(S("ysq"), 1)

            def group_norm(c):
                act.wait_ge(S("var_mm"), c + 1)
                act.activation(yv[:, :], ROT[VARB][:, :], ACT.Ln, bias=eps[:, 1:2]).then_inc(S("yln"), 1)
                act.wait_ge(S("yln"), c + 1)
                act.activation(yv[:, :], yv[:, :], ACT.Exp, scale=-0.5).then_inc(S("yrs"), 1)

            def step(c, p=None):
                last = isinstance(c, int) and c == IC - 1
                first = isinstance(c, int) and c == 0
                q = c % 2 if p is None else p
                for k in range(4):
                    act.wait_ge(S("turn_mm"), 4 * c + k + 1)
                    src = blocks(ROT[k][:, :])
                    if k == 0:
                        src = src.rearrange("p b (h k) -> p h b k", h=2)
                        for h in range(2):
                            act.activation(XK[:, h, :, 0:HD], src[:, h], ACT.Copy).then_inc(S("turned"), 1)
                    else:
                        act.activation(tok[("ke", "be", "v")[k - 1]][:, :, :], src, ACT.Copy)\
                            .then_inc(S("turned"), 1)
                if not last:
                    tanhs(c + 1, 1 - q)
                if not first:
                    center_square(c - 1)
                    group_norm(c - 1)
                if not last:
                    exps(c + 1)
                    evacuate(c + 1, 1 - q, 0, kraw[:, :], [("kp", c + 1)])
                    key_square(c + 1)
                    key_norm(c + 1)
                    evacuate(c + 1, 1 - q, 1, rraw[:, :], [("bon", c + 1), ("rt", c + 1)])
                act.wait_ge(S("mv_mm"), c + 1)
                for h in range(2):
                    act.activation(XK[:, h, :, HD:P],
                                   ROT[MVB][:, :].rearrange("p (b h k) -> p h b k", h=2, k=HD)[:, h],
                                   ACT.Copy, scale=-1.0).then_inc(S("mv"), 1)
                for h in range(2):
                    act.wait_ge(S("tkg_mm"), 2 * c + h + 1)
                    act.activation(NTG[:, h, :, :], blocks(ROT[TKGB[h]][:, :]), ACT.Copy, scale=-1.0)\
                        .then_inc(S("tkg"), 1)
                if not last:
                    evacuate(c + 1, 1 - q, 2, vT[:, :], [("bonus", c + 1), ("turn_mm", 4 * (c + 1))])
                act.wait_ge(S("y_mm"), c + 1)
                need(act, S("yc"), c)
                act.activation(y[:, :], YB[:, :], ACT.Copy).then_inc(S("y"), 1)

            tanhs(0, 0)
            exps(0)
            evacuate(0, 0, 0, kraw[:, :], [])
            key_square(0)
            key_norm(0)
            evacuate(0, 0, 1, rraw[:, :], [])
            evacuate(0, 0, 2, vT[:, :], [])
            run(step)(act)
            center_square(IC - 1)
            group_norm(IC - 1)

        @block.tensor
        def _(pe):
            def gemm(n, q):
                for k, name in enumerate("krv"):
                    for j in range(DC):
                        if j == 0:
                            pe.wait_ge(S("w_" + name), 16 * (n + 1))
                            bank_free(n, 2 + k)
                        m = pe.matmul(G[(q + k) % 2][:, :], ring[name][:, j * P:(j + 1) * P],
                                      lerp[name][:, j, :], start=(j == 0), stop=(j == DC - 1))
                        if j == DC - 1:
                            m.then_inc(S("gemm"), 1)
                        yield

            def bank_free(n, j):
                if j == 0:
                    need(pe, S("evac"), 3 * n - 1)
                elif j == 1:
                    need(pe, S("evac"), 3 * n)
                elif j < 4:
                    need(pe, S("tanh"), 2 * n + j - 1)
                else:
                    need(pe, S("evac"), 3 * n + 1)

            def loras(n, q):
                pe.wait_ge(S("w_lora"), 16 * (n + 1))
                for j in range(2):
                    bank_free(n, j)
                    pe.matmul(G[(q + j) % 2][:, :], lora[rows[j], :], hidden[rows[j], :], start=True, stop=True)\
                        .then_inc(S("gemm"), 1)

            def stat(weights, src, b, sem):
                pe.matmul(ROT[b][:, :], weights, src, start=True, stop=True).then_inc(sem, 1)

            def means(c):
                pe.wait_ge(S("y"), c + 1)
                stat(C["head_mean"], y[:, :], MEANB, S("mean_mm"))

            def variances(c):
                pe.wait_ge(S("ysq"), c + 1)
                stat(C["head_mean"], yv[:, :], VARB, S("var_mm"))

            def key_sums(n):
                pe.wait_ge(S("nsq"), n + 1)
                stat(C["head_sum"], nn[:, :], NNB, S("nn_mm"))

            def bonus_sums(n):
                pe.wait_ge(S("bon"), n + 1)
                stat(C["head_sum"], bon[:, :], BONB, S("bsum_mm"))

            def step(c, p=None):
                q = c % 2 if p is None else p
                last = isinstance(c, int) and c == IC - 1
                first = isinstance(c, int) and c == 0
                more = iter(()) if last else gemm(c + 1, 1 - q)

                def fill(k):
                    for _ in range(k):
                        next(more, None)

                pe.wait_ge(S("be"), c + 1)
                pe.wait_ge(S("kap"), 2 * (c + 1))
                pe.wait_ge(S("evac"), 3 * (c + 1))
                for k, src in enumerate((kap, ke, be, vT)):
                    if k == 0:
                        need(pe, S("phi"), 2 * c)
                    if k == 1:
                        need(pe, S("rh"), c)
                    if k == 2:
                        need(pe, S("st"), 7 * c)
                    if k == 3:
                        need(pe, S("bonus"), c + 1)
                    for b in range(TB):
                        m = pe.transpose(ROT[k][:, b * P:(b + 1) * P], src[:, b * P:(b + 1) * P], C["ident"])
                    m.then_inc(S("turn_mm"), 1)
                for h in range(2):
                    for k in range(4):
                        if h == 0:
                            pe.wait_ge(S("turned"), 5 * c + k + 2)
                        else:
                            pe.wait_ge(S("score"), 8 * c + k + 1)
                        lhs = (bet, kd)[k // 2]
                        for b in range(2):
                            blk = 2 * (k % 2) + b
                            tk = slice(blk * P, (blk + 1) * P)
                            pe.matmul(ROT[k][:, 2 * b * P:(2 * b + 1) * P], lhs[rows[h], tk], kap[rows[h], tk],
                                      start=True, stop=True)
                            m = pe.matmul(ROT[k][:, (2 * b + 1) * P:(2 * b + 2) * P], lhs[rows[h], tk],
                                          rt[rows[h], q, tk], start=True, stop=True)
                        m.then_inc(S("score_mm"), 1)
                if not last:
                    loras(c + 1, 1 - q)
                fill(1)
                if not first:
                    pe.wait_ge(S("score"), 8 * c + 5)
                    means(c - 1)
                fill(1)
                if not first:
                    pe.wait_ge(S("score"), 8 * c + 6)
                    variances(c - 1)
                fill(2)
                for lv in range(5):
                    for h in range(2):
                        if lv == 0 and h == 0 and not first:
                            pe.wait_ge(S("yc"), c)
                        if lv == 0:
                            pe.wait_ge(S("score"), 8 * c + 8)
                        if lv > 0:
                            pe.wait_ge(S("low"), 10 * c + 2 * (lv - 1) + h + 1)
                        if lv == 2 and h == 1 and not last:
                            pe.wait_ge(S("nclamp"), c + 2)
                        pe.wait_ge(S("inv"), INV(c, h, lv))
                        for b in range(TB):
                            m = pe.matmul(ROT[2 * h][:, b * P:(b + 1) * P], LA[:, h, b, 0:P], inv[:, h, b, :],
                                          start=True, stop=True)
                        m.then_inc(S("low_mm"), 1)
                    fill(1)
                    for h in range(2):
                        if lv == 0 and h == 0 and not first:
                            pe.wait_ge(S("yln"), c)
                        pe.wait_ge(S("low"), 10 * c + 2 * lv + h + 1)
                        lhs, rhs = (invT, low) if lv < 4 else (low, invT)
                        for b in range(TB):
                            m = pe.matmul(ROT[2 * h + 1][:, b * P:(b + 1) * P], lhs[:, h, b, :], rhs[:, h, b, :],
                                          start=True, stop=True)
                        m.then_inc(S("up_mm"), 1)
                    fill(2)
                    if lv == 1 and not last:
                        pe.wait_ge(S("low"), 10 * c + 4)
                        key_sums(c + 1)
                pe.wait_ge(S("low"), 10 * c + 9)
                for h in range(2):
                    for b in range(TB):
                        m = pe.matmul(ROT[MVB][:, (2 * b + h) * HD:(2 * b + h + 1) * HD], MK[:, h, b, 0:P],
                                      tok["v"][:, b, rows[h]], start=True, stop=True)
                m.then_inc(S("mv_mm"), 1)
                need(pe, S("y"), c)
                for h in range(2):
                    for b in range(TB):
                        pe.matmul(YB[rows[h], b * P:(b + 1) * P], tok["v"][:, b, rows[h]], MK[:, h, b, P:2 * P],
                                  start=(b == 0), stop=False, skip_group_check=True)
                pe.wait_ge(S("mv"), 2 * c + 2)
                for h in range(2):
                    pe.wait_ge(S("inv"), INV(c, h, 5))
                    if h == 0:
                        pe.wait_ge(S("low"), 10 * c + 10)
                    for b in range(TB):
                        m = pe.matmul(ROT[TKGB[h]][:, b * P:(b + 1) * P], invT[:, h, b, :], XK[:, h, b, :],
                                      start=True, stop=True)
                    m.then_inc(S("tkg_mm"), 1)
                fill(2)
                pe.wait_ge(S("tkg"), 2 * c + 2)
                apart(pe)
                for i in range(1, NCH - 1):
                    r = rows[i % 2]
                    for h in range(2):
                        m = pe.matmul(PH[i % 2][rows[h], (i - 1) * HD:i * HD], NTG[r, h, i // 2, 0:HD],
                                      tok["be"][r, i // 2, rows[h]], start=True, stop=True)
                m.then_inc(S("phi_mm"), 1)
                need(pe, S("st"), 7 * c)
                apart(pe)
                for i in range(NCH - 1):
                    r = rows[i % 2]
                    for h in range(2):
                        pe.matmul(SB[i % 2][rows[h], i * HD:(i + 1) * HD], tok["ke"][r, i // 2, rows[h]],
                                  tok["v"][r, i // 2, rows[h]], start=(i < 2), stop=False, skip_group_check=True)
                        m = pe.matmul(SB[i % 2][rows[h], i * HD:(i + 1) * HD], tok["be"][r, i // 2, rows[h]],
                                      NTG[r, h, i // 2, HD:P], start=False, stop=False, skip_group_check=True)
                m.then_inc(S("st_mm"), 1)
                for h in range(2):
                    for b in range(TB):
                        m = pe.matmul(ROT[RHB][rows[h], b * P:(b + 1) * P], NTG[:, h, b, 0:HD],
                                      LA[:, h, b, P:2 * P], start=True, stop=True)
                m.then_inc(S("rh_mm"), 1)
                for h in range(2):
                    for b in range(TB):
                        pe.matmul(YB[rows[h], b * P:(b + 1) * P], NTG[:, h, b, HD:P], LA[:, h, b, P:2 * P],
                                  start=False, stop=False, skip_group_check=True)
                pe.wait_ge(S("phi"), 2 * (c + 1))
                for i in range(1, NCH):
                    pe.wait_ge(S("st"), 7 * c + i)
                    apart(pe)
                    if i < NCH - 1:
                        for h in range(2):
                            m = pe.matmul(SB[i % 2][rows[h], i * HD:(i + 1) * HD], phi[rows[h], (i - 1) * HD:i * HD],
                                          st[rows[h], i, :], start=False, stop=True, skip_group_check=True)
                        m.then_inc(S("st_mm"), 1)
                    if i == 1:
                        pe.wait_ge(S("rh"), c + 1)
                        apart(pe)
                    for h in range(2):
                        m = pe.matmul(YB[rows[h], i * HD:(i + 1) * HD], st[rows[h], i, :],
                                      rh[rows[h], i * HD:(i + 1) * HD], start=False, stop=True,
                                      skip_group_check=True)
                    fill(1)
                m.then_inc(S("y_mm"), 1)
                fill(24)
                if not last:
                    pe.wait_ge(S("phi"), 2 * (c + 1))
                    bonus_sums(c + 1)

            loras(0, 0)
            for _ in gemm(0, 0):
                pass
            key_sums(0)
            bonus_sums(0)
            run(step)(pe)
            means(IC - 1)
            variances(IC - 1)

        @block.vector
        def _(dve):
            def channels(n, q):
                for name, k in (("kk0", 1), ("tanh", 2), ("bon", 1)):
                    need(dve, S(name), k * (n - 1))
                dve.tensor_copy(chan[:, q, :], mixpar[:, n, 0:6]).then_inc(S("chan"), 1)

            def affines(c):
                need(dve, S("affine"), c)
                dve.tensor_copy(affine[:, :], mixpar[:, c, 6:8]).then_inc(S("aff"), 1)

            def decay(n):
                dve.wait_ge(S("ld"), n + 1)
                need(dve, S("bet"), n)
                dve.tensor_tensor_scan(cum[:, :], C["scan_keep"], ld[:, :], 0.0, ALU.mult, ALU.add)\
                    .then_inc(S("cum"), 1)

            def keys(n):
                dve.wait_ge(S("kfac"), n + 1)
                dve.wait_ge(S("evac"), 3 * n + 1)
                dve.wait_ge(S("kk0"), n + 1)
                dve.tensor_tensor(kp[:, :], kraw[:, :], kp[:, :], ALU.mult).then_inc(S("kp"), 1)
                dve.wait_ge(S("kp"), n + 1)
                dve.wait_ge(S("exp"), 2 * n + 2)
                need(dve, S("score_mm"), 8 * n)
                dve.tensor_tensor(kd[:, :], kp[:, :], cum[:, :], ALU.mult).then_inc(S("kd"), 1)
                dve.wait_ge(S("kd"), n + 1)
                dve.tensor_tensor(chunks(ke[:, :]), chunks(kd[:, :]), ends(e1[:, :]), ALU.mult).then_inc(S("ke"), 1)

            def clamp(n):
                dve.wait_ge(S("nn_mm"), n + 1)
                dve.tensor_scalar(nn[:, :], ROT[NNB][:, :], 1e-24, None, ALU.max).then_inc(S("nclamp"), 1)

            def normed(n):
                dve.wait_ge(S("nrs"), n + 1)
                dve.tensor_tensor(kk[:, :], kk[:, :], nn[:, :], ALU.mult).then_inc(S("kk"), 1)

            def reads(n, p):
                dve.wait_ge(S("evac"), 3 * n + 2)
                dve.tensor_tensor(rt[:, p, :], rraw[:, :], e1[:, :], ALU.mult).then_inc(S("rt"), 1)
                need(dve, S("bsum_mm"), n)
                dve.scalar_tensor_tensor(out=bon[:, :], in0=rraw[:, :], scalar=chan[:, p, 5:6], in1=kp[:, :],
                                         op0=ALU.mult, op1=ALU.mult).then_inc(S("bon"), 1)

            def removals(n):
                dve.wait_ge(S("b"), n + 1)
                dve.tensor_tensor(bet[:, :], tha[:, :], cum[:, :], ALU.mult).then_inc(S("bet"), 1)
                dve.wait_ge(S("bet"), n + 1)
                dve.tensor_tensor(chunks(be[:, :]), chunks(bet[:, :]), ends(e1[:, :]), ALU.mult).then_inc(S("be"), 1)

            def bonuses(n, p):
                dve.wait_ge(S("bsum_mm"), n + 1)
                dve.wait_ge(S("evac"), 3 * n + 3)
                need(dve, S("plus"), n - 1)
                dve.tensor_tensor(bonus[:, p, :], ROT[BONB][:, :], vT[:, :], ALU.mult).then_inc(S("bonus"), 1)

            def center(c):
                dve.wait_ge(S("mean_mm"), c + 1)
                need(dve, S("affine"), c)
                dve.tensor_tensor(yc[:, :], y[:, :], ROT[MEANB][:, :], ALU.subtract).then_inc(S("yc"), 1)

            def scaled(c):
                dve.wait_ge(S("yrs"), c + 1)
                dve.tensor_tensor(yc[:, :], yc[:, :], yv[:, :], ALU.mult).then_inc(S("yn"), 1)

            def gated(c):
                dve.wait_ge(S("plus"), c + 1)
                dve.scalar_tensor_tensor(out=gate[:, c, :], in0=yv[:, :], scalar=0.5, in1=gate[:, c, :],
                                         op0=ALU.mult, op1=ALU.mult).then_inc(S("gated"), 1)

            def step(c, p=None):
                q = c % 2 if p is None else p
                last = isinstance(c, int) and c == IC - 1
                first = isinstance(c, int) and c == 0
                if not last:
                    channels(c + 1, 1 - q)
                if not first:
                    affines(c - 1)
                for h in range(2):
                    for k in range(4):
                        dve.wait_ge(S("score_mm"), 8 * c + 4 * h + k + 1)
                        dst = (LA, MK)[k // 2]
                        b = 2 * (k % 2)
                        dve.tensor_tensor(dst[:, h, b:b + 2, :], pairs(ROT[k][:, :]), over(C["score_mask"], 2),
                                          ALU.mult).then_inc(S("score"), 1)
                    dve.wait_ge(S("score"), 8 * c + 4 * h + 2)
                    dve.tensor_tensor(invT[:, h], LA[:, h, :, 0:P], over(C["level_first"], TB), ALU.mult)\
                        .then_inc(S("inv0"), 1)
                    dve.wait_ge(S("inv0"), 4 * c + 2 * h + 1)
                    dve.tensor_tensor(invT[:, h], invT[:, h], over(C["ident"], TB), ALU.add).then_inc(S("inv0"), 1)
                    dve.wait_ge(S("inv0"), 4 * c + 2 * h + 2)
                    dve.transpose(inv[:, h].rearrange("p b t -> p (b t)"), invT[:, h].rearrange("p b t -> p (b t)"))\
                        .then_inc(S("inv"), 1)
                if not first:
                    center(c - 1)
                for lv in range(5):
                    for h in range(2):
                        dve.wait_ge(S("low_mm"), 10 * c + 2 * lv + h + 1)
                        dve.tensor_tensor(low[:, h], blocks(ROT[2 * h][:, :]),
                                          over(C["level_mask"][:, lv * P:(lv + 1) * P], TB), ALU.mult)\
                            .then_inc(S("low"), 1)
                    if not last:
                        if lv == 0:
                            decay(c + 1)
                        if lv == 4:
                            removals(c + 1)
                    for h in range(2):
                        dve.wait_ge(S("up_mm"), 10 * c + 2 * lv + h + 1)
                        src = blocks(ROT[2 * h + 1][:, :])
                        if lv < 4:
                            dve.tensor_tensor(inv[:, h], inv[:, h], src, ALU.add).then_inc(S("inv_up"), 1)
                            dve.wait_ge(S("inv_up"), 8 * c + 2 * lv + h + 1)
                            dve.transpose(invT[:, h].rearrange("p b t -> p (b t)"),
                                          inv[:, h].rearrange("p b t -> p (b t)")).then_inc(S("inv"), 1)
                        else:
                            dve.tensor_tensor(invT[:, h], invT[:, h], src, ALU.add).then_inc(S("inv"), 1)
                    if lv == 0 and not first:
                        scaled(c - 1)
                    if lv == 1 and not last:
                        clamp(c + 1)
                    if lv == 1 and not last:
                        keys(c + 1)
                    if lv == 2 and not first:
                        gated(c - 1)
                    if lv == 2 and not last:
                        normed(c + 1)
                    if lv == 4 and not last:
                        reads(c + 1, 1 - q)
                dve.wait_ge(S("phi_mm"), c + 1)
                dve.wait_ge(S("dend"), c + 1)
                for i in range(2):
                    half = lambda ap: ap.rearrange("p (n t) -> p n t", t=2 * HD)[:, :, i * HD:(i + 1) * HD]
                    dve.tensor_tensor(half(phi[:, :]), half(PH[1 - i][:, 0:6 * HD]), half(dend[:, q, :]), ALU.add)\
                        .then_inc(S("phi"), 1)
                for i in range(1, NCH):
                    dve.wait_ge(S("st_mm"), 7 * c + i)
                    dve.tensor_copy(st[:, i, :], SB[(i - 1) % 2][:, (i - 1) * HD:i * HD]).then_inc(S("st"), 1)
                    if i == 1:
                        dve.wait_ge(S("rh_mm"), c + 1)
                        dve.tensor_tensor(rh[:, :], ROT[RHB][:, :], rt[:, q, :], ALU.add).then_inc(S("rh"), 1)
                if not last:
                    bonuses(c + 1, 1 - q)

            channels(0, 0)
            decay(0)
            keys(0)
            clamp(0)
            normed(0)
            removals(0)
            reads(0, 0)
            bonuses(0, 0)
            run(step)(dve)
            affines(IC - 1)
            center(IC - 1)
            scaled(IC - 1)
            gated(IC - 1)


def INV(c, h, lv):
    return 12 * c + 2 * lv + h + 1


def project_phase(K, tag, src, kt, weights, norm=None, squares=True, load_x=False, store=False, full=None):
    nc, ins, bank, C, V, sbt, x = (K[n] for n in ("nc", "ins", "bank", "C", "V", "sbt", "x"))
    U = kt // 2
    with ExitStack() as ctx:
        S = Sems(nc, ctx, tag)
        raw = sbt(ctx, tag + "_raw", [P, 2, U * P])
        w_hi, w_lo = (sbt(ctx, tag + n, [P, 4, U * P], F32R) for n in ("_whi", "_wlo"))
        sq = sbt(ctx, tag + "_sq", [P, 2, T])
        rstd = sbt(ctx, tag + "_rstd", [P, T])
        block = ctx.enter_context(nc.Block())

        def loop(eng, job):
            job(0, 0)
            job(1, 1)
            with eng.Fori(1, DC // 2) as i:
                job(2 * i, 0)
                job(2 * i + 1, 1)

        @block.sync
        def _(sp):
            def load(n, q):
                for u in range(2):
                    need(sp, S("wlo"), 2 * (n - 1) + u + 1)
                    sp.dma_start(raw[:, u, :], ins[weights][n, :, u * U * P:(u + 1) * U * P])\
                        .then_inc(S(f"w{u}"), 16)

            loop(sp, load)
            if store:
                for j in range(DC):
                    sp.wait_ge(S("norm_out"), j + 1)
                    sp.dma_start(K["out"][:, j, :], x[:, j, :]).then_inc(S("stored"), 16)
                sp.wait_ge(S("stored"), 16 * DC)

        @block.tensor
        def _(pe):
            def job(n, q):
                need(pe, S("added"), n - 1)
                for u in range(2):
                    pe.wait_ge(S("wlo"), 2 * n + u + 1)
                    if full is not None and isinstance(n, int) and n == 0:
                        for k in range(u * U, (u + 1) * U):
                            pe.wait_ge(S("src_lo"), k + 1)
                            m = products(pe, bank[q][:, :], w_hi[:, 2 * q + u, (k - u * U) * P:],
                                         w_lo[:, 2 * q + u, (k - u * U) * P:], src[0], src[1], [k], k == 0,
                                         k == kt - 1)
                    else:
                        m = products(pe, bank[q][:, :], w_hi[:, 2 * q + u, :], w_lo[:, 2 * q + u, :], src[0],
                                     src[1], range(u * U, (u + 1) * U), u == 0, u == 1)
                    m.then_inc(S("unit"), 1)

            loop(pe, job)
            if norm:
                norm_tensor(pe, S, "norm", C["row_mean"], sq, bank[5][:, :])
            if squares:
                norm_tensor(pe, S, "next", C["row_mean"], sq, bank[NORM_BANK][:, :])

        @block.scalar
        def _(act):
            def split(n, q):
                for u in range(2):
                    act.wait_ge(S(f"w{u}"), 16 * n + 16)
                    need(act, S("unit"), 2 * (n - 2) + u + 1)
                    act.activation(w_hi[:, 2 * q + u, :], raw[:, u, :], ACT.Copy).then_inc(S("whi"), 1)
                    if full is not None and isinstance(n, int) and n == 0:
                        for k in range(u * U, (u + 1) * U):
                            act.activation(src[0][:, k, :], full[:, k, :], ACT.Copy).then_inc(S("src_hi"), 1)

                    if load_x and isinstance(n, int) and n == 0 and u == 0:
                        act.dma_start(x[:, :, :], ins["x"]).then_inc(S("x"), 16)

            loop(act, split)
            if norm:
                norm_squares(act, S, "norm", x, sq, lambda j: act.wait_ge(S("added"), j + 1))
                act.wait_ge(S("norm_sum"), DC)
                norm_factor(act, S, "norm", bank[5][:, :], rstd[:, :], K["eps"][:, 0:1])
            if squares:
                norm_squares(act, S, "next", x, sq, lambda j: act.wait_ge(S("norm_out" if norm else "added"), j + 1))

        @block.vector
        def _(dve):
            def split(n, q):
                for u in range(2):
                    dve.wait_ge(S("whi"), 2 * n + u + 1)
                    split_lo(dve, w_lo[:, 2 * q + u, :], raw[:, u, :], w_hi[:, 2 * q + u, :])\
                        .then_inc(S("wlo"), 1)
                    if full is not None and isinstance(n, int) and n == 0:
                        for k in range(u * U, (u + 1) * U):
                            dve.wait_ge(S("src_hi"), k + 1)
                            split_lo(dve, src[1][:, k, :], full[:, k, :], src[0][:, k, :]).then_inc(S("src_lo"), 1)

            def add(n, q):
                dve.wait_ge(S("unit"), 2 * n + 2)
                dve.tensor_tensor(x[:, n, :], x[:, n, :], bank[q][:, :], ALU.add).then_inc(S("added"), 1)

            split(0, 0)
            split(1, 1)
            if load_x:
                dve.wait_ge(S("x"), 16)
            with dve.Fori(1, DC // 2) as i:
                for q in range(2):
                    add(2 * i - 2 + q, q)
                    split(2 * i + q, q)
            add(DC - 2, 0)
            add(DC - 1, 1)
            if norm:
                norm_vector(dve, S, "norm", x, V[norm], rstd[:, :], x)


def conv_phase(K):
    nc, ins, bank, C, V, sbt, h, y = (K[n] for n in ("nc", "ins", "bank", "C", "V", "sbt", "h", "y"))
    JOBS = 4
    with ExitStack() as ctx:
        S = Sems(nc, ctx, "conv")
        raw = sbt(ctx, "conv_raw", [P, 2, DC * P])
        w_hi, w_lo = (sbt(ctx, "conv" + n, [P, JOBS, DC * P], F32R) for n in ("_whi", "_wlo"))
        full, u, cu, cv, th, gg, rstd = (K["gate"][:, n, :] for n in range(7))
        tmp = K["gate"][:, 7:9, :]
        taps = sbt(ctx, "conv_taps", [P, IC, 3])
        tap = sbt(ctx, "conv_tap", [P, 2, 3])
        block = ctx.enter_context(nc.Block())

        def loop(eng, chunk):
            chunk(0, 0)
            chunk(1, 1)
            with eng.Fori(1, IC // 2 - 1) as i:
                chunk(2 * i, 0)
                chunk(2 * i + 1, 1)
            chunk(IC - 2, 0)
            chunk(IC - 1, 1)

        def last(n):
            return isinstance(n, int) and n == IC - 1

        @block.sync
        def _(sp):
            def load(n, q=None):
                for j in range(JOBS):
                    need(sp, S("wlo"), JOBS * n + j - 1)
                    sp.dma_start(raw[:, j % 2, :], ins["w_conv"][n, j]).then_inc(S(f"w{j % 2}"), 16)

            loop(sp, load)

        @block.tensor
        def _(pe):
            def chunk(n, q):
                if isinstance(n, int) and n == 0:
                    return head_tensor(pe, S, K, bank, w_hi, w_lo)
                for j in range(JOBS):
                    pe.wait_ge(S("wlo"), JOBS * n + j + 1)
                    need(pe, S(("u", "cu", "gg", "full")[j]), n - 1)
                    products(pe, bank[4 * q + j][:, :], w_hi[:, j, :], w_lo[:, j, :], h[0], h[1], range(DC))\
                        .then_inc(S("mm"), 1)

            loop(pe, chunk)

        @block.scalar
        def _(act):
            def split(n, j):
                act.wait_ge(S(f"w{j % 2}"), 32 * n + 16 * (j // 2) + 16)
                need(act, S("mm"), JOBS * (n - 1) + j + 1)
                act.activation(w_hi[:, j, :], raw[:, j % 2, :], ACT.Copy).then_inc(S("whi"), 1)

            def keep(n):
                act.wait_ge(S("full"), n + 1)
                act.activation(y[0][:, n, :], full[:, :], ACT.Copy).then_inc(S("y_hi"), 1)

            head_scalar(act, S, K, rstd, tmp, lambda j: split(0, j))

            def chunk(n, q):
                act.wait_ge(S("mm"), JOBS * n + 1)
                need(act, S("cu"), n)
                act.activation(u[:, :], bank[4 * q][:, :], ACT.Copy).then_inc(S("u"), 1)
                if not (isinstance(n, int) and n == 0):
                    keep(n - 1)
                if not last(n):
                    split(n + 1, 0)
                act.wait_ge(S("cu"), n + 1)
                act.wait_ge(S("tap"), n + 1)
                need(act, S("full"), n)
                act.activation(cv[:, :], cu[:, :], ACT.Copy, scale=tap[:, q, 2:3]).then_inc(S("tap2"), 1)
                if not last(n):
                    split(n + 1, 1)
                act.wait_ge(S("mm"), JOBS * n + 3)
                need(act, S("gg"), n)
                act.activation(th[:, :], bank[4 * q + 2][:, :], ACT.Tanh, scale=0.5).then_inc(S("th"), 1)
                if not last(n):
                    split(n + 1, 2)
                    split(n + 1, 3)

            loop(act, chunk)
            keep(IC - 1)

        @block.vector
        def _(dve):
            for j in range(3):
                dve.tensor_copy(taps[:, :, j], V["b_conv"][:, j * IC:(j + 1) * IC]).then_inc(S("taps"), 1)
            dve.wait_ge(S("taps"), 3)

            def split(n, j):
                dve.wait_ge(S("whi"), JOBS * n + j + 1)
                split_lo(dve, w_lo[:, j, :], raw[:, j % 2, :], w_hi[:, j, :]).then_inc(S("wlo"), 1)

            def keep(n):
                dve.wait_ge(S("y_hi"), n + 1)
                split_lo(dve, y[1][:, n, :], full[:, :], y[0][:, n, :]).then_inc(S("y_lo"), 1)

            head_vector(dve, S, K, "b_norm", rstd, tmp, lambda j: split(0, j))

            def chunk(n, q):
                need(dve, S("tap2"), n - 1)
                need(dve, S("taps1"), n - 1)
                dve.tensor_copy(tap[:, q, :], taps[:, n, :]).then_inc(S("tap"), 1)
                dve.wait_ge(S("u"), n + 1)
                dve.wait_ge(S("mm"), JOBS * n + 2)
                need(dve, S("taps1"), n)
                dve.tensor_tensor(cu[:, :], bank[4 * q + 1][:, :], u[:, :], ALU.mult).then_inc(S("cu"), 1)
                if not (isinstance(n, int) and n == 0):
                    keep(n - 1)
                if not last(n):
                    split(n + 1, 0)
                dve.wait_ge(S("tap2"), n + 1)
                dve.wait_ge(S("tap"), n + 1)
                dve.scalar_tensor_tensor(out=cv[:, 1:T], in0=cu[:, 0:T - 1], scalar=tap[:, q, 1:2], in1=cv[:, 1:T],
                                         op0=ALU.mult, op1=ALU.add).then_inc(S("taps2"), 1)
                dve.wait_ge(S("taps2"), n + 1)
                dve.scalar_tensor_tensor(out=cv[:, 2:T], in0=cu[:, 0:T - 2], scalar=tap[:, q, 0:1], in1=cv[:, 2:T],
                                         op0=ALU.mult, op1=ALU.add).then_inc(S("taps1"), 1)
                if not last(n):
                    split(n + 1, 1)
                dve.wait_ge(S("th"), n + 1)
                need(dve, S("cg"), n)
                dve.scalar_tensor_tensor(out=gg[:, :], in0=th[:, :], scalar=1.0, in1=bank[4 * q + 2][:, :],
                                         op0=ALU.add, op1=ALU.mult).then_inc(S("gg"), 1)
                dve.wait_ge(S("taps1"), n + 1)
                dve.wait_ge(S("gg"), n + 1)
                dve.scalar_tensor_tensor(out=cv[:, :], in0=cv[:, :], scalar=0.5, in1=gg[:, :],
                                         op0=ALU.mult, op1=ALU.mult).then_inc(S("cg"), 1)
                if not last(n):
                    split(n + 1, 2)
                dve.wait_ge(S("mm"), JOBS * n + 4)
                dve.wait_ge(S("cg"), n + 1)
                need(dve, S("y_lo"), n)
                dve.tensor_tensor(full[:, :], cv[:, :], bank[4 * q + 3][:, :], ALU.mult).then_inc(S("full"), 1)
                if not last(n):
                    split(n + 1, 3)

            loop(dve, chunk)
            keep(IC - 1)


def input_phase(K):
    nc, ins, bank, sbt, h, proj, vals = (K[n] for n in ("nc", "ins", "bank", "sbt", "h", "proj", "vals"))
    RING, NCHN, NTOK = 4, 16, 4
    LAST = (NCHN + NTOK) // RING
    with ExitStack() as ctx:
        S = Sems(nc, ctx, "in2")
        raw = sbt(ctx, "in2_raw", [P, RING, DC * P])
        w_hi, w_lo = (sbt(ctx, "in2" + n, [P, RING, DC * P], F32R) for n in ("_whi", "_wlo"))
        rstd, tmp = sbt(ctx, "in2_rstd", [P, T]), sbt(ctx, "in2_tmp", [P, 2, T])
        block = ctx.enter_context(nc.Block())

        def loop(eng, job, last):
            for s in range(RING):
                job(0, s)
            with eng.Fori(1, last) as i:
                for s in range(RING):
                    job(i, s)

        @block.sync
        def _(sp):
            def load(i, s):
                need(sp, S("wlo"), RING * (i - 1) + s + 1)
                sp.dma_start(raw[:, s, :], ins["w_in2"][RING * i + s]).then_inc(S(f"w{s}"), 16)

            loop(sp, load, LAST)

        @block.tensor
        def _(pe):
            def job(i, s):
                pe.wait_ge(S("wlo"), RING * i + s + 1)
                need(pe, S("copied"), RING * (i - 1) + s + 1)
                products(pe, bank[s][:, :], w_hi[:, s, :], w_lo[:, s, :], h[0], h[1], range(DC))\
                    .then_inc(S("mm"), 1)

            head_tensor(pe, S, K, bank, w_hi, w_lo)
            with pe.Fori(1, NCHN // RING) as i:
                for s in range(RING):
                    job(i, s)
            for s in range(NTOK):
                pe.wait_ge(S("wlo"), NCHN + s + 1)
                pe.wait_ge(S("copied"), NCHN - RING + s + 1)
                for b in range(TB):
                    tk = slice(b * P, (b + 1) * P)
                    for k in range(DC):
                        w = slice(k * P, (k + 1) * P)
                        pe.matmul(bank[s][:, tk], h[0][:, k, tk], w_hi[:, s, w], start=(k == 0), stop=False)
                        pe.matmul(bank[s][:, tk], h[0][:, k, tk], w_lo[:, s, w], start=False, stop=False)
                        m = pe.matmul(bank[s][:, tk], h[1][:, k, tk], w_hi[:, s, w], start=False,
                                      stop=(k == DC - 1))
                m.then_inc(S("mm"), 1)

        @block.vector
        def _(dve):
            def split(i, s):
                dve.wait_ge(S("whi"), RING * i + s + 1)
                split_lo(dve, w_lo[:, s, :], raw[:, s, :], w_hi[:, s, :]).then_inc(S("wlo"), 1)

            head_vector(dve, S, K, "norm1_g_2", rstd[:, :], tmp, lambda j: split(0, j))
            with dve.Fori(1, LAST) as i:
                for s in range(RING):
                    split(i, s)

        @block.scalar
        def _(act):
            def split(i, s):
                act.wait_ge(S(f"w{s}"), 16 * i + 16)
                need(act, S("mm"), RING * (i - 1) + s + 1)
                act.activation(w_hi[:, s, :], raw[:, s, :], ACT.Copy).then_inc(S("whi"), 1)

            head_scalar(act, S, K, rstd[:, :], tmp, lambda j: split(0, j))

            def job(i, s):
                act.wait_ge(S("mm"), RING * i + s + 1)
                split(i + 1, s)
                act.activation(proj[:, RING * i + s, :], bank[s][:, :], ACT.Copy).then_inc(S("copied"), 1)

            loop(act, job, NCHN // RING)
            for s in range(NTOK):
                act.wait_ge(S("mm"), NCHN + s + 1)
                act.activation(vals[:, :, s * P:(s + 1) * P], bank[s][:, :].rearrange("p (b t) -> p b t", t=P),
                               ACT.Copy).then_inc(S("copied"), 1)


def mixer_phase(K):
    nc, ins, bank, C, V, sbt, proj, vals, mixed = (K[n] for n in ("nc", "ins", "bank", "C", "V", "sbt", "proj",
                                                                  "vals", "mixed"))
    SB_SCALE, DF_SCALE = 64 ** -0.5, 32 ** -0.5
    LAM_INIT = 0.8 - 0.6 * float(np.exp(0.0))
    SLOPE = [2.0 ** (-8.0 * (n + 1) / 4) for n in range(4)]
    GELU = float(np.sqrt(2.0 / np.pi))
    with ExitStack() as ctx:
        S = Sems(nc, ctx, "mixer")
        t_ = lambda name, shape: sbt(ctx, name, shape)
        wbd = t_("wbd", [P, 2, 4, P])
        lp = t_("lp", [P, 16, 4])
        m4 = lp[:, 7, :]
        xc, rr, ii, la, aa, g1, g2, gl = (t_("lru_" + n, [P, T]) for n in ("xc", "rr", "ii", "la", "aa", "g1", "g2", "gl"))
        za, sp_, ex = (t_("sb_" + n, [P, TB, T]) for n in ("za", "sp", "ex"))
        dist = t_("dist", [P, DIST[-1]])
        bias = t_("bias", [P, DIST[-1]])
        pr = [t_(f"pr{m}", [P, DIST[-1]]) for m in range(2)]
        pT = t_("pT", [P, TB, T])
        ds_ = t_("ds", [P, 5, 2, TB])
        lam = t_("lam", [P, 4, 32])
        lamp = t_("lamp", [P, 2, 32])
        lams = t_("lams", [P, 8])
        gsub = t_("gsub", [P, 1])
        do, dsq = t_("do", [P, T]), t_("dsq", [P, T])
        one = t_("one", [P, 1])
        rows = (slice(0, HD), slice(HD, P))
        block = ctx.enter_context(nc.Block())
        N = lambda i: T - i * P

        @block.sync
        def _(sp):
            sp.wait_ge(S("wbd0"), 1)
            for r in range(2):
                for g in range(2):
                    sp.dma_start(wbd[rows[r], g, :, rows[r]], ins["w_lru"][rows[r], g]).then_inc(S("wbd"), 16)
            sp.dma_start(dist[:, :], ins["distance"]).then_inc(S("dist"), 16)
            sp.dma_start(lam[:, :, :], ins["lam"].rearrange("(o a) b -> o a b", o=1).broadcast_to([P, 4, 32]))\
                .then_inc(S("lam"), 16)

        @block.gpsimd
        def _(pool):
            pool.memset(wbd[:, :, :, :], 0.0).then_inc(S("wbd0"), 1)
            pool.memset(one[:, :], 1.0).then_inc(S("one"), 1)

            def gates(n):
                pool.wait_ge(S("lru_th"), n + 1)
                pool.tensor_scalar(g1[:, :], g1[:, :], -2.0, 1e-18, ALU.mult, ALU.max).then_inc(S("lru_tm"), 1)

            def gelu(n):
                pool.wait_ge(S("ysq"), n + 1)
                pool.tensor_scalar(gl[:, :], gl[:, :], 0.044715, 1.0, ALU.mult, ALU.add).then_inc(S("ycube"), 1)
                pool.wait_ge(S("ycube"), n + 1)
                pool.tensor_tensor(gl[:, :], gl[:, :], proj[:, 4 + n, :], ALU.mult).then_inc(S("yin"), 1)

            def distance(n):
                need(pool, S("dscore"), 8 * n)
                pool.tensor_scalar(bias[:, :], dist[:, :], -SLOPE[n], None, ALU.mult).then_inc(S("bias"), 1)

            gelu(0)
            pool.wait_ge(S("dist"), 16)
            distance(0)
            gates(0)
            for n in range(4):
                for i in range(TB):
                    pool.wait_ge(S("relu"), 4 * n + i + 1)
                    pool.wait_ge(S("sb_ln"), 4 * n + i + 1)
                    pool.tensor_tensor(sp_[:, i, 0:N(i)], sp_[:, i, 0:N(i)], za[:, i, 0:N(i)], ALU.add)\
                        .then_inc(S("sp"), 1)
                if n < 3:
                    distance(n + 1)
                    gelu(n + 1)
                    gates(n + 1)

        @block.tensor
        def _(pe):
            pe.wait_ge(S("wbd"), 64)

            def gates(n):
                pe.wait_ge(S("conv"), 3 * n + 3)
                need(pe, S("pT"), 4 * n)
                for g in range(2):
                    pe.matmul(bank[g][:, :], wbd[:, g, n, :], xc[:, :], start=True, stop=True).then_inc(S("rg_mm"), 1)

            gates(0)
            for n in range(4):
                hp = rows[n % 2]
                need(pe, S("sum"), 4 * n)
                for i in range(TB):
                    pe.matmul(bank[2 + i][:, 0:N(i)], proj[hp, 10 + n // 2, i * P:(i + 1) * P],
                              proj[hp, 8 + n // 2, i * P:T], start=True, stop=True).then_inc(S("z_mm"), 1)
                for b in range(TB):
                    for m_ in range(2):
                        k = 2 * b + m_
                        if b == 0:
                            pe.wait_ge(S("gate"), 2 * n + m_ + 1)
                        else:
                            pe.wait_ge(S("dscore"), 8 * n + k - 1)
                        r = slice(hp.start + 32 * m_, hp.start + 32 * m_ + 32)
                        pe.matmul(bank[m_][:, 0:(b + 1) * P], proj[r, 12 + n // 2, b * P:(b + 1) * P],
                                  proj[r, 14 + n // 2, 0:(b + 1) * P], start=True, stop=True)\
                            .then_inc(S("d_mm"), 1)
                pe.wait_ge(S("spm"), 4 * (n + 1))
                for i in range(TB - 1, -1, -1):
                    m = pe.matmul(bank[2 + i][:, 0:N(i)], C["minus_after"], sp_[:, i, 0:N(i)], start=True,
                                  stop=(i == TB - 1), skip_group_check=True)
                    for j in range(i + 1, TB):
                        m = pe.matmul(bank[2 + i][:, (j - i) * P:N(i)], C["minus_all"], sp_[:, j, 0:N(j)],
                                      start=False, stop=(j == TB - 1), skip_group_check=True)
                    m.then_inc(S("tail_mm"), 1)
                pe.wait_ge(S("dscore"), 8 * n + 8)
                for b in range(TB):
                    pe.wait_ge(S("dp"), 4 * n + b + 1)
                    if b >= 2:
                        pe.wait_ge(S("pT"), 4 * n + b - 1)
                    for j in range(b + 1):
                        m = pe.transpose(bank[b % 2][:, j * P:(j + 1) * P],
                                         pr[0][:, DIST[b] + j * P:DIST[b] + (j + 1) * P], C["ident"])
                    m.then_inc(S("pT_mm"), 1)
                need(pe, S("sb_out"), n // 2)
                pe.wait_ge(S("wm"), 4 * n + 4)
                for i in range(TB):
                    m = pe.matmul(bank[6][hp, i * P:T], vals[:, i, n * HD:(n + 1) * HD], ex[:, i, 0:N(i)],
                                  start=(i == 0), stop=(i == TB - 1), skip_group_check=True)
                m.then_inc(S("sb_mm"), 1)
                pe.wait_ge(S("pT"), 4 * n + 4)
                need(pe, S("dln"), n // 2)
                for j in range(TB):
                    m = pe.matmul(bank[7][hp, j * P:T], vals[:, j, 256 + n * HD:256 + (n + 1) * HD], pT[:, j, j * P:T],
                                  start=(j == 0), stop=(j == TB - 1), skip_group_check=True)
                m.then_inc(S("do_mm"), 1)
                if n % 2:
                    pe.wait_ge(S("dsq"), n // 2 + 1)
                    pe.matmul(bank[7][:, :], C["head_mean"], dsq[:, :], start=True, stop=True).then_inc(S("dv_mm"), 1)
                if n < 3:
                    gates(n + 1)

        @block.scalar
        def _(act):
            act.wait_ge(S("one"), 1)
            act.activation(lp[:, 0, :], V["lru_lambda_2"], ACT.Abs).then_inc(S("sp_abs"), 1)
            act.wait_ge(S("sp_abs"), 1)
            act.activation(lp[:, 1, :], lp[:, 0, :], ACT.Exp, scale=-1.0).then_inc(S("sp_e"), 1)
            act.wait_ge(S("sp_u"), 1)
            act.activation(lp[:, 3, :], lp[:, 2, :], ACT.Ln).then_inc(S("sp_ln"), 1)
            act.wait_ge(S("lam_sum"), 2)
            act.activation(lams[:, 2:4], lams[:, 0:2], ACT.Exp).then_inc(S("lam_e"), 1)
            act.wait_ge(S("chp"), 1)

            def conv_start(n):
                need(act, S("ix"), n)
                act.activation(xc[:, :], proj[:, n, :], ACT.Identity, bias=V["conv_a_b_2"][:, n:n + 1],
                               scale=V["conv_a_w_2"][:, 12 + n:13 + n]).then_inc(S("xc0"), 1)

            def gates(n):
                need(act, S("lru_out"), n)
                act.activation(gl[:, :], proj[:, 4 + n, :], ACT.Square).then_inc(S("ysq"), 1)
                for g, dst in enumerate((rr, ii)):
                    act.wait_ge(S("rg_mm"), 2 * n + g + 1)
                    act.activation(dst[:, :], bank[g][:, :], ACT.Tanh, bias=lp[:, 8 + g, n:n + 1], scale=0.5)\
                        .then_inc(S("gate"), 1)
                act.wait_ge(S("yin"), n + 1)
                act.activation(gl[:, :], gl[:, :], ACT.Tanh, scale=GELU).then_inc(S("yth"), 1)
                act.wait_ge(S("la"), n + 1)
                act.activation(g1[:, :], la[:, :], ACT.Tanh).then_inc(S("lru_th"), 1)
                act.activation(aa[:, :], la[:, :], ACT.Exp).then_inc(S("lru_a"), 1)

            conv_start(0)
            gates(0)
            for n in range(4):
                need(act, S("sp"), 4 * n)
                for i in range(TB):
                    act.wait_ge(S("z_mm"), 4 * n + i + 1)
                    act.activation(za[:, i, 0:N(i)], bank[2 + i][:, 0:N(i)], ACT.Abs, scale=SB_SCALE)\
                        .then_inc(S("zabs"), 1)
                for i in range(TB):
                    act.wait_ge(S("zabs"), 4 * n + i + 1)
                    act.activation(za[:, i, 0:N(i)], za[:, i, 0:N(i)], ACT.Exp, scale=-1.0).then_inc(S("sb_e"), 1)
                for i in range(TB):
                    act.wait_ge(S("sb_e"), 4 * n + i + 1)
                    act.activation(za[:, i, 0:N(i)], za[:, i, 0:N(i)], ACT.Ln, bias=one[:, 0:1]).then_inc(S("sb_ln"), 1)
                act.wait_ge(S("one_minus"), n + 1)
                act.activation(g2[:, :], g2[:, :], ACT.Ln).then_inc(S("ln2"), 1)
                act.wait_ge(S("lru_tm"), n + 1)
                act.activation(g1[:, :], g1[:, :], ACT.Ln).then_inc(S("ln1"), 1)
                for b in range(TB):
                    for m_ in range(2):
                        act.wait_ge(S("dmax"), 8 * n + 2 * b + m_ + 1)
                        act.activation(pr[m_][:, DIST[b]:DIST[b + 1]], pr[m_][:, DIST[b]:DIST[b + 1]], ACT.Exp,
                                       bias=ds_[:, 0, m_, b:b + 1], accum_out=ds_[:, 1, m_, b:b + 1])\
                            .then_inc(S("dexp"), 1)
                act.wait_ge(S("lndiff"), n + 1)
                act.activation(g1[:, :], g1[:, :], ACT.Exp, scale=0.5).then_inc(S("gam"), 1)
                for i in range(TB - 1, -1, -1):
                    act.wait_ge(S("sum"), 4 * n + TB - i)
                    act.activation(ex[:, i, 0:N(i)], ex[:, i, 0:N(i)], ACT.Exp).then_inc(S("w"), 1)
                if n < 3:
                    conv_start(n + 1)
                for b in range(TB):
                    act.wait_ge(S("pT_mm"), 4 * n + b + 1)
                    act.activation(pT[:, 0:b + 1, b * P:(b + 1) * P],
                                   bank[b % 2][:, 0:(b + 1) * P].rearrange("p (j t) -> p j t", t=P), ACT.Copy)\
                        .then_inc(S("pT"), 1)
                if n % 2:
                    act.wait_ge(S("sb_mm"), n + 1)
                    act.activation(mixed[:, 4 + n // 2, :], bank[6][:, :], ACT.Copy).then_inc(S("sb_out"), 1)
                    act.wait_ge(S("do_mm"), n + 1)
                    need(act, S("dout"), n // 2)
                    act.activation(do[:, :], bank[7][:, :], ACT.Copy).then_inc(S("do"), 1)
                    act.activation(dsq[:, :], bank[7][:, :], ACT.Square).then_inc(S("dsq"), 1)
                    act.wait_ge(S("dv_mm"), n // 2 + 1)
                    act.activation(dsq[:, :], bank[7][:, :], ACT.Ln, bias=K["eps"][:, 0:1]).then_inc(S("dln"), 1)
                    act.wait_ge(S("dln"), n // 2 + 1)
                    act.activation(dsq[:, :], dsq[:, :], ACT.Exp, scale=-0.5).then_inc(S("drs"), 1)
                if n < 3:
                    gates(n + 1)

        @block.vector
        def _(dve):
            lamb = V["lru_lambda_2"]
            seq = [0]

            def then(ins_):
                seq[0] += 1
                ins_.then_inc(S("small"), 1)
                dve.wait_ge(S("small"), seq[0])

            then(dve.tensor_scalar(lp[:, 8, :], V["b_rgate_2"], 0.5, None, ALU.mult))
            then(dve.tensor_scalar(lp[:, 9, :], V["b_igate_2"], 0.5, None, ALU.mult))
            then(dve.tensor_scalar(gsub[:, :], V["subln_g_2"], 1.0 - LAM_INIT, None, ALU.mult))
            dve.wait_ge(S("sp_e"), 1)
            dve.tensor_scalar(lp[:, 2, :], lp[:, 1, :], 1.0, None, ALU.add).then_inc(S("sp_u"), 1)
            dve.wait_ge(S("sp_u"), 1)
            then(dve.tensor_scalar(lp[:, 4, :], lp[:, 2, :], -1.0, None, ALU.add))
            then(dve.tensor_scalar(lp[:, 5, :], lp[:, 4, :], 0.0, None, ALU.is_equal))
            then(dve.tensor_tensor(lp[:, 4, :], lp[:, 4, :], lp[:, 5, :], ALU.add))
            then(dve.reciprocal(lp[:, 4, :], lp[:, 4, :]))
            dve.wait_ge(S("sp_ln"), 1)
            then(dve.tensor_tensor(lp[:, 4, :], lp[:, 4, :], lp[:, 3, :], ALU.mult))
            then(dve.tensor_tensor(lp[:, 4, :], lp[:, 4, :], lp[:, 5, :], ALU.add))
            then(dve.tensor_tensor(lp[:, 4, :], lp[:, 4, :], lp[:, 1, :], ALU.mult))
            then(dve.tensor_scalar(lp[:, 6, :], lamb, -1.0, 0.0, ALU.mult, ALU.max))
            then(dve.tensor_tensor(lp[:, 4, :], lp[:, 4, :], lp[:, 6, :], ALU.add))
            dve.tensor_scalar(m4, lp[:, 4, :], -4.0, None, ALU.mult).then_inc(S("chp"), 1)
            dve.wait_ge(S("chp"), 1)
            dve.wait_ge(S("lam"), 16)
            for k in range(2):
                then(dve.tensor_tensor(lamp[:, k, :], lam[:, 2 * k, :], lam[:, 2 * k + 1, :], ALU.mult))
                dve.tensor_reduce(lams[:, k:k + 1], lamp[:, k, :], AX_X, ALU.add).then_inc(S("lam_sum"), 1)
            dve.wait_ge(S("lam_e"), 1)
            then(dve.tensor_tensor(lams[:, 4:5], lams[:, 3:4], lams[:, 2:3], ALU.subtract))
            then(dve.tensor_scalar(lams[:, 5:6], lams[:, 4:5], -LAM_INIT, None, ALU.add))

            def conv(n):
                for k in range(3):
                    if k == 0:
                        dve.wait_ge(S("xc0"), n + 1)
                    else:
                        dve.wait_ge(S("conv"), 3 * n + k)
                    dve.scalar_tensor_tensor(out=xc[:, k + 1:T], in0=proj[:, n, 0:T - k - 1],
                                             scalar=V["conv_a_w_2"][:, 4 * (2 - k) + n:4 * (2 - k) + n + 1],
                                             in1=xc[:, k + 1:T], op0=ALU.mult, op1=ALU.add).then_inc(S("conv"), 1)

            def gates(n):
                dve.wait_ge(S("gate"), 2 * n + 1)
                need(dve, S("lru_a"), n)
                dve.tensor_scalar(la[:, :], rr[:, :], m4[:, n:n + 1], m4[:, n:n + 1], ALU.mult, ALU.add)\
                    .then_inc(S("la"), 1)
                dve.wait_ge(S("gate"), 2 * n + 2)
                dve.wait_ge(S("conv"), 3 * n + 3)
                dve.scalar_tensor_tensor(out=ii[:, :], in0=ii[:, :], scalar=1.0, in1=xc[:, :], op0=ALU.add,
                                         op1=ALU.mult).then_inc(S("ix"), 1)

            def scores(n, b):
                for m_ in range(2):
                    k = 8 * n + 2 * b + m_ + 1
                    part = pr[m_][:, DIST[b]:DIST[b + 1]]
                    dve.wait_ge(S("d_mm"), k)
                    dve.scalar_tensor_tensor(out=part, in0=bank[m_][:, 0:(b + 1) * P], scalar=DF_SCALE,
                                             in1=bias[:, DIST[b]:DIST[b + 1]], op0=ALU.mult, op1=ALU.add)\
                        .then_inc(S("dscore"), 1)
                for m_ in range(2):
                    k = 8 * n + 2 * b + m_ + 1
                    dve.wait_ge(S("dscore"), k)
                    dve.tensor_reduce(ds_[:, 2, m_, b:b + 1], pr[m_][:, DIST[b]:DIST[b + 1]], AX_X, ALU.max)\
                        .then_inc(S("dm"), 1)
                for m_ in range(2):
                    k = 8 * n + 2 * b + m_ + 1
                    dve.wait_ge(S("dm"), k)
                    dve.tensor_scalar(ds_[:, 0, m_, b:b + 1], ds_[:, 2, m_, b:b + 1], -1.0, None, ALU.mult)\
                        .then_inc(S("dmax"), 1)

            conv(0)
            gates(0)
            for n in range(4):
                for i in range(TB):
                    dve.wait_ge(S("zabs"), 4 * n + i + 1)
                    dve.tensor_scalar(sp_[:, i, 0:N(i)], bank[2 + i][:, 0:N(i)], SB_SCALE, 0.0, ALU.mult,
                                      ALU.max).then_inc(S("relu"), 1)
                need(dve, S("ln2"), n)
                dve.wait_ge(S("lru_tm"), n + 1)
                dve.tensor_scalar(g2[:, :], g1[:, :], 0.5, 1.0, ALU.mult, ALU.add).then_inc(S("one_minus"), 1)
                dve.wait_ge(S("bias"), n + 1)
                scores(n, 0)
                scores(n, 1)
                scores(n, 2)
                for i in range(TB):
                    dve.wait_ge(S("sp"), 4 * n + i + 1)
                    dve.scalar_tensor_tensor(out=ex[:, i, 0:N(i)], in0=bank[2 + i][:, 0:N(i)], scalar=SB_SCALE,
                                             in1=sp_[:, i, 0:N(i)], op0=ALU.mult, op1=ALU.subtract)\
                        .then_inc(S("logw"), 1)
                    dve.wait_ge(S("logw"), 4 * n + i + 1)
                    dve.tensor_tensor(sp_[:, i, 0:P], sp_[:, i, 0:P], C["before"], ALU.mult).then_inc(S("spm"), 1)
                scores(n, 3)
                dve.wait_ge(S("ln1"), n + 1)
                dve.wait_ge(S("ln2"), n + 1)
                dve.tensor_tensor(g1[:, :], g1[:, :], g2[:, :], ALU.subtract).then_inc(S("lndiff"), 1)
                dve.wait_ge(S("logw"), 4 * n + 4)
                for i in range(TB - 1, -1, -1):
                    dve.wait_ge(S("tail_mm"), 4 * n + TB - i)
                    dve.tensor_tensor(ex[:, i, 0:N(i)], ex[:, i, 0:N(i)], bank[2 + i][:, 0:N(i)], ALU.add)\
                        .then_inc(S("sum"), 1)
                for b in range(TB):
                    k = 8 * n + 2 * b
                    dve.wait_ge(S("dexp"), k + 2)
                    dve.reciprocal(ds_[:, 3, :, b:b + 1], ds_[:, 1, :, b:b + 1]).then_inc(S("drec"), 1)
                    dve.wait_ge(S("drec"), 4 * n + b + 1)
                    dve.tensor_scalar(ds_[:, 4, 1, b:b + 1], ds_[:, 3, 1, b:b + 1], lams[:, 5:6], None, ALU.mult)\
                        .then_inc(S("dlam"), 1)
                    dve.tensor_scalar(pr[0][:, DIST[b]:DIST[b + 1]], pr[0][:, DIST[b]:DIST[b + 1]],
                                      ds_[:, 3, 0, b:b + 1], None, ALU.mult).then_inc(S("dp0"), 1)
                    dve.wait_ge(S("dp0"), 4 * n + b + 1)
                    dve.wait_ge(S("dlam"), 4 * n + b + 1)
                    dve.scalar_tensor_tensor(out=pr[0][:, DIST[b]:DIST[b + 1]], in0=pr[1][:, DIST[b]:DIST[b + 1]],
                                             scalar=ds_[:, 4, 1, b:b + 1], in1=pr[0][:, DIST[b]:DIST[b + 1]],
                                             op0=ALU.mult, op1=ALU.add).then_inc(S("dp"), 1)
                for i in range(TB - 1, -1, -1):
                    dve.wait_ge(S("w"), 4 * n + TB - i)
                    dve.tensor_tensor(ex[:, i, 0:P], ex[:, i, 0:P], C["before"], ALU.mult).then_inc(S("wm"), 1)
                dve.wait_ge(S("gam"), n + 1)
                dve.wait_ge(S("ix"), n + 1)
                dve.scalar_tensor_tensor(out=ii[:, :], in0=ii[:, :], scalar=0.5, in1=g1[:, :], op0=ALU.mult,
                                         op1=ALU.mult).then_inc(S("u"), 1)
                dve.wait_ge(S("yth"), n + 1)
                dve.scalar_tensor_tensor(out=gl[:, :], in0=gl[:, :], scalar=1.0, in1=proj[:, 4 + n, :], op0=ALU.add,
                                         op1=ALU.mult).then_inc(S("gelu"), 1)
                dve.wait_ge(S("u"), n + 1)
                dve.wait_ge(S("lru_a"), n + 1)
                dve.tensor_tensor_scan(rr[:, :], aa[:, :], ii[:, :], 0.0, ALU.mult, ALU.add).then_inc(S("hl"), 1)
                dve.wait_ge(S("gelu"), n + 1)
                dve.wait_ge(S("hl"), n + 1)
                dve.scalar_tensor_tensor(out=mixed[:, n, :], in0=rr[:, :], scalar=0.5, in1=gl[:, :], op0=ALU.mult,
                                         op1=ALU.mult).then_inc(S("lru_out"), 1)
                if n < 3:
                    conv(n + 1)
                if n % 2:
                    dve.wait_ge(S("drs"), n // 2 + 1)
                    dve.scalar_tensor_tensor(out=mixed[:, 6 + n // 2, :], in0=do[:, :], scalar=gsub[:, 0:1],
                                             in1=dsq[:, :], op0=ALU.mult, op1=ALU.mult).then_inc(S("dout"), 1)
                if n < 3:
                    gates(n + 1)


def up_phase(K):
    nc, ins, bank, V, sbt, h, ff = (K[n] for n in ("nc", "ins", "bank", "V", "sbt", "h", "ff"))
    JOBS = 4
    with ExitStack() as ctx:
        S = Sems(nc, ctx, "up")
        raw = sbt(ctx, "up_raw", [P, 2, DC * P])
        w_hi, w_lo = (sbt(ctx, "up" + n, [P, JOBS, DC * P], F32R) for n in ("_whi", "_wlo"))
        z = sbt(ctx, "up_z", [P, 2, T])
        u = sbt(ctx, "up_u", [P, 2, T])
        th, full, rstd = (sbt(ctx, "up_" + n, [P, T]) for n in ("th", "full", "rstd"))
        cols = sbt(ctx, "up_cols", [P, FC, 8])
        col = sbt(ctx, "up_col", [P, 2, 8])
        block = ctx.enter_context(nc.Block())

        def loop(eng, chunk):
            chunk(0, 0)
            chunk(1, 1)
            with eng.Fori(1, FC // 2 - 1) as i:
                chunk(2 * i, 0)
                chunk(2 * i + 1, 1)
            chunk(FC - 2, 0)
            chunk(FC - 1, 1)

        def splits(n):
            return not (isinstance(n, int) and n >= FC - 2)

        @block.sync
        def _(sp):
            def load(n, q):
                for g in range(2):
                    need(sp, S("wlo"), 2 * (n - 1) + g + 1)
                    sp.dma_start(raw[:, g, :], ins["w_up"][n, g]).then_inc(S(f"w{g}"), 16)

            loop(sp, load)

        @block.tensor
        def _(pe):
            def chunk(n, q):
                if isinstance(n, int) and n < 2:
                    return n or head_tensor(pe, S, K, bank, w_hi, w_lo)
                for g in range(2):
                    pe.wait_ge(S("wlo"), 2 * n + g + 1)
                    need(pe, S("u0"), 2 * (n - 1) + g - 1)
                    products(pe, bank[2 * q + g][:, :], w_hi[:, 2 * q + g, :], w_lo[:, 2 * q + g, :], h[0], h[1],
                             range(DC)).then_inc(S("mm"), 1)

            loop(pe, chunk)

        @block.scalar
        def _(act):
            def split(n, q, g):
                act.wait_ge(S(f"w{g}"), 16 * n + 16)
                need(act, S("mm"), 2 * (n - 2) + g + 1)
                act.activation(w_hi[:, 2 * q + g, :], raw[:, g, :], ACT.Copy).then_inc(S("whi"), 1)

            def keep(n):
                act.wait_ge(S("ff"), n + 1)
                act.activation(ff[0][:, n, :], full[:, :], ACT.Copy).then_inc(S("ff_hi"), 1)

            head_scalar(act, S, K, rstd[:, :], z, lambda j: split(j // 2, j // 2, j % 2))

            def chunk(n, q):
                act.wait_ge(S("col"), n + 1)
                for g in range(2):
                    act.wait_ge(S("mm"), 2 * n + g + 1)
                    need(act, S("tap1"), 2 * (n - 1) + g + 1)
                    act.activation(z[:, g, :], bank[2 * q + g][:, :], ACT.Copy).then_inc(S("z"), 1)
                    need(act, S("ff"), n)
                    act.activation(u[:, g, :], bank[2 * q + g][:, :], ACT.Identity, bias=col[:, q, 4 * g + 3:4 * g + 4],
                                   scale=col[:, q, 4 * g + 2:4 * g + 3]).then_inc(S("u0"), 1)
                act.wait_ge(S("tap1"), 2 * n + 1)
                act.activation(th[:, :], u[:, 0, :], ACT.Tanh, scale=0.5).then_inc(S("th"), 1)
                if splits(n):
                    split(n + 2, q, 0)
                    split(n + 2, q, 1)
                keep(n)

            loop(act, chunk)

        @block.vector
        def _(dve):
            for g in range(2):
                for k in range(3):
                    at = 2 * FC * k + FC * g
                    dve.tensor_copy(cols[:, :, 4 * g + k], V["conv_ff_w_2"][:, at:at + FC]).then_inc(S("cols"), 1)
                dve.tensor_copy(cols[:, :, 4 * g + 3], V["conv_ff_b_2"][:, FC * g:FC * (g + 1)]).then_inc(S("cols"), 1)
            dve.wait_ge(S("cols"), 8)

            def split(n, q, g):
                dve.wait_ge(S("whi"), 2 * n + g + 1)
                split_lo(dve, w_lo[:, 2 * q + g, :], raw[:, g, :], w_hi[:, 2 * q + g, :]).then_inc(S("wlo"), 1)

            def keep(n):
                dve.wait_ge(S("ff_hi"), n + 1)
                split_lo(dve, ff[1][:, n, :], full[:, :], ff[0][:, n, :]).then_inc(S("ff_lo"), 1)

            head_vector(dve, S, K, "norm2_g_2", rstd[:, :], z, lambda j: split(j // 2, j // 2, j % 2))

            def chunk(n, q):
                need(dve, S("u0"), 2 * (n - 1))
                need(dve, S("tap1"), 2 * (n - 1))
                dve.tensor_copy(col[:, q, :], cols[:, n, :]).then_inc(S("col"), 1)
                for g in range(2):
                    dve.wait_ge(S("u0"), 2 * n + g + 1)
                    if g == 0:
                        dve.wait_ge(S("col"), n + 1)
                    dve.scalar_tensor_tensor(out=u[:, g, 1:T], in0=z[:, g, 0:T - 1],
                                             scalar=col[:, q, 4 * g + 1:4 * g + 2], in1=u[:, g, 1:T],
                                             op0=ALU.mult, op1=ALU.add).then_inc(S("tap2"), 1)
                    dve.wait_ge(S("tap2"), 2 * n + g + 1)
                    dve.scalar_tensor_tensor(out=u[:, g, 2:T], in0=z[:, g, 0:T - 2],
                                             scalar=col[:, q, 4 * g:4 * g + 1], in1=u[:, g, 2:T],
                                             op0=ALU.mult, op1=ALU.add).then_inc(S("tap1"), 1)
                dve.wait_ge(S("th"), n + 1)
                dve.scalar_tensor_tensor(out=u[:, 0, :], in0=th[:, :], scalar=1.0, in1=u[:, 0, :], op0=ALU.add,
                                         op1=ALU.mult).then_inc(S("silu"), 1)
                dve.wait_ge(S("silu"), n + 1)
                need(dve, S("ff_lo"), n)
                dve.scalar_tensor_tensor(out=full[:, :], in0=u[:, 0, :], scalar=0.5, in1=u[:, 1, :], op0=ALU.mult,
                                         op1=ALU.mult).then_inc(S("ff"), 1)
                if splits(n):
                    split(n + 2, q, 0)
                    split(n + 2, q, 1)
                keep(n)

            loop(dve, chunk)


def tiles(w):
    k, n = w.shape
    return np.ascontiguousarray(w.reshape(k // P, P, n // P, P).transpose(2, 1, 0, 3)).reshape(n // P, P, k)


def layout(inputs):
    a = {k: np.asarray(v) for k, v in inputs.items()}
    o = {"consts": constants(), "distance": distances()}
    a["subln_g_2"] = np.tile(a["subln_g_2"], (1, 2))
    vec = lambda n: a[n].reshape(-1, P).T
    o["params"] = np.ascontiguousarray(np.concatenate([vec(n) for n, _ in PARAMS], 1))
    o["x"] = np.ascontiguousarray(a["x"][0].T.reshape(DC, P, T).transpose(1, 0, 2))
    lora = np.concatenate([a["a_w1"][0], a["a_a1"][0]], 1)
    o["lora1"] = np.ascontiguousarray(lora.reshape(DC, P, P).transpose(1, 0, 2))
    lora = np.concatenate([a["a_w2"][0], a["a_a2"][0]], 0)
    o["lora2"] = np.ascontiguousarray(lora.reshape(P, IC, P).transpose(1, 0, 2))
    for n, name in enumerate("rkvg"):
        o["w_" + name] = tiles(a["a_w_in"][0, n])
    o["w_out1"] = tiles(a["a_w_out"][0])
    cbug = tiles(a["b_w_in"][0]).reshape(4, IC, P, D)
    o["w_conv"] = np.ascontiguousarray(cbug[[2, 0, 3, 1]].transpose(1, 0, 2, 3))
    o["w_out2"] = tiles(a["b_w_out"][0])
    o["w_in2"] = tiles(a["w_in_2"][0][:, IN_ORDER])
    o["w_lru"] = np.ascontiguousarray(np.stack([a["w_rgate_2"][0], a["w_igate_2"][0]]).reshape(2, 4, 2, HD, HD)
                                      .transpose(2, 3, 0, 1, 4)).reshape(P, 2, 4, HD)
    o["lam"] = np.ascontiguousarray(np.stack([a[n][0] for n in ("lam_q1_2", "lam_k1_2", "lam_q2_2", "lam_k2_2")]))
    o["w_out3"] = tiles(a["w_out_2"][0])
    up = tiles(a["w_ff_up_2"][0]).reshape(2, FC, P, D)
    o["w_up"] = np.ascontiguousarray(up.transpose(1, 0, 2, 3))
    o["w_down"] = tiles(a["w_ff_down_2"][0])
    return o


def kernel(**inputs):
    import concourse.bacc as bacc
    from concourse.bass_utils import run_bass_kernel_spmd

    nc = bacc.Bacc("TRN2", target_bir_lowering=False, num_devices=1)
    arrays = layout(inputs)
    ins = {n: nc.dram_tensor(f"in_{n}", a.shape, F32, kind="ExternalInput").ap() for n, a in arrays.items()}
    out = nc.dram_tensor("out_y", (P, DC, T), F32, kind="ExternalOutput").ap()
    program(nc, ins, out)
    r = run_bass_kernel_spmd(nc, [{f"in_{n}": a for n, a in arrays.items()}], core_ids=[0])
    y = r.results[0]["out_y"]
    return np.ascontiguousarray(y.transpose(2, 1, 0).reshape(1, T, D))
```

```python
from contextlib import ExitStack

import numpy as np
import concourse.bass as bass
from concourse import mybir

ALU = mybir.AluOpType
ACT = mybir.ActivationFunctionType
AX_X = mybir.AxisListType.X
F32 = mybir.dt.float32
F32R = mybir.dt.float32r

P = 128
T = 512
D = 1024
DC = D // P
DI = 2048
IC = DI // P
HD = 64
NCH = T // HD
TB = T // P
LORA = 64
RMS_EPS = 1e-6
GN_EPS = 64e-5
EXP_HALF = 0.6065306597126334
LRU = 512
DFF = 2816
FC = DFF // P
PIN = 2560
IN_ORDER = np.r_[0:1536, 1792:2304, 1536:1792, 2304:2560]
LVL = 6
FAR = 1e30
DIST = [0, 1 * P, 3 * P, 6 * P, 10 * P]
LN2 = 0.6931471805599453
LAM_INIT = 0.8 - 0.6 * float(np.exp(0.0))

PARAMS = [("a_norm", D), ("a_mu", 6 * D), ("a_w0", DI), ("a_a0", DI), ("a_kk", DI), ("a_ka", DI), ("a_rk", DI),
          ("a_lnw", DI), ("a_lnb", DI), ("b_norm", D), ("b_conv", 3 * DI), ("final_norm", D), ("norm1_g_2", D),
          ("conv_a_w_2", 4 * LRU), ("conv_a_b_2", LRU), ("b_rgate_2", LRU), ("b_igate_2", LRU), ("lru_lambda_2", LRU),
          ("subln_g_2", P),
          ("norm2_g_2", D), ("conv_ff_w_2", 6 * DFF), ("conv_ff_b_2", 2 * DFF), ("final_g_2", D)]
PCOL = {}
_at = 0
for _name, _len in PARAMS:
    PCOL[_name] = _at
    _at += _len // P
NPAR = _at

CONSTS = [("ident", P), ("head_sum", P), ("head_mean", P), ("row_mean", P), ("score_mask", 2 * P),
          ("level_first", P), ("level_mask", 5 * HD), ("scan_keep", T), ("eye", 6 * HD),
          ("minus_after", P), ("minus_all", P), ("before", P)]
CCOL = {}
_at = 0
for _name, _len in CONSTS:
    CCOL[_name] = _at
    _at += _len
NCON = _at


def constants():
    c = np.zeros((P, NCON), np.float32)
    i, j = np.meshgrid(np.arange(P), np.arange(P), indexing="ij")
    same = (i // HD) == (j // HD)

    def put(name, a):
        c[:, CCOL[name]:CCOL[name] + a.shape[1]] = a

    put("ident", i == j)
    put("head_sum", same)
    put("head_mean", same / HD)
    put("row_mean", np.full((P, P), 1.0 / D))
    put("score_mask", np.concatenate([-1.0 * (same & (j > i)), 1.0 * (same & (j >= i))], 1))
    below = lambda n: (i // (2 * n) == j // (2 * n)) & (i % (2 * n) >= n) & (j % (2 * n) < n)
    put("level_first", below(1).T)
    put("level_mask", np.concatenate([np.tile(below(1 << k)[0:HD, 0:HD], (2, 1)) for k in range(1, LVL)], 1))
    put("scan_keep", np.tile((np.arange(T) % HD != 0), (P, 1)))
    put("eye", np.tile(np.eye(HD), (2, 6)))
    put("minus_after", -1.0 * (i > j))
    put("minus_all", -np.ones((P, P)))
    put("before", i < j)
    return c


def distances():
    d = np.zeros((P, DIST[-1]), np.float32)
    for b in range(TB):
        t, s = np.meshgrid(b * P + np.arange(P), np.arange((b + 1) * P), indexing="ij")
        d[:, DIST[b]:DIST[b + 1]] = np.where(s // HD <= t // HD, np.abs(t - s), FAR)
    return d


def need(eng, sem, n):
    if isinstance(n, int) and n <= 0:
        return
    eng.wait_ge(sem, n)


def apart(eng):
    eng.nop(nofuse=True)


class Sems:

    def __init__(self, nc, ctx, phase):
        self.nc, self.ctx, self.phase, self.have = nc, ctx, phase, {}
        ctx.callback(self.clear)

    def __call__(self, name):
        if name not in self.have:
            self.have[name] = self.ctx.enter_context(self.nc.semaphore(f"{self.phase}_{name}"))
        return self.have[name]

    def clear(self):
        numbers = sorted(s.num for s in self.have.values())
        first = 0
        for n in range(1, len(numbers) + 1):
            if n == len(numbers) or numbers[n] != numbers[n - 1] + 1:
                self.nc.gpsimd.sem_clear(range(numbers[first], numbers[n - 1] + 1))
                first = n
        self.nc.all_engine_barrier()


def products(pe, out, w_hi, w_lo, x_hi, x_lo, ks, first=True, last=True):
    for n, k in enumerate(ks):
        w = slice(n * P, (n + 1) * P)
        pe.matmul(out, w_hi[:, w], x_hi[:, k, :], start=(first and n == 0), stop=False)
        pe.matmul(out, w_hi[:, w], x_lo[:, k, :], start=False, stop=False)
        m = pe.matmul(out, w_lo[:, w], x_hi[:, k, :], start=False, stop=(last and n == len(ks) - 1))
    return m


def split_lo(dve, lo, full, hi):
    return dve.tensor_tensor(lo, full, hi.bitcast(F32), ALU.subtract)


def norm_squares(act, S, tag, x, sq, ready):
    for j in range(DC):
        ready(j)
        need(act, S(tag + "_sum"), j - 1)
        act.activation(sq[:, j % 2, :], x[:, j, :], ACT.Square).then_inc(S(tag + "_sq"), 1)


def norm_tensor(pe, S, tag, row_mean, sq, bank):
    for j in range(DC):
        pe.wait_ge(S(tag + "_sq"), j + 1)
        pe.matmul(bank, row_mean, sq[:, j % 2, :], start=(j == 0), stop=(j == DC - 1)).then_inc(S(tag + "_sum"), 1)


def norm_factor(act, S, tag, bank, rstd, eps):
    act.activation(rstd, bank, ACT.Ln, bias=eps).then_inc(S(tag + "_ln"), 1)
    act.wait_ge(S(tag + "_ln"), 1)
    act.activation(rstd, rstd, ACT.Exp, scale=-0.5).then_inc(S(tag + "_rstd"), 1)


def norm_vector(dve, S, tag, x, g, rstd, out):
    dve.wait_ge(S(tag + "_rstd"), 1)
    for j in range(DC):
        dve.scalar_tensor_tensor(out=out[:, j, :], in0=x[:, j, :], scalar=g[:, j:j + 1], in1=rstd,
                                 op0=ALU.mult, op1=ALU.mult).then_inc(S(tag + "_out"), 1)


NORM_BANK = 4


def head_scalar(act, S, K, rstd, tmp, split):
    norm_factor(act, S, "norm", K["bank"][NORM_BANK][:, :], rstd, K["eps"][:, 0:1])
    split(0)
    split(1)
    for k in range(DC):
        act.wait_ge(S("norm_out"), k + 1)
        act.activation(K["h"][0][:, k, :], tmp[:, k % 2, :], ACT.Copy).then_inc(S("norm_hi"), 1)
        if k in (1, 3):
            split(2 + k // 2)


def head_vector(dve, S, K, gain, rstd, tmp, split):
    hi, lo = K["h"]

    def scaled(k):
        need(dve, S("norm_lo"), k - 1)
        dve.scalar_tensor_tensor(out=tmp[:, k % 2, :], in0=K["x"][:, k, :], scalar=K["V"][gain][:, k:k + 1],
                                 in1=rstd, op0=ALU.mult, op1=ALU.mult).then_inc(S("norm_out"), 1)

    dve.wait_ge(S("norm_rstd"), 1)
    scaled(0)
    scaled(1)
    split(0)
    split(1)
    for k in range(DC):
        dve.wait_ge(S("norm_hi"), k + 1)
        split_lo(dve, lo[:, k, :], tmp[:, k % 2, :], hi[:, k, :]).then_inc(S("norm_lo"), 1)
        if k + 2 < DC:
            scaled(k + 2)
        if k in (1, 3):
            split(2 + k // 2)


def head_tensor(pe, S, K, banks, w_hi, w_lo):
    half = DC // 2
    for first in (0, half):
        for pair in (0, 2):
            for k in range(first, first + half):
                if pair == 0:
                    pe.wait_ge(S("norm_lo"), k + 1)
                for j in (pair, pair + 1):
                    if k == 0:
                        pe.wait_ge(S("wlo"), j + 1)
                    m = products(pe, banks[j][:, :], w_hi[:, j, k * P:], w_lo[:, j, k * P:], *K["h"], [k],
                                 k == 0, k == DC - 1)
                    if k == DC - 1:
                        m.then_inc(S("mm"), 1)


def program(nc, ins, out, stop_after=None):
    with ExitStack() as top:
        def sbt(ctx, name, shape, dt=F32, side="left"):
            return ctx.enter_context(nc.sbuf_tensor(name, shape, dt, side=side))

        def pair(ctx, name, chunks, side="left"):
            return [sbt(ctx, name + part, [P, chunks, T], F32R, side) for part in ("_hi", "_lo")]

        bank = [top.enter_context(nc.psum_tensor(f"bank{i}", [P, T], F32)) for i in range(8)]
        con = sbt(top, "con", [P, NCON])
        par = sbt(top, "par", [P, NPAR])
        eps = sbt(top, "eps", [P, 3])
        C = {n: con[:, CCOL[n]:CCOL[n] + k] for n, k in CONSTS}
        V = {n: par[:, PCOL[n]:PCOL[n] + k // P] for n, k in PARAMS}
        K = dict(nc=nc, ins=ins, out=out, bank=bank, C=C, V=V, eps=eps, con=con, par=par, sbt=sbt, pair=pair)
        with ExitStack() as right:
            gate = K["gate"] = sbt(right, "gate", [P, IC, T], side="right")
            with ExitStack() as left:
                K["lerp"] = {n: sbt(left, f"lerp_{n}", [P, DC, T]) for n in "rkv"}
                K["hidden"] = sbt(left, "hidden", [P, T])
                K["mixpar"] = sbt(left, "mixpar", [P, IC, 8])
                lerp_phase(K)
                rwkv_phase(K)
            if stop_after == "rwkv":
                return
            x = K["x"] = sbt(top, "x", [P, DC, T])
            norms = top.enter_context(ExitStack())
            h = K["h"] = pair(norms, "h", DC)
            with ExitStack() as inner:
                y = K["y"] = pair(inner, "y", IC, "right")
                project_phase(K, "out1", y, IC, "w_out1", load_x=True, full=gate)
                conv_phase(K)
                project_phase(K, "out2", y, IC, "w_out2", norm="final_norm")
            if stop_after == "x3":
                return
            mix = top.enter_context(ExitStack())
            mixed = K["mixed"] = sbt(mix, "mixed", [P, DC, T])
            K["proj"] = gate
            with ExitStack() as left:
                K["vals"] = sbt(left, "vals", [P, TB, 4 * P])
                K["dist"] = sbt(left, "dist", [P, DIST[-1]])
                K["lams"] = sbt(left, "lams", [P, 8])
                input_phase(K)
                mixer_phase(K)
            if stop_after == "mixed":
                return
        with ExitStack() as right:
            y = pair(right, "m", DC, "right")
            project_phase(K, "out3", y, DC, "w_out3", full=mixed)
        mix.close()
        with ExitStack() as right:
            ff = K["ff"] = pair(right, "ff", FC, "right")
            up_phase(K)
            norms.close()
            project_phase(K, "down", ff, FC, "w_down", norm="final_g_2", squares=False, store=True)


def lerp_phase(K):
    nc, ins, bank, C, V = (K[n] for n in ("nc", "ins", "bank", "C", "V"))
    eps, gate, lerp, hidden, mixpar = (K[n] for n in ("eps", "gate", "lerp", "hidden", "mixpar"))
    RING, JOBS = 2, 4
    with ExitStack() as ctx:
        S = Sems(nc, ctx, "lerp")
        x = K["sbt"](ctx, "x_in", [P, DC, T])
        xx = K["sbt"](ctx, "xx", [P, DC, T])
        tmp = [gate[:, 0:DC, :], x]
        h = gate[:, DC:2 * DC, :]
        xg_hi, xg_lo = K["pair"](ctx, "xg", DC)
        raw, w_hi, w_lo = (K["sbt"](ctx, "g_" + n, [P, RING, DC * P], t) for n, t in
                           (("raw", F32), ("hi", F32R), ("lo", F32R)))
        tmp2 = K["sbt"](ctx, "xg_full", [P, 2, T])
        wl = K["sbt"](ctx, "lora_w1", [P, DC, P])
        sq = K["sbt"](ctx, "sq", [P, 2, T])
        rstd = K["sbt"](ctx, "rstd", [P, T])
        thg = K["sbt"](ctx, "thg", [P, 2, T])
        block = ctx.enter_context(nc.Block())
        mu = V["a_mu"].rearrange("p (j c) -> p j c", j=6)
        MU = {"r": 0, "w": 1, "k": 2, "v": 3, "a": 4, "g": 5}
        dst = {"w": tmp[0], "a": tmp[1], **lerp}

        @block.sync
        def _(sp):
            for n in range(2):
                half = slice(n * DC // 2, (n + 1) * DC // 2)
                sp.dma_start(x[:, half, :], ins["x"][:, half, :]).then_inc(S(f"x{n}"), 16)
                if n == 0:
                    sp.dma_start(K["con"][:, :], ins["consts"]).then_inc(S("const"), 16)
            sp.dma_start(K["par"][:, :], ins["params"]).then_inc(S("param"), 16)
            sp.dma_start(wl[:, :, :], ins["lora1"]).then_inc(S("wl"), 16)

            def load(i, s):
                n = RING * i + s
                need(sp, S("wlo"), n - RING + 1)
                sp.dma_start(raw[:, s, :], ins["w_g"][n]).then_inc(S(f"w{s}"), 16)

            for s in range(RING):
                load(0, s)
            with sp.Fori(1, IC // RING) as i:
                for s in range(RING):
                    load(i, s)

        @block.gpsimd
        def _(pool):
            for n, v in enumerate((RMS_EPS, GN_EPS, 10 * LN2)):
                pool.memset(eps[:, n:n + 1], v).then_inc(S("eps"), 1)
            pool.wait_ge(S("param"), 16)
            for n, (name, a, b) in enumerate((("a_w0", 0.5, 0.0), ("a_a0", 0.5, 0.0), ("a_ka", 0.5, 0.0),
                                              ("a_ka", -0.5, 1.0), ("a_kk", 1.0, 0.0), ("a_rk", 1.0, 0.0),
                                              ("a_lnw", 1.0, 0.0), ("a_lnb", 1.0, 0.0))):
                pool.tensor_scalar(mixpar[:, :, n], V[name], a, b, ALU.mult, ALU.add).then_inc(S("mixpar"), 1)
            for j in range(DC):
                pool.wait_ge(S("norm_out"), j + 1)
                pool.tensor_tensor(xx[:, j, 1:T], h[:, j, 0:T - 1], h[:, j, 1:T], ALU.subtract).then_inc(S("xx"), 1)

        @block.scalar
        def _(act):
            act.wait_ge(S("eps"), 3)
            norm_squares(act, S, "norm", x, sq,
                         lambda j: act.wait_ge(S(f"x{2 * j // DC}"), 16) if 2 * j % DC == 0 else None)
            act.wait_ge(S("norm_sum"), DC)
            norm_factor(act, S, "norm", bank[0][:, :], rstd[:, :], eps[:, 0:1])

            def split(n):
                act.wait_ge(S(f"w{n % RING}"), 16 * (n // RING) + 16)
                need(act, S("g_mm"), n - RING + 1)
                act.activation(w_hi[:, n % RING, :], raw[:, n % RING, :], ACT.Copy).then_inc(S("whi"), 1)

            for n in range(RING):
                split(n)
            for j in range(DC):
                act.wait_ge(S("lerp_g"), j + 1)
                act.activation(xg_hi[:, j, :], tmp2[:, j % 2, :], ACT.Copy).then_inc(S("xg_hi"), 1)
            for n in range(IC):
                act.wait_ge(S("g_mm"), n + 1)
                if n + RING < IC:
                    split(n + RING)
                if n == 2:
                    act.wait_ge(S("hid_mm"), 1)
                    act.activation(hidden[0:LORA, :], bank[1][0:LORA, :], ACT.Tanh).then_inc(S("hid"), 1)
                if n == 6:
                    act.wait_ge(S("hid_mm"), 2)
                    act.activation(hidden[LORA:P, :], bank[1][LORA:P, :], ACT.Copy).then_inc(S("hid"), 1)
                need(act, S("gate"), n - 1)
                act.activation(thg[:, n % 2, :], bank[2 + n % JOBS][:, :], ACT.Tanh, scale=0.5).then_inc(S("thg"), 1)

        @block.tensor
        def _(pe):
            pe.wait_ge(S("const"), 16)
            norm_tensor(pe, S, "norm", C["row_mean"], sq, bank[0][:, :])

            def job(i, s, ks=range(DC)):
                n = JOBS * i + s
                if ks[0] == 0:
                    pe.wait_ge(S("wlo"), n + 1)
                    need(pe, S("gate"), n - JOBS + 1)
                at = s % RING
                m = products(pe, bank[2 + s][:, :], w_hi[:, at, ks[0] * P:], w_lo[:, at, ks[0] * P:], xg_hi, xg_lo, ks,
                             ks[0] == 0, ks[-1] == DC - 1)
                if ks[-1] == DC - 1:
                    m.then_inc(S("g_mm"), 1)

            def hiddens(n):
                lo, hi = ((0, LORA), (LORA, P))[n]
                for j in range(DC):
                    pe.wait_ge(S("lerp"), DC * n + j + 1)
                    m = pe.matmul(bank[1][lo:hi, :], wl[:, j, lo:hi], tmp[n][:, j, :], start=(j == 0),
                                  stop=(j == DC - 1))
                m.then_inc(S("hid_mm"), 1)

            for k in range(DC):
                pe.wait_ge(S("xg_lo"), k + 1)
                for s in range(2):
                    job(0, s, [k])
            job(0, 2)
            pe.wait_ge(S("wl"), 16)
            hiddens(0)
            job(0, 3)
            for s in range(JOBS):
                job(1, s)
                if s == 1:
                    hiddens(1)
            with pe.Fori(2, IC // JOBS) as i:
                for s in range(JOBS):
                    job(i, s)

        @block.vector
        def _(dve):
            dve.wait_ge(S("param"), 16)
            dve.wait_ge(S("norm_rstd"), 1)

            def normed(j):
                dve.scalar_tensor_tensor(out=h[:, j, :], in0=x[:, j, :], scalar=V["a_norm"][:, j:j + 1],
                                         in1=rstd[:, :], op0=ALU.mult, op1=ALU.mult).then_inc(S("norm_out"), 1)

            def lerps(name, js=range(DC)):
                for j in js:
                    dve.scalar_tensor_tensor(out=dst[name][:, j, :], in0=xx[:, j, :],
                                             scalar=mu[:, MU[name], j:j + 1], in1=h[:, j, :],
                                             op0=ALU.mult, op1=ALU.add).then_inc(S("lerp"), 1)

            def split(n):
                dve.wait_ge(S("whi"), n + 1)
                split_lo(dve, w_lo[:, n % RING, :], raw[:, n % RING, :], w_hi[:, n % RING, :]).then_inc(S("wlo"), 1)

            def lo(j):
                dve.wait_ge(S("xg_hi"), j + 1)
                split_lo(dve, xg_lo[:, j, :], tmp2[:, j % 2, :], xg_hi[:, j, :]).then_inc(S("xg_lo"), 1)

            normed(0)
            normed(1)
            for n in range(RING):
                split(n)
            for j in range(DC):
                dve.wait_ge(S("norm_out"), j + 1)
                dve.tensor_scalar(xx[:, j, 0:1], h[:, j, 0:1], -1.0, None, ALU.mult).then_inc(S("xx0"), 1)
                if j + 2 < DC:
                    normed(j + 2)
                dve.wait_ge(S("xx"), j + 1)
                dve.wait_ge(S("xx0"), j + 1)
                need(dve, S("xg_lo"), j - 1)
                dve.scalar_tensor_tensor(out=tmp2[:, j % 2, :], in0=xx[:, j, :], scalar=mu[:, MU["g"], j:j + 1],
                                         in1=h[:, j, :], op0=ALU.mult, op1=ALU.add).then_inc(S("lerp_g"), 1)
                if j:
                    lo(j - 1)
            lo(DC - 1)
            split(RING)
            split(RING + 1)
            lerps("w")
            left = [(name, range(k, k + DC // 2)) for name in "arkv" for k in (0, DC // 2)]
            dve.wait_ge(S("hid_mm"), 1)
            for n in range(IC):
                if n >= RING and n + RING < IC:
                    split(n + RING)
                if n == IC // 2:
                    dve.wait_ge(S("lerp"), DC * 5)
                dve.wait_ge(S("thg"), n + 1)
                dve.scalar_tensor_tensor(out=gate[:, n, :], in0=thg[:, n % 2, :], scalar=1.0,
                                         in1=bank[2 + n % JOBS][:, :], op0=ALU.add, op1=ALU.mult)\
                    .then_inc(S("gate"), 1)
                if n < len(left):
                    lerps(*left[n])


def rwkv_phase(K):
    nc, ins, bank, C, V = (K[n] for n in ("nc", "ins", "bank", "C", "V"))
    eps, gate, lerp, hidden, mixpar, sbt = (K[n] for n in ("eps", "gate", "lerp", "hidden", "mixpar", "sbt"))
    with ExitStack() as ctx:
        S = Sems(nc, ctx, "mix")
        ring = {n: sbt(ctx, f"w_{n}", [P, DC * P]) for n in "krv"}
        lora = sbt(ctx, "w_lora2", [P, P])
        kap, bet, kd, ke, be, vT = (sbt(ctx, n, [P, T]) for n in ("kap", "bet", "kd", "ke", "be", "vT"))
        rt, bonus = sbt(ctx, "rt", [P, 2, T]), sbt(ctx, "bonus", [P, 2, T])
        dend = sbt(ctx, "dend", [P, 2, 6 * HD])
        ld, cum, e1, tha, kp, kraw, kk, nn, rraw, bon = (
            sbt(ctx, n, [P, T]) for n in ("ld", "cum", "e1", "tha", "kp", "kraw", "kk", "nn", "rraw", "bon"))
        LA = sbt(ctx, "LA", [P, 2, TB, 2 * P])
        MK = sbt(ctx, "MK", [P, 2, TB, 2 * P])
        XK = sbt(ctx, "XK", [P, 2, TB, P])
        NTG = sbt(ctx, "NTG", [P, 2, TB, P])
        tok = {n: sbt(ctx, f"{n}_tok", [P, TB, P]) for n in ("ke", "be", "v")}
        inv, low = (sbt(ctx, n, [P, 2, TB, HD]) for n in ("inv", "low"))
        invT, low_wide = (sbt(ctx, n, [P, 2, TB, P]) for n in ("invT", "low_wide"))
        rh = sbt(ctx, "rh", [P, T])
        phi = sbt(ctx, "phi", [P, 6 * HD])
        st = sbt(ctx, "st", [P, NCH, HD])
        y = sbt(ctx, "y", [P, T])
        yc, yv = sbt(ctx, "yc", [P, T]), sbt(ctx, "yv", [P, T])
        chan = sbt(ctx, "chan", [P, 2, 6])
        affine = sbt(ctx, "affine", [P, 2])
        block = ctx.enter_context(nc.Block())

        G, YB, ROT = bank[0:2], bank[2], bank[4:8]
        SB = (bank[3], ROT[2])
        PH = (ROT[3], ROT[0])
        MEANB, VARB, NNB, BONB = 0, 1, 2, 3
        MVB, TKGB, RHB = 0, (1, 2), 1
        chunks = lambda ap: ap.rearrange("p (n t) -> p n t", t=HD)
        blocks = lambda ap: ap.rearrange("p (b t) -> p b t", t=P)
        pairs = lambda ap: ap.rearrange("p (b t) -> p b t", t=2 * P)
        thin = lambda ap: ap.rearrange("p (b t) -> p b t", t=HD)
        over = lambda ap, n: ap.rearrange("p (o k) -> p o k", o=1).broadcast_to([ap.shape[0], n, ap.shape[1]])
        ends = lambda ap: chunks(ap)[:, :, HD - 1:HD].broadcast_to([P, NCH, HD])
        rows = (slice(0, HD), slice(HD, P))
        JOBS = ["w", "a", "k", "r", "v"]
        NJ = len(JOBS)

        def run(step):
            def loop(eng):
                step(0)
                step(1)
                with eng.Fori(1, IC // 2 - 1) as i:
                    step(2 * i, 0)
                    step(2 * i + 1, 1)
                step(IC - 2)
                step(IC - 1)
            return loop

        @block.sync
        def _(sp):
            def load(c, p=None):
                for n, name in enumerate("krv"):
                    need(sp, S("gemm"), NJ * (c - 1) + 3 + n)
                    sp.dma_start(ring[name][:, :], ins["w_" + name][c]).then_inc(S("w_" + name), 16)
                    if n == 0:
                        sp.dma_start(lora[:, :], ins["lora2"][c]).then_inc(S("w_lora"), 16)

            load(0)
            load(1)
            with sp.Fori(2, IC) as c:
                load(c)

        @block.gpsimd
        def _(pool):
            def prepare(n, p):
                pool.wait_ge(S("tanh"), 2 * n + 1)
                apart(pool)
                pool.tensor_scalar(ld[:, :], ld[:, :], -EXP_HALF / 2, -EXP_HALF / 2, ALU.mult, ALU.add)\
                    .then_inc(S("ld"), 1)
                pool.wait_ge(S("tanh"), 2 * n + 2)
                need(pool, S("bon"), n)
                apart(pool)
                pool.tensor_scalar(kp[:, :], tha[:, :], chan[:, p, 2:3], chan[:, p, 3:4], ALU.mult, ALU.add)\
                    .then_inc(S("kfac"), 1)
                pool.wait_ge(S("kfac"), n + 1)
                apart(pool)
                pool.tensor_scalar(tha[:, :], tha[:, :], 0.5, 0.5, ALU.mult, ALU.add).then_inc(S("a"), 1)

            def prepare_keys(n, p):
                pool.wait_ge(S("exp"), 2 * n + 1)
                need(pool, S("phi"), 2 * (n - 1))
                pool.tensor_tensor(dend[:, p, :].rearrange("p (n t) -> p n t", t=HD),
                                   C["eye"].rearrange("p (n t) -> p n t", t=HD),
                                   chunks(e1[:, :])[:, 1:7, HD - 1:HD].broadcast_to([P, 6, HD]), ALU.mult)\
                    .then_inc(S("dend"), 1)
                pool.wait_ge(S("kk"), n + 1)
                pool.wait_ge(S("a"), n + 1)
                pool.tensor_tensor(tha[:, :], tha[:, :], kk[:, :], ALU.mult).then_inc(S("b"), 1)
                need(pool, S("score_mm"), 8 * n)
                pool.tensor_tensor(chunks(kap[:, :])[:, :, 1:HD], chunks(kk[:, :])[:, :, 1:HD],
                                   chunks(e1[:, :])[:, :, 0:HD - 1], ALU.mult).then_inc(S("kap"), 1)
                apart(pool)
                pool.tensor_scalar(chunks(kap[:, :])[:, :, 0:1], chunks(kk[:, :])[:, :, 0:1], 1.0, None, ALU.mult)\
                    .then_inc(S("kap"), 1)

            def finish(c, p):
                pool.wait_ge(S("yn"), c + 1)
                pool.wait_ge(S("aff"), c + 1)
                apart(pool)
                pool.tensor_scalar(yv[:, :], yc[:, :], affine[:, 0:1], affine[:, 1:2], ALU.mult, ALU.add)\
                    .then_inc(S("affine"), 1)
                pool.wait_ge(S("affine"), c + 1)
                pool.wait_ge(S("bonus"), c + 1)
                pool.tensor_tensor(yv[:, :], yv[:, :], bonus[:, p, :], ALU.add).then_inc(S("plus"), 1)

            def step(c, p=None):
                q = c % 2 if p is None else p
                last = isinstance(c, int) and c == IC - 1
                if not last:
                    prepare(c + 1, 1 - q)
                if not (isinstance(c, int) and c == 0):
                    finish(c - 1, 1 - q)
                if not last:
                    prepare_keys(c + 1, 1 - q)

            prepare(0, 0)
            prepare_keys(0, 0)
            run(step)(pool)
            finish(IC - 1, 1)

        @block.scalar
        def _(act):
            def tanhs(n, q):
                act.wait_ge(S("gemm"), NJ * n + 1)
                act.wait_ge(S("chan"), n + 1)
                need(act, S("cum"), n)
                act.activation(ld[:, :], G[(q + 0) % 2][:, :], ACT.Tanh, bias=chan[:, q, 0:1], scale=0.5)\
                    .then_inc(S("tanh"), 1)
                act.wait_ge(S("gemm"), NJ * n + 2)
                need(act, S("bet"), n)
                act.activation(tha[:, :], G[(q + 1) % 2][:, :], ACT.Tanh, bias=chan[:, q, 1:2], scale=0.5)\
                    .then_inc(S("tanh"), 1)

            def evacuate(n, q, k, dst, readers):
                act.wait_ge(S("gemm"), NJ * n + 3 + k)
                for name, count in readers:
                    need(act, S(name), count)
                act.activation(dst, G[(q + k) % 2][:, :], ACT.Copy).then_inc(S("evac"), 1)

            def exps(n):
                act.wait_ge(S("cum"), n + 1)
                need(act, S("rt"), n)
                need(act, S("kap"), 2 * n)
                act.activation(e1[:, :], cum[:, :], ACT.Exp).then_inc(S("exp"), 1)
                act.wait_ge(S("exp"), 2 * n + 1)
                act.activation(cum[:, :], cum[:, :], ACT.Exp, scale=-1.0).then_inc(S("exp"), 1)

            def keys_scaled(n, q):
                act.wait_ge(S("gemm"), NJ * n + 3)
                need(act, S("kap"), 2 * n)
                act.activation(kk[:, :], G[q % 2][:, :], ACT.Copy, scale=chan[:, q, 4:5]).then_inc(S("kk0"), 1)

            def key_square(n):
                act.wait_ge(S("kk0"), n + 1)
                need(act, S("kk"), n)
                act.activation(nn[:, :], kk[:, :], ACT.Square).then_inc(S("nsq"), 1)

            def key_norm(n):
                act.wait_ge(S("nclamp"), n + 1)
                act.activation(nn[:, :], nn[:, :], ACT.Ln, scale=float(2 ** 20)).then_inc(S("nln"), 1)
                act.wait_ge(S("nln"), n + 1)
                act.activation(nn[:, :], nn[:, :], ACT.Exp, scale=-0.5, bias=eps[:, 2:3]).then_inc(S("nrs"), 1)

            def center_square(c):
                act.wait_ge(S("yc"), c + 1)
                need(act, S("gated"), c)
                act.activation(yv[:, :], yc[:, :], ACT.Square).then_inc(S("ysq"), 1)

            def group_norm(c):
                act.wait_ge(S("var_mm"), c + 1)
                act.activation(yv[:, :], ROT[VARB][:, :], ACT.Ln, bias=eps[:, 1:2]).then_inc(S("yln"), 1)
                act.wait_ge(S("yln"), c + 1)
                act.activation(yv[:, :], yv[:, :], ACT.Exp, scale=-0.5).then_inc(S("yrs"), 1)

            def step(c, p=None):
                last = isinstance(c, int) and c == IC - 1
                first = isinstance(c, int) and c == 0
                q = c % 2 if p is None else p
                for k in range(4):
                    act.wait_ge(S("turn_mm"), 4 * c + k + 1)
                    src = blocks(ROT[k][:, :])
                    if k == 0:
                        src = src.rearrange("p b (h k) -> p h b k", h=2)
                        for h in range(2):
                            act.activation(XK[:, h, :, 0:HD], src[:, h], ACT.Copy).then_inc(S("turned"), 1)
                    else:
                        act.activation(tok[("ke", "be", "v")[k - 1]][:, :, :], src, ACT.Copy)\
                            .then_inc(S("turned"), 1)
                if not last:
                    tanhs(c + 1, 1 - q)
                if not first:
                    center_square(c - 1)
                    group_norm(c - 1)
                if not last:
                    exps(c + 1)
                    keys_scaled(c + 1, 1 - q)
                    evacuate(c + 1, 1 - q, 0, kraw[:, :], [("kp", c + 1)])
                    key_square(c + 1)
                    key_norm(c + 1)
                    evacuate(c + 1, 1 - q, 1, rraw[:, :], [("bon", c + 1), ("rt", c + 1)])
                act.wait_ge(S("mv_mm"), c + 1)
                for h in range(2):
                    act.activation(XK[:, h, :, HD:P],
                                   ROT[MVB][:, :].rearrange("p (b h k) -> p h b k", h=2, k=HD)[:, h],
                                   ACT.Copy, scale=-1.0).then_inc(S("mv"), 1)
                for h in range(2):
                    act.wait_ge(S("tkg_mm"), 2 * c + h + 1)
                    act.activation(NTG[:, h, :, :], blocks(ROT[TKGB[h]][:, :]), ACT.Copy, scale=-1.0)\
                        .then_inc(S("tkg"), 1)
                if not last:
                    evacuate(c + 1, 1 - q, 2, vT[:, :], [("bonus", c + 1), ("turn_mm", 4 * (c + 1))])
                act.wait_ge(S("y_mm"), c + 1)
                need(act, S("yc"), c)
                act.activation(y[:, :], YB[:, :], ACT.Copy).then_inc(S("y"), 1)

            tanhs(0, 0)
            exps(0)
            keys_scaled(0, 0)
            evacuate(0, 0, 0, kraw[:, :], [])
            key_square(0)
            key_norm(0)
            evacuate(0, 0, 1, rraw[:, :], [])
            evacuate(0, 0, 2, vT[:, :], [])
            run(step)(act)
            center_square(IC - 1)
            group_norm(IC - 1)

        @block.tensor
        def _(pe):
            def gemm(n, q):
                for k, name in enumerate("krv"):
                    for j in range(DC):
                        if j == 0:
                            pe.wait_ge(S("w_" + name), 16 * (n + 1))
                            bank_free(n, 2 + k)
                        m = pe.matmul(G[(q + k) % 2][:, :], ring[name][:, j * P:(j + 1) * P],
                                      lerp[name][:, j, :], start=(j == 0), stop=(j == DC - 1))
                        if j == DC - 1:
                            m.then_inc(S("gemm"), 1)
                        yield

            def bank_free(n, j):
                if j == 0:
                    need(pe, S("evac"), 3 * n - 1)
                elif j == 1:
                    need(pe, S("evac"), 3 * n)
                elif j < 4:
                    need(pe, S("tanh"), 2 * n + j - 1)
                else:
                    need(pe, S("evac"), 3 * n + 1)

            def loras(n, q):
                pe.wait_ge(S("w_lora"), 16 * (n + 1))
                for j in range(2):
                    bank_free(n, j)
                    pe.matmul(G[(q + j) % 2][:, :], lora[rows[j], :], hidden[rows[j], :], start=True, stop=True)\
                        .then_inc(S("gemm"), 1)

            def stat(weights, src, b, sem):
                pe.matmul(ROT[b][:, :], weights, src, start=True, stop=True).then_inc(sem, 1)

            def means(c):
                pe.wait_ge(S("y"), c + 1)
                stat(C["head_mean"], y[:, :], MEANB, S("mean_mm"))

            def variances(c):
                pe.wait_ge(S("ysq"), c + 1)
                stat(C["head_mean"], yv[:, :], VARB, S("var_mm"))

            def key_sums(n):
                pe.wait_ge(S("nsq"), n + 1)
                stat(C["head_sum"], nn[:, :], NNB, S("nn_mm"))

            def bonus_sums(n):
                pe.wait_ge(S("bon"), n + 1)
                stat(C["head_sum"], bon[:, :], BONB, S("bsum_mm"))

            def step(c, p=None):
                q = c % 2 if p is None else p
                last = isinstance(c, int) and c == IC - 1
                first = isinstance(c, int) and c == 0
                more = iter(()) if last else gemm(c + 1, 1 - q)

                def fill(k):
                    for _ in range(k):
                        next(more, None)

                pe.wait_ge(S("be"), c + 1)
                pe.wait_ge(S("kap"), 2 * (c + 1))
                pe.wait_ge(S("evac"), 3 * (c + 1))
                for k, src in enumerate((kap, ke, be, vT)):
                    if k == 0:
                        need(pe, S("phi"), 2 * c)
                    if k == 1:
                        need(pe, S("rh"), c)
                    if k == 2:
                        need(pe, S("st"), 7 * c)
                    if k == 3:
                        need(pe, S("bonus"), c + 1)
                    for b in range(TB):
                        m = pe.transpose(ROT[k][:, b * P:(b + 1) * P], src[:, b * P:(b + 1) * P], C["ident"])
                    m.then_inc(S("turn_mm"), 1)
                for h in range(2):
                    for k in range(4):
                        if h == 0:
                            pe.wait_ge(S("turned"), 5 * c + k + 2)
                        else:
                            pe.wait_ge(S("score"), 8 * c + k + 1)
                        lhs = (bet, kd)[k // 2]
                        for b in range(2):
                            blk = 2 * (k % 2) + b
                            tk = slice(blk * P, (blk + 1) * P)
                            pe.matmul(ROT[k][:, 2 * b * P:(2 * b + 1) * P], lhs[rows[h], tk], kap[rows[h], tk],
                                      start=True, stop=True)
                            m = pe.matmul(ROT[k][:, (2 * b + 1) * P:(2 * b + 2) * P], lhs[rows[h], tk],
                                          rt[rows[h], q, tk], start=True, stop=True)
                        m.then_inc(S("score_mm"), 1)
                if not last:
                    loras(c + 1, 1 - q)
                fill(2)
                if not first:
                    pe.wait_ge(S("score"), 8 * c + 5)
                    means(c - 1)
                fill(2)
                if not first:
                    pe.wait_ge(S("score"), 8 * c + 6)
                    variances(c - 1)
                fill(1)
                for lv in range(5):
                    for h in range(2):
                        if lv == 0 and h == 0 and not first:
                            pe.wait_ge(S("yc"), c)
                        if lv == 0:
                            pe.wait_ge(S("score"), 8 * c + 8)
                        if lv > 0:
                            pe.wait_ge(S("low"), 10 * c + 2 * (lv - 1) + h + 1)
                        if lv == 2 and h == 1 and not last:
                            pe.wait_ge(S("nclamp"), c + 2)
                        if lv == 0:
                            pe.wait_ge(S("inv"), INV(c, h, 0))
                        else:
                            pe.wait_ge(S("inv_up"), 8 * c + 2 * (lv - 1) + h + 1)
                        for b in range(TB):
                            m = pe.matmul(ROT[2 * h][:, b * HD:(b + 1) * HD], LA[:, h, b, 0:P], inv[:, h, b, :],
                                          start=True, stop=True)
                        m.then_inc(S("low_mm"), 1)
                    fill(1)
                    for h in range(2):
                        if lv == 0 and h == 0 and not first:
                            pe.wait_ge(S("yln"), c)
                        pe.wait_ge(S("low"), 10 * c + 2 * lv + h + 1)
                        if lv > 0:
                            pe.wait_ge(S("inv"), INV(c, h, lv))
                        lhs, rhs, w = (invT, low, HD) if lv < 4 else (low_wide, invT, P)
                        for b in range(TB):
                            m = pe.matmul(ROT[2 * h + 1][:, b * w:(b + 1) * w], lhs[:, h, b, :], rhs[:, h, b, :],
                                          start=True, stop=True)
                        m.then_inc(S("up_mm"), 1)
                    fill((2, 2, 1, 0, 1)[lv])
                    if lv == 1 and not last:
                        pe.wait_ge(S("low"), 10 * c + 4)
                        key_sums(c + 1)
                pe.wait_ge(S("low"), 10 * c + 9)
                for h in range(2):
                    for b in range(TB):
                        m = pe.matmul(ROT[MVB][:, (2 * b + h) * HD:(2 * b + h + 1) * HD], MK[:, h, b, 0:P],
                                      tok["v"][:, b, rows[h]], start=True, stop=True)
                m.then_inc(S("mv_mm"), 1)
                need(pe, S("y"), c)
                for h in range(2):
                    for b in range(TB):
                        pe.matmul(YB[rows[h], b * P:(b + 1) * P], tok["v"][:, b, rows[h]], MK[:, h, b, P:2 * P],
                                  start=(b == 0), stop=False, skip_group_check=True)
                pe.wait_ge(S("mv"), 2 * c + 2)
                for h in range(2):
                    pe.wait_ge(S("inv"), INV(c, h, 5))
                    if h == 0:
                        pe.wait_ge(S("low"), 10 * c + 10)
                    for b in range(TB):
                        m = pe.matmul(ROT[TKGB[h]][:, b * P:(b + 1) * P], invT[:, h, b, :], XK[:, h, b, :],
                                      start=True, stop=True)
                    m.then_inc(S("tkg_mm"), 1)
                fill(2)
                pe.wait_ge(S("tkg"), 2 * c + 2)
                apart(pe)
                for i in range(1, NCH - 1):
                    r = rows[i % 2]
                    for h in range(2):
                        m = pe.matmul(PH[i % 2][rows[h], (i - 1) * HD:i * HD], NTG[r, h, i // 2, 0:HD],
                                      tok["be"][r, i // 2, rows[h]], start=True, stop=True)
                m.then_inc(S("phi_mm"), 1)
                need(pe, S("st"), 7 * c)
                apart(pe)
                for i in range(NCH - 1):
                    r = rows[i % 2]
                    for h in range(2):
                        pe.matmul(SB[i % 2][rows[h], i * HD:(i + 1) * HD], tok["ke"][r, i // 2, rows[h]],
                                  tok["v"][r, i // 2, rows[h]], start=(i < 2), stop=False, skip_group_check=True)
                        m = pe.matmul(SB[i % 2][rows[h], i * HD:(i + 1) * HD], tok["be"][r, i // 2, rows[h]],
                                      NTG[r, h, i // 2, HD:P], start=False, stop=False, skip_group_check=True)
                m.then_inc(S("st_mm"), 1)
                for h in range(2):
                    for b in range(TB):
                        m = pe.matmul(ROT[RHB][rows[h], b * P:(b + 1) * P], NTG[:, h, b, 0:HD],
                                      LA[:, h, b, P:2 * P], start=True, stop=True)
                m.then_inc(S("rh_mm"), 1)
                for h in range(2):
                    for b in range(TB):
                        pe.matmul(YB[rows[h], b * P:(b + 1) * P], NTG[:, h, b, HD:P], LA[:, h, b, P:2 * P],
                                  start=False, stop=False, skip_group_check=True)
                pe.wait_ge(S("phi"), 2 * (c + 1))
                for i in range(1, NCH):
                    pe.wait_ge(S("st"), 7 * c + i)
                    apart(pe)
                    if i < NCH - 1:
                        for h in range(2):
                            m = pe.matmul(SB[i % 2][rows[h], i * HD:(i + 1) * HD], phi[rows[h], (i - 1) * HD:i * HD],
                                          st[rows[h], i, :], start=False, stop=True, skip_group_check=True)
                        m.then_inc(S("st_mm"), 1)
                    if i == 1:
                        pe.wait_ge(S("rh"), c + 1)
                        apart(pe)
                    for h in range(2):
                        m = pe.matmul(YB[rows[h], i * HD:(i + 1) * HD], st[rows[h], i, :],
                                      rh[rows[h], i * HD:(i + 1) * HD], start=False, stop=True,
                                      skip_group_check=True)
                    fill(1)
                m.then_inc(S("y_mm"), 1)
                fill(24)
                if not last:
                    pe.wait_ge(S("phi"), 2 * (c + 1))
                    bonus_sums(c + 1)

            loras(0, 0)
            for _ in gemm(0, 0):
                pass
            key_sums(0)
            bonus_sums(0)
            run(step)(pe)
            means(IC - 1)
            variances(IC - 1)

        @block.vector
        def _(dve):
            def channels(n, q):
                for name, k in (("kk0", 1), ("tanh", 2), ("bon", 1)):
                    need(dve, S(name), k * (n - 1))
                dve.tensor_copy(chan[:, q, :], mixpar[:, n, 0:6]).then_inc(S("chan"), 1)

            def turn(dst, src, h):
                for half in rows:
                    m = dve.transpose(*(t[half, h] if t is inv else t[half, h, :, half] for t in (dst, src)))
                m.then_inc(S("inv"), 1)

            dve.memset(low_wide[:, :, :, :], 0.0).then_inc(S("wide0"), 1)
            dve.wait_ge(S("wide0"), 1)

            def affines(c):
                need(dve, S("affine"), c)
                dve.tensor_copy(affine[:, :], mixpar[:, c, 6:8]).then_inc(S("aff"), 1)

            def decay(n):
                dve.wait_ge(S("ld"), n + 1)
                need(dve, S("bet"), n)
                dve.tensor_tensor_scan(cum[:, :], C["scan_keep"], ld[:, :], 0.0, ALU.mult, ALU.add)\
                    .then_inc(S("cum"), 1)

            def keys(n):
                key_factor(n)
                decayed_keys(n)

            def key_factor(n):
                dve.wait_ge(S("kfac"), n + 1)
                dve.wait_ge(S("evac"), 3 * n + 1)
                dve.wait_ge(S("kk0"), n + 1)
                dve.tensor_tensor(kp[:, :], kraw[:, :], kp[:, :], ALU.mult).then_inc(S("kp"), 1)

            def decayed_keys(n):
                dve.wait_ge(S("kp"), n + 1)
                dve.wait_ge(S("exp"), 2 * n + 2)
                need(dve, S("score_mm"), 8 * n)
                dve.tensor_tensor(kd[:, :], kp[:, :], cum[:, :], ALU.mult).then_inc(S("kd"), 1)
                dve.wait_ge(S("kd"), n + 1)
                dve.tensor_tensor(chunks(ke[:, :]), chunks(kd[:, :]), ends(e1[:, :]), ALU.mult).then_inc(S("ke"), 1)

            def clamp(n):
                dve.wait_ge(S("nn_mm"), n + 1)
                dve.tensor_scalar(nn[:, :], ROT[NNB][:, :], 1e-24, None, ALU.max).then_inc(S("nclamp"), 1)

            def normed(n):
                dve.wait_ge(S("nrs"), n + 1)
                dve.tensor_tensor(kk[:, :], kk[:, :], nn[:, :], ALU.mult).then_inc(S("kk"), 1)

            def reads(n, p):
                dve.wait_ge(S("evac"), 3 * n + 2)
                dve.tensor_tensor(rt[:, p, :], rraw[:, :], e1[:, :], ALU.mult).then_inc(S("rt"), 1)
                need(dve, S("bsum_mm"), n)
                dve.scalar_tensor_tensor(out=bon[:, :], in0=rraw[:, :], scalar=chan[:, p, 5:6], in1=kp[:, :],
                                         op0=ALU.mult, op1=ALU.mult).then_inc(S("bon"), 1)

            def removals(n):
                dve.wait_ge(S("b"), n + 1)
                dve.tensor_tensor(bet[:, :], tha[:, :], cum[:, :], ALU.mult).then_inc(S("bet"), 1)
                dve.wait_ge(S("bet"), n + 1)
                dve.tensor_tensor(chunks(be[:, :]), chunks(bet[:, :]), ends(e1[:, :]), ALU.mult).then_inc(S("be"), 1)

            def bonuses(n, p):
                dve.wait_ge(S("bsum_mm"), n + 1)
                dve.wait_ge(S("evac"), 3 * n + 3)
                need(dve, S("plus"), n - 1)
                dve.tensor_tensor(bonus[:, p, :], ROT[BONB][:, :], vT[:, :], ALU.mult).then_inc(S("bonus"), 1)

            def center(c):
                dve.wait_ge(S("mean_mm"), c + 1)
                need(dve, S("affine"), c)
                dve.tensor_tensor(yc[:, :], y[:, :], ROT[MEANB][:, :], ALU.subtract).then_inc(S("yc"), 1)

            def scaled(c):
                dve.wait_ge(S("yrs"), c + 1)
                dve.tensor_tensor(yc[:, :], yc[:, :], yv[:, :], ALU.mult).then_inc(S("yn"), 1)

            def gated(c):
                dve.wait_ge(S("plus"), c + 1)
                dve.scalar_tensor_tensor(out=gate[:, c, :], in0=yv[:, :], scalar=0.5, in1=gate[:, c, :],
                                         op0=ALU.mult, op1=ALU.mult).then_inc(S("gated"), 1)

            def step(c, p=None):
                q = c % 2 if p is None else p
                last = isinstance(c, int) and c == IC - 1
                first = isinstance(c, int) and c == 0
                if not last:
                    channels(c + 1, 1 - q)
                if not first:
                    affines(c - 1)
                for h in range(2):
                    for k in range(4):
                        dve.wait_ge(S("score_mm"), 8 * c + 4 * h + k + 1)
                        dst = (LA, MK)[k // 2]
                        b = 2 * (k % 2)
                        dve.tensor_tensor(dst[:, h, b:b + 2, :], pairs(ROT[k][:, :]), over(C["score_mask"], 2),
                                          ALU.mult).then_inc(S("score"), 1)
                    dve.wait_ge(S("score"), 8 * c + 4 * h + 2)
                    dve.tensor_tensor(invT[:, h], LA[:, h, :, 0:P], over(C["level_first"], TB), ALU.mult)\
                        .then_inc(S("inv0"), 1)
                    dve.wait_ge(S("inv0"), 4 * c + 2 * h + 1)
                    dve.tensor_tensor(invT[:, h], invT[:, h], over(C["ident"], TB), ALU.add).then_inc(S("inv0"), 1)
                    dve.wait_ge(S("inv0"), 4 * c + 2 * h + 2)
                    turn(inv, invT, h)
                if not first:
                    center(c - 1)
                for lv in range(5):
                    for h in range(2):
                        dve.wait_ge(S("low_mm"), 10 * c + 2 * lv + h + 1)
                        for half in ((slice(0, P),) if lv < 4 else rows):
                            dst = low[half, h] if lv < 4 else low_wide[half, h, :, half]
                            m = dve.tensor_tensor(dst, thin(ROT[2 * h][half, 0:TB * HD]),
                                                  over(C["level_mask"][half, lv * HD:(lv + 1) * HD], TB), ALU.mult)
                        m.then_inc(S("low"), 1)
                    if not last:
                        if lv == 0:
                            decay(c + 1)
                        if lv == 2:
                            decayed_keys(c + 1)
                        if lv == 3:
                            normed(c + 1)
                        if lv == 4:
                            removals(c + 1)
                    for h in range(2):
                        dve.wait_ge(S("up_mm"), 10 * c + 2 * lv + h + 1)
                        if lv < 4:
                            dve.tensor_tensor(inv[:, h], inv[:, h], thin(ROT[2 * h + 1][:, 0:TB * HD]), ALU.add)\
                                .then_inc(S("inv_up"), 1)
                        else:
                            dve.tensor_tensor(invT[:, h], invT[:, h], blocks(ROT[2 * h + 1][:, :]), ALU.add)\
                                .then_inc(S("inv"), 1)
                    for h in range(2 if lv < 4 else 0):
                        dve.wait_ge(S("inv_up"), 8 * c + 2 * lv + h + 1)
                        turn(invT, inv, h)
                    if lv == 0 and not first:
                        scaled(c - 1)
                    if lv == 1 and not last:
                        clamp(c + 1)
                    if lv == 1 and not last:
                        key_factor(c + 1)
                    if lv == 2 and not first:
                        gated(c - 1)
                    if lv == 4 and not last:
                        reads(c + 1, 1 - q)
                dve.wait_ge(S("phi_mm"), c + 1)
                dve.wait_ge(S("dend"), c + 1)
                for i in range(2):
                    half = lambda ap: ap.rearrange("p (n t) -> p n t", t=2 * HD)[:, :, i * HD:(i + 1) * HD]
                    dve.tensor_tensor(half(phi[:, :]), half(PH[1 - i][:, 0:6 * HD]), half(dend[:, q, :]), ALU.add)\
                        .then_inc(S("phi"), 1)
                for i in range(1, NCH):
                    dve.wait_ge(S("st_mm"), 7 * c + i)
                    dve.tensor_copy(st[:, i, :], SB[(i - 1) % 2][:, (i - 1) * HD:i * HD]).then_inc(S("st"), 1)
                    if i == 1:
                        dve.wait_ge(S("rh_mm"), c + 1)
                        dve.tensor_tensor(rh[:, :], ROT[RHB][:, :], rt[:, q, :], ALU.add).then_inc(S("rh"), 1)
                if not last:
                    bonuses(c + 1, 1 - q)

            channels(0, 0)
            decay(0)
            keys(0)
            clamp(0)
            normed(0)
            removals(0)
            reads(0, 0)
            bonuses(0, 0)
            run(step)(dve)
            affines(IC - 1)
            center(IC - 1)
            scaled(IC - 1)
            gated(IC - 1)


def INV(c, h, lv):
    return 12 * c + 2 * lv + h + 1


def project_phase(K, tag, src, kt, weights, norm=None, squares=True, load_x=False, store=False, full=None):
    nc, ins, bank, C, V, sbt, x = (K[n] for n in ("nc", "ins", "bank", "C", "V", "sbt", "x"))
    U = kt // 2
    with ExitStack() as ctx:
        S = Sems(nc, ctx, tag)
        raw = sbt(ctx, tag + "_raw", [P, 2, U * P])
        w_hi, w_lo = (sbt(ctx, tag + n, [P, 4, U * P], F32R) for n in ("_whi", "_wlo"))
        sq = sbt(ctx, tag + "_sq", [P, 2, T])
        rstd = sbt(ctx, tag + "_rstd", [P, T])
        block = ctx.enter_context(nc.Block())

        def loop(eng, job):
            job(0, 0)
            job(1, 1)
            with eng.Fori(1, DC // 2) as i:
                job(2 * i, 0)
                job(2 * i + 1, 1)

        @block.sync
        def _(sp):
            def load(n, q):
                for u in range(2):
                    need(sp, S("wlo"), 2 * (n - 1) + u + 1)
                    sp.dma_start(raw[:, u, :], ins[weights][n, :, u * U * P:(u + 1) * U * P])\
                        .then_inc(S(f"w{u}"), 16)

            loop(sp, load)
            if store:
                for j in range(DC):
                    sp.wait_ge(S("norm_out"), j + 1)
                    sp.dma_start(K["out"][:, j, :], x[:, j, :]).then_inc(S("stored"), 16)
                sp.wait_ge(S("stored"), 16 * DC)

        @block.tensor
        def _(pe):
            def job(n, q):
                need(pe, S("added"), n - 1)
                for u in range(2):
                    pe.wait_ge(S("wlo"), 2 * n + u + 1)
                    if full is not None and isinstance(n, int) and n == 0:
                        for k in range(u * U, (u + 1) * U):
                            pe.wait_ge(S("src_lo"), k + 1)
                            m = products(pe, bank[q][:, :], w_hi[:, 2 * q + u, (k - u * U) * P:],
                                         w_lo[:, 2 * q + u, (k - u * U) * P:], src[0], src[1], [k], k == 0,
                                         k == kt - 1)
                    else:
                        m = products(pe, bank[q][:, :], w_hi[:, 2 * q + u, :], w_lo[:, 2 * q + u, :], src[0],
                                     src[1], range(u * U, (u + 1) * U), u == 0, u == 1)
                    m.then_inc(S("unit"), 1)

            loop(pe, job)
            if norm:
                norm_tensor(pe, S, "norm", C["row_mean"], sq, bank[5][:, :])
            if squares:
                norm_tensor(pe, S, "next", C["row_mean"], sq, bank[NORM_BANK][:, :])

        @block.scalar
        def _(act):
            def split(n, q):
                for u in range(2):
                    act.wait_ge(S(f"w{u}"), 16 * n + 16)
                    need(act, S("unit"), 2 * (n - 2) + u + 1)
                    act.activation(w_hi[:, 2 * q + u, :], raw[:, u, :], ACT.Copy).then_inc(S("whi"), 1)
                    if full is not None and isinstance(n, int) and n == 0:
                        for k in range(u * U, (u + 1) * U):
                            act.activation(src[0][:, k, :], full[:, k, :], ACT.Copy).then_inc(S("src_hi"), 1)

                    if load_x and isinstance(n, int) and n == 0 and u == 0:
                        act.dma_start(x[:, :, :], ins["x"]).then_inc(S("x"), 16)

            loop(act, split)
            if norm:
                norm_squares(act, S, "norm", x, sq, lambda j: act.wait_ge(S("added"), j + 1))
                act.wait_ge(S("norm_sum"), DC)
                norm_factor(act, S, "norm", bank[5][:, :], rstd[:, :], K["eps"][:, 0:1])
            if squares:
                norm_squares(act, S, "next", x, sq, lambda j: act.wait_ge(S("norm_out" if norm else "added"), j + 1))

        @block.vector
        def _(dve):
            def split(n, q):
                for u in range(2):
                    dve.wait_ge(S("whi"), 2 * n + u + 1)
                    split_lo(dve, w_lo[:, 2 * q + u, :], raw[:, u, :], w_hi[:, 2 * q + u, :])\
                        .then_inc(S("wlo"), 1)
                    if full is not None and isinstance(n, int) and n == 0:
                        for k in range(u * U, (u + 1) * U):
                            dve.wait_ge(S("src_hi"), k + 1)
                            split_lo(dve, src[1][:, k, :], full[:, k, :], src[0][:, k, :]).then_inc(S("src_lo"), 1)

            def add(n, q):
                dve.wait_ge(S("unit"), 2 * n + 2)
                dve.tensor_tensor(x[:, n, :], x[:, n, :], bank[q][:, :], ALU.add).then_inc(S("added"), 1)

            split(0, 0)
            split(1, 1)
            if load_x:
                dve.wait_ge(S("x"), 16)
            with dve.Fori(1, DC // 2) as i:
                for q in range(2):
                    add(2 * i - 2 + q, q)
                    split(2 * i + q, q)
            add(DC - 2, 0)
            add(DC - 1, 1)
            if norm:
                norm_vector(dve, S, "norm", x, V[norm], rstd[:, :], x)


def conv_phase(K):
    nc, ins, bank, C, V, sbt, h, y = (K[n] for n in ("nc", "ins", "bank", "C", "V", "sbt", "h", "y"))
    JOBS = 4
    with ExitStack() as ctx:
        S = Sems(nc, ctx, "conv")
        raw = sbt(ctx, "conv_raw", [P, 2, DC * P])
        w_hi, w_lo = (sbt(ctx, "conv" + n, [P, JOBS, DC * P], F32R) for n in ("_whi", "_wlo"))
        full, u, cu, cv, th, gg, rstd = (K["gate"][:, n, :] for n in range(7))
        tmp = K["gate"][:, 7:9, :]
        taps = sbt(ctx, "conv_taps", [P, IC, 3])
        tap = sbt(ctx, "conv_tap", [P, 2, 3])
        block = ctx.enter_context(nc.Block())

        def loop(eng, chunk):
            chunk(0, 0)
            chunk(1, 1)
            with eng.Fori(1, IC // 2 - 1) as i:
                chunk(2 * i, 0)
                chunk(2 * i + 1, 1)
            chunk(IC - 2, 0)
            chunk(IC - 1, 1)

        def last(n):
            return isinstance(n, int) and n == IC - 1

        @block.sync
        def _(sp):
            def load(n, q=None):
                for j in range(JOBS):
                    need(sp, S("wlo"), JOBS * n + j - 1)
                    sp.dma_start(raw[:, j % 2, :], ins["w_conv"][n, j]).then_inc(S(f"w{j % 2}"), 16)

            loop(sp, load)

        @block.tensor
        def _(pe):
            def chunk(n, q):
                if isinstance(n, int) and n == 0:
                    return head_tensor(pe, S, K, bank, w_hi, w_lo)
                for j in range(JOBS):
                    pe.wait_ge(S("wlo"), JOBS * n + j + 1)
                    need(pe, S(("u", "cu", "gg", "full")[j]), n - 1)
                    products(pe, bank[4 * q + j][:, :], w_hi[:, j, :], w_lo[:, j, :], h[0], h[1], range(DC))\
                        .then_inc(S("mm"), 1)

            loop(pe, chunk)

        @block.scalar
        def _(act):
            def split(n, j):
                act.wait_ge(S(f"w{j % 2}"), 32 * n + 16 * (j // 2) + 16)
                need(act, S("mm"), JOBS * (n - 1) + j + 1)
                act.activation(w_hi[:, j, :], raw[:, j % 2, :], ACT.Copy).then_inc(S("whi"), 1)

            def keep(n):
                act.wait_ge(S("full"), n + 1)
                act.activation(y[0][:, n, :], full[:, :], ACT.Copy).then_inc(S("y_hi"), 1)

            head_scalar(act, S, K, rstd, tmp, lambda j: split(0, j))

            def chunk(n, q):
                act.wait_ge(S("mm"), JOBS * n + 1)
                need(act, S("cu"), n)
                act.activation(u[:, :], bank[4 * q][:, :], ACT.Copy).then_inc(S("u"), 1)
                if not (isinstance(n, int) and n == 0):
                    keep(n - 1)
                if not last(n):
                    split(n + 1, 0)
                act.wait_ge(S("cu"), n + 1)
                act.wait_ge(S("tap"), n + 1)
                need(act, S("full"), n)
                act.activation(cv[:, :], cu[:, :], ACT.Copy, scale=tap[:, q, 2:3]).then_inc(S("tap2"), 1)
                if not last(n):
                    split(n + 1, 1)
                act.wait_ge(S("mm"), JOBS * n + 3)
                need(act, S("gg"), n)
                act.activation(th[:, :], bank[4 * q + 2][:, :], ACT.Tanh, scale=0.5).then_inc(S("th"), 1)
                if not last(n):
                    split(n + 1, 2)
                    split(n + 1, 3)

            loop(act, chunk)
            keep(IC - 1)

        @block.vector
        def _(dve):
            for j in range(3):
                dve.tensor_copy(taps[:, :, j], V["b_conv"][:, j * IC:(j + 1) * IC]).then_inc(S("taps"), 1)
            dve.wait_ge(S("taps"), 3)

            def split(n, j):
                dve.wait_ge(S("whi"), JOBS * n + j + 1)
                split_lo(dve, w_lo[:, j, :], raw[:, j % 2, :], w_hi[:, j, :]).then_inc(S("wlo"), 1)

            def keep(n):
                dve.wait_ge(S("y_hi"), n + 1)
                split_lo(dve, y[1][:, n, :], full[:, :], y[0][:, n, :]).then_inc(S("y_lo"), 1)

            head_vector(dve, S, K, "b_norm", rstd, tmp, lambda j: split(0, j))

            def chunk(n, q):
                need(dve, S("tap2"), n - 1)
                need(dve, S("taps1"), n - 1)
                dve.tensor_copy(tap[:, q, :], taps[:, n, :]).then_inc(S("tap"), 1)
                dve.wait_ge(S("u"), n + 1)
                dve.wait_ge(S("mm"), JOBS * n + 2)
                need(dve, S("taps1"), n)
                dve.tensor_tensor(cu[:, :], bank[4 * q + 1][:, :], u[:, :], ALU.mult).then_inc(S("cu"), 1)
                if not (isinstance(n, int) and n == 0):
                    keep(n - 1)
                if not last(n):
                    split(n + 1, 0)
                dve.wait_ge(S("tap2"), n + 1)
                dve.wait_ge(S("tap"), n + 1)
                dve.scalar_tensor_tensor(out=cv[:, 1:T], in0=cu[:, 0:T - 1], scalar=tap[:, q, 1:2], in1=cv[:, 1:T],
                                         op0=ALU.mult, op1=ALU.add).then_inc(S("taps2"), 1)
                dve.wait_ge(S("taps2"), n + 1)
                dve.scalar_tensor_tensor(out=cv[:, 2:T], in0=cu[:, 0:T - 2], scalar=tap[:, q, 0:1], in1=cv[:, 2:T],
                                         op0=ALU.mult, op1=ALU.add).then_inc(S("taps1"), 1)
                if not last(n):
                    split(n + 1, 1)
                dve.wait_ge(S("th"), n + 1)
                need(dve, S("cg"), n)
                dve.scalar_tensor_tensor(out=gg[:, :], in0=th[:, :], scalar=1.0, in1=bank[4 * q + 2][:, :],
                                         op0=ALU.add, op1=ALU.mult).then_inc(S("gg"), 1)
                dve.wait_ge(S("taps1"), n + 1)
                dve.wait_ge(S("gg"), n + 1)
                dve.scalar_tensor_tensor(out=cv[:, :], in0=cv[:, :], scalar=0.5, in1=gg[:, :],
                                         op0=ALU.mult, op1=ALU.mult).then_inc(S("cg"), 1)
                if not last(n):
                    split(n + 1, 2)
                dve.wait_ge(S("mm"), JOBS * n + 4)
                dve.wait_ge(S("cg"), n + 1)
                need(dve, S("y_lo"), n)
                dve.tensor_tensor(full[:, :], cv[:, :], bank[4 * q + 3][:, :], ALU.mult).then_inc(S("full"), 1)
                if not last(n):
                    split(n + 1, 3)

            loop(dve, chunk)
            keep(IC - 1)


def input_phase(K):
    nc, ins, bank, V, sbt, h, proj, vals, mixed = (K[n] for n in ("nc", "ins", "bank", "V", "sbt", "h", "proj",
                                                                  "vals", "mixed"))
    dist, lams = K["dist"], K["lams"]
    RING, NCHN, NTOK = 4, 16, 4
    NJ = NCHN + NTOK
    GELU = float(np.sqrt(2.0 / np.pi))
    RG = bank[5:7]
    with ExitStack() as ctx:
        S = Sems(nc, ctx, "in2")
        raw = sbt(ctx, "in2_raw", [P, RING, DC * P])
        w_hi, w_lo = (sbt(ctx, "in2" + n, [P, RING, DC * P], F32R) for n in ("_whi", "_wlo"))
        rstd, tmp = sbt(ctx, "in2_rstd", [P, T]), sbt(ctx, "in2_tmp", [P, 2, T])
        wbd = sbt(ctx, "wbd", [P, 2, 4, P])
        lp = sbt(ctx, "lp", [P, 16, 4])
        m4 = lp[:, 7, :]
        xc, rr, ii, la, aa, g1, g2, gl = (sbt(ctx, "lru_" + n, [P, T])
                                          for n in ("xc", "rr", "ii", "la", "aa", "g1", "g2", "gl"))
        lam = sbt(ctx, "lam", [P, 4, 32])
        lamp = sbt(ctx, "lamp", [P, 2, 32])
        rows = (slice(0, HD), slice(HD, P))
        block = ctx.enter_context(nc.Block())

        @block.sync
        def _(sp):
            def load(i, s):
                need(sp, S("wlo"), RING * (i - 1) + s + 1)
                sp.dma_start(raw[:, s, :], ins["w_in2"][RING * i + s]).then_inc(S(f"w{s}"), 16)

            for s in range(RING):
                load(0, s)
            sp.dma_start(lam[:, :, :], ins["lam"].rearrange("(o a) b -> o a b", o=1).broadcast_to([P, 4, 32]))\
                .then_inc(S("lam"), 16)
            sp.wait_ge(S("wbd0"), 1)
            for r in range(2):
                for g in range(2):
                    sp.dma_start(wbd[rows[r], g, :, rows[r]], ins["w_lru"][rows[r], g]).then_inc(S("wbd"), 16)
            sp.dma_start(dist[:, :], ins["distance"]).then_inc(S("dist"), 16)
            with sp.Fori(1, NJ // RING) as i:
                for s in range(RING):
                    load(i, s)

        @block.gpsimd
        def _(pool):
            pool.memset(wbd[:, :, :, :], 0.0).then_inc(S("wbd0"), 1)
            for n in range(4):
                pool.wait_ge(S("ysq"), n + 1)
                pool.tensor_scalar(gl[:, :], gl[:, :], 0.044715, 1.0, ALU.mult, ALU.add).then_inc(S("ycube"), 1)
                pool.wait_ge(S("ycube"), n + 1)
                pool.tensor_tensor(gl[:, :], gl[:, :], proj[:, 4 + n, :], ALU.mult).then_inc(S("yin"), 1)
                pool.wait_ge(S("lru_th"), n + 1)
                pool.tensor_scalar(g1[:, :], g1[:, :], -2.0, 1e-18, ALU.mult, ALU.max).then_inc(S("lru_tm"), 1)
            pool.wait_ge(S("dist"), 16)

        @block.tensor
        def _(pe):
            def job(k):
                s = k % RING
                pe.wait_ge(S("wlo"), k + 1)
                pe.wait_ge(S("copied"), k - RING + 1)
                if k < NCHN:
                    m = products(pe, bank[s][:, :], w_hi[:, s, :], w_lo[:, s, :], h[0], h[1], range(DC))
                else:
                    for b in range(TB):
                        tk = slice(b * P, (b + 1) * P)
                        for k_ in range(DC):
                            w = slice(k_ * P, (k_ + 1) * P)
                            pe.matmul(bank[s][:, tk], h[0][:, k_, tk], w_hi[:, s, w], start=(k_ == 0), stop=False)
                            pe.matmul(bank[s][:, tk], h[0][:, k_, tk], w_lo[:, s, w], start=False, stop=False)
                            m = pe.matmul(bank[s][:, tk], h[1][:, k_, tk], w_hi[:, s, w], start=False,
                                          stop=(k_ == DC - 1))
                m.then_inc(S("mm"), 1)

            def gates(n):
                if n == 0:
                    pe.wait_ge(S("wbd"), 64)
                pe.wait_ge(S("conv"), 3 * n + 3)
                need(pe, S("gate"), 2 * n)
                for g in range(2):
                    pe.matmul(RG[g][:, :], wbd[:, g, n, :], xc[:, :], start=True, stop=True).then_inc(S("rg_mm"), 1)

            head_tensor(pe, S, K, bank, w_hi, w_lo)
            for k in range(RING, NJ):
                job(k)
                if k % 4 == 1:
                    gates(k // 4 - 1)

        @block.scalar
        def _(act):
            def split(k):
                s = k % RING
                act.wait_ge(S(f"w{s}"), 16 * (k // RING) + 16)
                need(act, S("mm"), k - RING + 1)
                act.activation(w_hi[:, s, :], raw[:, s, :], ACT.Copy).then_inc(S("whi"), 1)

            def job(k):
                s = k % RING
                act.wait_ge(S("mm"), k + 1)
                if k + RING < NJ:
                    split(k + RING)
                dst, src = ((proj[:, k, :], bank[s][:, :]) if k < NCHN else
                            (vals[:, :, s * P:(s + 1) * P], bank[s][:, :].rearrange("p (b t) -> p b t", t=P)))
                act.activation(dst, src, ACT.Copy).then_inc(S("copied"), 1)

            def lru(n, stage):
                if stage == 0:
                    act.wait_ge(S("chp"), 1)
                    act.wait_ge(S("copied"), 5 + n)
                    need(act, S("ix"), n)
                    act.activation(xc[:, :], proj[:, n, :], ACT.Identity, bias=V["conv_a_b_2"][:, n:n + 1],
                                   scale=V["conv_a_w_2"][:, 12 + n:13 + n]).then_inc(S("xc0"), 1)
                    need(act, S("lru_out"), n)
                    act.activation(gl[:, :], proj[:, 4 + n, :], ACT.Square).then_inc(S("ysq"), 1)
                elif stage == 1:
                    for g, dst in enumerate((rr, ii)):
                        act.wait_ge(S("rg_mm"), 2 * n + g + 1)
                        act.activation(dst[:, :], RG[g][:, :], ACT.Tanh, bias=lp[:, 8 + g, n:n + 1], scale=0.5)\
                            .then_inc(S("gate"), 1)
                    act.wait_ge(S("yin"), n + 1)
                    act.activation(gl[:, :], gl[:, :], ACT.Tanh, scale=GELU).then_inc(S("yth"), 1)
                elif stage == 2:
                    act.wait_ge(S("la"), n + 1)
                    act.activation(g1[:, :], la[:, :], ACT.Tanh).then_inc(S("lru_th"), 1)
                    act.activation(aa[:, :], la[:, :], ACT.Exp).then_inc(S("lru_a"), 1)
                else:
                    act.wait_ge(S("one_minus"), n + 1)
                    act.activation(g2[:, :], g2[:, :], ACT.Ln).then_inc(S("ln2"), 1)
                    act.wait_ge(S("lru_tm"), n + 1)
                    act.activation(g1[:, :], g1[:, :], ACT.Ln).then_inc(S("ln1"), 1)
                    act.wait_ge(S("lndiff"), n + 1)
                    act.activation(g1[:, :], g1[:, :], ACT.Exp, scale=0.5).then_inc(S("gam"), 1)

            head_scalar(act, S, K, rstd[:, :], tmp, split)
            act.activation(lp[:, 0, :], V["lru_lambda_2"], ACT.Abs).then_inc(S("sp_abs"), 1)
            act.wait_ge(S("sp_abs"), 1)
            act.activation(lp[:, 1, :], lp[:, 0, :], ACT.Exp, scale=-1.0).then_inc(S("sp_e"), 1)
            act.wait_ge(S("sp_u"), 1)
            act.activation(lp[:, 3, :], lp[:, 2, :], ACT.Ln).then_inc(S("sp_ln"), 1)
            act.wait_ge(S("lam_sum"), 2)
            act.activation(lams[:, 2:4], lams[:, 0:2], ACT.Exp).then_inc(S("lam_e"), 1)
            for k in range(NJ):
                job(k)
                if k >= RING:
                    lru(k // 4 - 1, k % 4)

        @block.vector
        def _(dve):
            def split(k):
                s = k % RING
                dve.wait_ge(S("whi"), k + 1)
                split_lo(dve, w_lo[:, s, :], raw[:, s, :], w_hi[:, s, :]).then_inc(S("wlo"), 1)

            head_vector(dve, S, K, "norm1_g_2", rstd[:, :], tmp, split)
            lamb = V["lru_lambda_2"]
            seq = [0]

            def then(ins_):
                seq[0] += 1
                ins_.then_inc(S("small"), 1)
                dve.wait_ge(S("small"), seq[0])

            then(dve.tensor_scalar(lp[:, 8, :], V["b_rgate_2"], 0.5, None, ALU.mult))
            then(dve.tensor_scalar(lp[:, 9, :], V["b_igate_2"], 0.5, None, ALU.mult))
            dve.wait_ge(S("sp_e"), 1)
            dve.tensor_scalar(lp[:, 2, :], lp[:, 1, :], 1.0, None, ALU.add).then_inc(S("sp_u"), 1)
            dve.wait_ge(S("sp_u"), 1)
            then(dve.tensor_scalar(lp[:, 4, :], lp[:, 2, :], -1.0, None, ALU.add))
            then(dve.tensor_scalar(lp[:, 5, :], lp[:, 4, :], 0.0, None, ALU.is_equal))
            then(dve.tensor_tensor(lp[:, 4, :], lp[:, 4, :], lp[:, 5, :], ALU.add))
            then(dve.reciprocal(lp[:, 4, :], lp[:, 4, :]))
            dve.wait_ge(S("sp_ln"), 1)
            then(dve.tensor_tensor(lp[:, 4, :], lp[:, 4, :], lp[:, 3, :], ALU.mult))
            then(dve.tensor_tensor(lp[:, 4, :], lp[:, 4, :], lp[:, 5, :], ALU.add))
            then(dve.tensor_tensor(lp[:, 4, :], lp[:, 4, :], lp[:, 1, :], ALU.mult))
            then(dve.tensor_scalar(lp[:, 6, :], lamb, -1.0, 0.0, ALU.mult, ALU.max))
            then(dve.tensor_tensor(lp[:, 4, :], lp[:, 4, :], lp[:, 6, :], ALU.add))
            dve.tensor_scalar(m4, lp[:, 4, :], -4.0, None, ALU.mult).then_inc(S("chp"), 1)
            dve.wait_ge(S("chp"), 1)
            dve.wait_ge(S("lam"), 16)
            for k in range(2):
                then(dve.tensor_tensor(lamp[:, k, :], lam[:, 2 * k, :], lam[:, 2 * k + 1, :], ALU.mult))
                dve.tensor_reduce(lams[:, k:k + 1], lamp[:, k, :], AX_X, ALU.add).then_inc(S("lam_sum"), 1)
            dve.wait_ge(S("lam_e"), 1)
            then(dve.tensor_tensor(lams[:, 4:5], lams[:, 3:4], lams[:, 2:3], ALU.subtract))
            then(dve.tensor_scalar(lams[:, 5:6], lams[:, 4:5], -LAM_INIT, None, ALU.add))

            def lru(n, stage):
                if stage == 0:
                    for k in range(3):
                        if k == 0:
                            dve.wait_ge(S("xc0"), n + 1)
                        else:
                            dve.wait_ge(S("conv"), 3 * n + k)
                        dve.scalar_tensor_tensor(out=xc[:, k + 1:T], in0=proj[:, n, 0:T - k - 1],
                                                 scalar=V["conv_a_w_2"][:, 4 * (2 - k) + n:4 * (2 - k) + n + 1],
                                                 in1=xc[:, k + 1:T], op0=ALU.mult, op1=ALU.add)\
                            .then_inc(S("conv"), 1)
                elif stage == 1:
                    dve.wait_ge(S("gate"), 2 * n + 1)
                    dve.tensor_scalar(la[:, :], rr[:, :], m4[:, n:n + 1], m4[:, n:n + 1], ALU.mult, ALU.add)\
                        .then_inc(S("la"), 1)
                    dve.wait_ge(S("gate"), 2 * n + 2)
                    dve.scalar_tensor_tensor(out=ii[:, :], in0=ii[:, :], scalar=1.0, in1=xc[:, :], op0=ALU.add,
                                             op1=ALU.mult).then_inc(S("ix"), 1)
                elif stage == 2:
                    dve.wait_ge(S("yth"), n + 1)
                    dve.scalar_tensor_tensor(out=gl[:, :], in0=gl[:, :], scalar=1.0, in1=proj[:, 4 + n, :],
                                             op0=ALU.add, op1=ALU.mult).then_inc(S("gelu"), 1)
                    dve.wait_ge(S("lru_tm"), n + 1)
                    dve.tensor_scalar(g2[:, :], g1[:, :], 0.5, 1.0, ALU.mult, ALU.add).then_inc(S("one_minus"), 1)
                else:
                    dve.wait_ge(S("ln1"), n + 1)
                    dve.wait_ge(S("ln2"), n + 1)
                    dve.tensor_tensor(g1[:, :], g1[:, :], g2[:, :], ALU.subtract).then_inc(S("lndiff"), 1)
                    dve.wait_ge(S("gam"), n + 1)
                    dve.wait_ge(S("ix"), n + 1)
                    dve.scalar_tensor_tensor(out=ii[:, :], in0=ii[:, :], scalar=0.5, in1=g1[:, :], op0=ALU.mult,
                                             op1=ALU.mult).then_inc(S("u"), 1)
                    dve.wait_ge(S("u"), n + 1)
                    dve.wait_ge(S("lru_a"), n + 1)
                    dve.tensor_tensor_scan(rr[:, :], aa[:, :], ii[:, :], 0.0, ALU.mult, ALU.add).then_inc(S("hl"), 1)
                    dve.wait_ge(S("gelu"), n + 1)
                    dve.wait_ge(S("hl"), n + 1)
                    dve.scalar_tensor_tensor(out=mixed[:, n, :], in0=rr[:, :], scalar=0.5, in1=gl[:, :], op0=ALU.mult,
                                             op1=ALU.mult).then_inc(S("lru_out"), 1)

            for k in range(NJ):
                if k + RING < NJ:
                    split(k + RING)
                if k >= RING:
                    lru(k // 4 - 1, k % 4)


def mixer_phase(K):
    nc, ins, bank, C, V, sbt, proj, vals, mixed = (K[n] for n in ("nc", "ins", "bank", "C", "V", "sbt", "proj",
                                                                  "vals", "mixed"))
    SB_SCALE, DF_SCALE = 64 ** -0.5, 32 ** -0.5
    SLOPE = [2.0 ** (-8.0 * (n + 1) / 4) for n in range(4)]
    with ExitStack() as ctx:
        S = Sems(nc, ctx, "mixer")
        t_ = lambda name, shape: sbt(ctx, name, shape)
        za, sp_, ex = (t_("sb_" + n, [P, TB, T]) for n in ("za", "sp", "ex"))
        dist, lams = K["dist"], K["lams"]
        bias = t_("bias", [P, DIST[-1]])
        pr = [t_(f"pr{m}", [P, DIST[-1]]) for m in range(2)]
        pT = t_("pT", [P, TB, T])
        ds_ = t_("ds", [P, 5, 2, TB])
        gsub = t_("gsub", [P, 1])
        do, dsq = t_("do", [P, T]), t_("dsq", [P, T])
        one = t_("one", [P, 1])
        rows = (slice(0, HD), slice(HD, P))
        block = ctx.enter_context(nc.Block())
        N = lambda i: T - i * P

        @block.gpsimd
        def _(pool):
            pool.memset(one[:, :], 1.0).then_inc(S("one"), 1)
            def distance(n):
                need(pool, S("dscore"), 8 * n)
                pool.tensor_scalar(bias[:, :], dist[:, :], -SLOPE[n], None, ALU.mult).then_inc(S("bias"), 1)

            distance(0)
            for n in range(4):
                for i in range(TB):
                    pool.wait_ge(S("relu"), 4 * n + i + 1)
                    pool.wait_ge(S("sb_ln"), 4 * n + i + 1)
                    pool.tensor_tensor(sp_[:, i, 0:N(i)], sp_[:, i, 0:N(i)], za[:, i, 0:N(i)], ALU.add)\
                        .then_inc(S("sp"), 1)
                if n < 3:
                    distance(n + 1)

        @block.tensor
        def _(pe):
            for n in range(4):
                hp = rows[n % 2]
                need(pe, S("sum"), 4 * n)
                for i in range(TB):
                    pe.matmul(bank[2 + i][:, 0:N(i)], proj[hp, 10 + n // 2, i * P:(i + 1) * P],
                              proj[hp, 8 + n // 2, i * P:T], start=True, stop=True).then_inc(S("z_mm"), 1)
                for b in range(TB):
                    for m_ in range(2):
                        k = 2 * b + m_
                        if b == 0:
                            need(pe, S("pT"), 4 * n)
                        else:
                            pe.wait_ge(S("dscore"), 8 * n + k - 1)
                        r = slice(hp.start + 32 * m_, hp.start + 32 * m_ + 32)
                        pe.matmul(bank[m_][:, 0:(b + 1) * P], proj[r, 12 + n // 2, b * P:(b + 1) * P],
                                  proj[r, 14 + n // 2, 0:(b + 1) * P], start=True, stop=True)\
                            .then_inc(S("d_mm"), 1)
                pe.wait_ge(S("spm"), 4 * (n + 1))
                for i in range(TB - 1, -1, -1):
                    m = pe.matmul(bank[2 + i][:, 0:N(i)], C["minus_after"], sp_[:, i, 0:N(i)], start=True,
                                  stop=(i == TB - 1), skip_group_check=True)
                    for j in range(i + 1, TB):
                        m = pe.matmul(bank[2 + i][:, (j - i) * P:N(i)], C["minus_all"], sp_[:, j, 0:N(j)],
                                      start=False, stop=(j == TB - 1), skip_group_check=True)
                    m.then_inc(S("tail_mm"), 1)
                pe.wait_ge(S("dscore"), 8 * n + 8)
                for b in range(TB):
                    pe.wait_ge(S("dp"), 4 * n + b + 1)
                    if b >= 2:
                        pe.wait_ge(S("pT"), 4 * n + b - 1)
                    for j in range(b + 1):
                        m = pe.transpose(bank[b % 2][:, j * P:(j + 1) * P],
                                         pr[0][:, DIST[b] + j * P:DIST[b] + (j + 1) * P], C["ident"])
                    m.then_inc(S("pT_mm"), 1)
                need(pe, S("sb_out"), n // 2)
                pe.wait_ge(S("wm"), 4 * n + 4)
                for i in range(TB):
                    m = pe.matmul(bank[6][hp, i * P:T], vals[:, i, n * HD:(n + 1) * HD], ex[:, i, 0:N(i)],
                                  start=(i == 0), stop=(i == TB - 1), skip_group_check=True)
                m.then_inc(S("sb_mm"), 1)
                pe.wait_ge(S("pT"), 4 * n + 4)
                need(pe, S("dln"), n // 2)
                for j in range(TB):
                    m = pe.matmul(bank[7][hp, j * P:T], vals[:, j, 256 + n * HD:256 + (n + 1) * HD], pT[:, j, j * P:T],
                                  start=(j == 0), stop=(j == TB - 1), skip_group_check=True)
                m.then_inc(S("do_mm"), 1)
                if n % 2:
                    pe.wait_ge(S("dsq"), n // 2 + 1)
                    pe.matmul(bank[7][:, :], C["head_mean"], dsq[:, :], start=True, stop=True).then_inc(S("dv_mm"), 1)

        @block.scalar
        def _(act):
            act.wait_ge(S("one"), 1)
            for n in range(4):
                need(act, S("sp"), 4 * n)
                for i in range(TB):
                    act.wait_ge(S("z_mm"), 4 * n + i + 1)
                    act.activation(za[:, i, 0:N(i)], bank[2 + i][:, 0:N(i)], ACT.Abs, scale=SB_SCALE)\
                        .then_inc(S("zabs"), 1)
                for i in range(TB):
                    act.wait_ge(S("zabs"), 4 * n + i + 1)
                    act.activation(za[:, i, 0:N(i)], za[:, i, 0:N(i)], ACT.Exp, scale=-1.0).then_inc(S("sb_e"), 1)
                for i in range(TB):
                    act.wait_ge(S("sb_e"), 4 * n + i + 1)
                    act.activation(za[:, i, 0:N(i)], za[:, i, 0:N(i)], ACT.Ln, bias=one[:, 0:1]).then_inc(S("sb_ln"), 1)
                for b in range(TB):
                    for m_ in range(2):
                        act.wait_ge(S("dmax"), 8 * n + 2 * b + m_ + 1)
                        act.activation(pr[m_][:, DIST[b]:DIST[b + 1]], pr[m_][:, DIST[b]:DIST[b + 1]], ACT.Exp,
                                       bias=ds_[:, 0, m_, b:b + 1], accum_out=ds_[:, 1, m_, b:b + 1])\
                            .then_inc(S("dexp"), 1)
                for i in range(TB - 1, -1, -1):
                    act.wait_ge(S("sum"), 4 * n + TB - i)
                    act.activation(ex[:, i, 0:N(i)], ex[:, i, 0:N(i)], ACT.Exp).then_inc(S("w"), 1)
                for b in range(TB):
                    act.wait_ge(S("pT_mm"), 4 * n + b + 1)
                    act.activation(pT[:, 0:b + 1, b * P:(b + 1) * P],
                                   bank[b % 2][:, 0:(b + 1) * P].rearrange("p (j t) -> p j t", t=P), ACT.Copy)\
                        .then_inc(S("pT"), 1)
                if n % 2:
                    act.wait_ge(S("sb_mm"), n + 1)
                    act.activation(mixed[:, 4 + n // 2, :], bank[6][:, :], ACT.Copy).then_inc(S("sb_out"), 1)
                    act.wait_ge(S("do_mm"), n + 1)
                    need(act, S("dout"), n // 2)
                    act.activation(do[:, :], bank[7][:, :], ACT.Copy).then_inc(S("do"), 1)
                    act.activation(dsq[:, :], bank[7][:, :], ACT.Square).then_inc(S("dsq"), 1)
                    act.wait_ge(S("dv_mm"), n // 2 + 1)
                    act.activation(dsq[:, :], bank[7][:, :], ACT.Ln, bias=K["eps"][:, 0:1]).then_inc(S("dln"), 1)
                    act.wait_ge(S("dln"), n // 2 + 1)
                    act.activation(dsq[:, :], dsq[:, :], ACT.Exp, scale=-0.5).then_inc(S("drs"), 1)

        @block.vector
        def _(dve):
            dve.tensor_scalar(gsub[:, :], V["subln_g_2"], 1.0 - LAM_INIT, None, ALU.mult).then_inc(S("gsub"), 1)

            def scores(n, b):
                for m_ in range(2):
                    k = 8 * n + 2 * b + m_ + 1
                    part = pr[m_][:, DIST[b]:DIST[b + 1]]
                    dve.wait_ge(S("d_mm"), k)
                    dve.scalar_tensor_tensor(out=part, in0=bank[m_][:, 0:(b + 1) * P], scalar=DF_SCALE,
                                             in1=bias[:, DIST[b]:DIST[b + 1]], op0=ALU.mult, op1=ALU.add)\
                        .then_inc(S("dscore"), 1)
                for m_ in range(2):
                    k = 8 * n + 2 * b + m_ + 1
                    dve.wait_ge(S("dscore"), k)
                    dve.tensor_reduce(ds_[:, 2, m_, b:b + 1], pr[m_][:, DIST[b]:DIST[b + 1]], AX_X, ALU.max)\
                        .then_inc(S("dm"), 1)
                for m_ in range(2):
                    k = 8 * n + 2 * b + m_ + 1
                    dve.wait_ge(S("dm"), k)
                    dve.tensor_scalar(ds_[:, 0, m_, b:b + 1], ds_[:, 2, m_, b:b + 1], -1.0, None, ALU.mult)\
                        .then_inc(S("dmax"), 1)

            for n in range(4):
                for i in range(TB):
                    dve.wait_ge(S("zabs"), 4 * n + i + 1)
                    dve.tensor_scalar(sp_[:, i, 0:N(i)], bank[2 + i][:, 0:N(i)], SB_SCALE, 0.0, ALU.mult,
                                      ALU.max).then_inc(S("relu"), 1)
                dve.wait_ge(S("bias"), n + 1)
                scores(n, 0)
                scores(n, 1)
                scores(n, 2)
                for i in range(TB):
                    dve.wait_ge(S("sp"), 4 * n + i + 1)
                    dve.scalar_tensor_tensor(out=ex[:, i, 0:N(i)], in0=bank[2 + i][:, 0:N(i)], scalar=SB_SCALE,
                                             in1=sp_[:, i, 0:N(i)], op0=ALU.mult, op1=ALU.subtract)\
                        .then_inc(S("logw"), 1)
                    dve.wait_ge(S("logw"), 4 * n + i + 1)
                    dve.tensor_tensor(sp_[:, i, 0:P], sp_[:, i, 0:P], C["before"], ALU.mult).then_inc(S("spm"), 1)
                scores(n, 3)
                dve.wait_ge(S("logw"), 4 * n + 4)
                for i in range(TB - 1, -1, -1):
                    dve.wait_ge(S("tail_mm"), 4 * n + TB - i)
                    dve.tensor_tensor(ex[:, i, 0:N(i)], ex[:, i, 0:N(i)], bank[2 + i][:, 0:N(i)], ALU.add)\
                        .then_inc(S("sum"), 1)
                for b in range(TB):
                    k = 8 * n + 2 * b
                    dve.wait_ge(S("dexp"), k + 2)
                    dve.reciprocal(ds_[:, 3, :, b:b + 1], ds_[:, 1, :, b:b + 1]).then_inc(S("drec"), 1)
                    dve.wait_ge(S("drec"), 4 * n + b + 1)
                    dve.tensor_scalar(ds_[:, 4, 1, b:b + 1], ds_[:, 3, 1, b:b + 1], lams[:, 5:6], None, ALU.mult)\
                        .then_inc(S("dlam"), 1)
                    dve.tensor_scalar(pr[0][:, DIST[b]:DIST[b + 1]], pr[0][:, DIST[b]:DIST[b + 1]],
                                      ds_[:, 3, 0, b:b + 1], None, ALU.mult).then_inc(S("dp0"), 1)
                    dve.wait_ge(S("dp0"), 4 * n + b + 1)
                    dve.wait_ge(S("dlam"), 4 * n + b + 1)
                    dve.scalar_tensor_tensor(out=pr[0][:, DIST[b]:DIST[b + 1]], in0=pr[1][:, DIST[b]:DIST[b + 1]],
                                             scalar=ds_[:, 4, 1, b:b + 1], in1=pr[0][:, DIST[b]:DIST[b + 1]],
                                             op0=ALU.mult, op1=ALU.add).then_inc(S("dp"), 1)
                for i in range(TB - 1, -1, -1):
                    dve.wait_ge(S("w"), 4 * n + TB - i)
                    dve.tensor_tensor(ex[:, i, 0:P], ex[:, i, 0:P], C["before"], ALU.mult).then_inc(S("wm"), 1)
                if n % 2:
                    dve.wait_ge(S("drs"), n // 2 + 1)
                    dve.wait_ge(S("gsub"), 1)
                    dve.scalar_tensor_tensor(out=mixed[:, 6 + n // 2, :], in0=do[:, :], scalar=gsub[:, 0:1],
                                             in1=dsq[:, :], op0=ALU.mult, op1=ALU.mult).then_inc(S("dout"), 1)


def up_phase(K):
    nc, ins, bank, V, sbt, h, ff = (K[n] for n in ("nc", "ins", "bank", "V", "sbt", "h", "ff"))
    JOBS = 4
    with ExitStack() as ctx:
        S = Sems(nc, ctx, "up")
        raw = sbt(ctx, "up_raw", [P, 2, DC * P])
        w_hi, w_lo = (sbt(ctx, "up" + n, [P, JOBS, DC * P], F32R) for n in ("_whi", "_wlo"))
        z = sbt(ctx, "up_z", [P, 2, T])
        u = sbt(ctx, "up_u", [P, 2, T])
        th, full, rstd = (sbt(ctx, "up_" + n, [P, T]) for n in ("th", "full", "rstd"))
        cols = sbt(ctx, "up_cols", [P, FC, 8])
        col = sbt(ctx, "up_col", [P, 2, 8])
        block = ctx.enter_context(nc.Block())

        def loop(eng, chunk):
            chunk(0, 0)
            chunk(1, 1)
            with eng.Fori(1, FC // 2 - 1) as i:
                chunk(2 * i, 0)
                chunk(2 * i + 1, 1)
            chunk(FC - 2, 0)
            chunk(FC - 1, 1)

        def splits(n):
            return not (isinstance(n, int) and n >= FC - 2)

        @block.sync
        def _(sp):
            def load(n, q):
                for g in range(2):
                    need(sp, S("wlo"), 2 * (n - 1) + g + 1)
                    sp.dma_start(raw[:, g, :], ins["w_up"][n, g]).then_inc(S(f"w{g}"), 16)

            loop(sp, load)

        @block.tensor
        def _(pe):
            def chunk(n, q):
                if isinstance(n, int) and n < 2:
                    if n == 0:
                        head_tensor(pe, S, K, bank, w_hi, w_lo)
                    return
                for g in range(2):
                    pe.wait_ge(S("wlo"), 2 * n + g + 1)
                    need(pe, S("u0"), 2 * (n - 1) + g - 1)
                    products(pe, bank[2 * q + g][:, :], w_hi[:, 2 * q + g, :], w_lo[:, 2 * q + g, :], h[0], h[1],
                             range(DC)).then_inc(S("mm"), 1)

            loop(pe, chunk)

        @block.scalar
        def _(act):
            def split(n, q, g):
                act.wait_ge(S(f"w{g}"), 16 * n + 16)
                need(act, S("mm"), 2 * (n - 2) + g + 1)
                act.activation(w_hi[:, 2 * q + g, :], raw[:, g, :], ACT.Copy).then_inc(S("whi"), 1)

            def keep(n):
                act.wait_ge(S("ff"), n + 1)
                act.activation(ff[0][:, n, :], full[:, :], ACT.Copy).then_inc(S("ff_hi"), 1)

            head_scalar(act, S, K, rstd[:, :], z, lambda j: split(j // 2, j // 2, j % 2))

            def chunk(n, q):
                act.wait_ge(S("col"), n + 1)
                for g in range(2):
                    act.wait_ge(S("mm"), 2 * n + g + 1)
                    need(act, S("tap1"), 2 * (n - 1) + g + 1)
                    act.activation(z[:, g, :], bank[2 * q + g][:, :], ACT.Copy).then_inc(S("z"), 1)
                    need(act, S("ff"), n)
                    act.activation(u[:, g, :], bank[2 * q + g][:, :], ACT.Identity, bias=col[:, q, 4 * g + 3:4 * g + 4],
                                   scale=col[:, q, 4 * g + 2:4 * g + 3]).then_inc(S("u0"), 1)
                act.wait_ge(S("tap1"), 2 * n + 1)
                act.activation(th[:, :], u[:, 0, :], ACT.Tanh, scale=0.5).then_inc(S("th"), 1)
                if splits(n):
                    split(n + 2, q, 0)
                    split(n + 2, q, 1)
                keep(n)

            loop(act, chunk)

        @block.vector
        def _(dve):
            for g in range(2):
                for k in range(3):
                    at = 2 * FC * k + FC * g
                    dve.tensor_copy(cols[:, :, 4 * g + k], V["conv_ff_w_2"][:, at:at + FC]).then_inc(S("cols"), 1)
                dve.tensor_copy(cols[:, :, 4 * g + 3], V["conv_ff_b_2"][:, FC * g:FC * (g + 1)]).then_inc(S("cols"), 1)
            dve.wait_ge(S("cols"), 8)

            def split(n, q, g):
                dve.wait_ge(S("whi"), 2 * n + g + 1)
                split_lo(dve, w_lo[:, 2 * q + g, :], raw[:, g, :], w_hi[:, 2 * q + g, :]).then_inc(S("wlo"), 1)

            def keep(n):
                dve.wait_ge(S("ff_hi"), n + 1)
                split_lo(dve, ff[1][:, n, :], full[:, :], ff[0][:, n, :]).then_inc(S("ff_lo"), 1)

            head_vector(dve, S, K, "norm2_g_2", rstd[:, :], z, lambda j: split(j // 2, j // 2, j % 2))

            def chunk(n, q):
                need(dve, S("u0"), 2 * (n - 1))
                need(dve, S("tap1"), 2 * (n - 1))
                dve.tensor_copy(col[:, q, :], cols[:, n, :]).then_inc(S("col"), 1)
                for g in range(2):
                    dve.wait_ge(S("u0"), 2 * n + g + 1)
                    if g == 0:
                        dve.wait_ge(S("col"), n + 1)
                    dve.scalar_tensor_tensor(out=u[:, g, 1:T], in0=z[:, g, 0:T - 1],
                                             scalar=col[:, q, 4 * g + 1:4 * g + 2], in1=u[:, g, 1:T],
                                             op0=ALU.mult, op1=ALU.add).then_inc(S("tap2"), 1)
                    dve.wait_ge(S("tap2"), 2 * n + g + 1)
                    dve.scalar_tensor_tensor(out=u[:, g, 2:T], in0=z[:, g, 0:T - 2],
                                             scalar=col[:, q, 4 * g:4 * g + 1], in1=u[:, g, 2:T],
                                             op0=ALU.mult, op1=ALU.add).then_inc(S("tap1"), 1)
                dve.wait_ge(S("th"), n + 1)
                dve.scalar_tensor_tensor(out=u[:, 0, :], in0=th[:, :], scalar=1.0, in1=u[:, 0, :], op0=ALU.add,
                                         op1=ALU.mult).then_inc(S("silu"), 1)
                dve.wait_ge(S("silu"), n + 1)
                need(dve, S("ff_lo"), n)
                dve.scalar_tensor_tensor(out=full[:, :], in0=u[:, 0, :], scalar=0.5, in1=u[:, 1, :], op0=ALU.mult,
                                         op1=ALU.mult).then_inc(S("ff"), 1)
                if splits(n):
                    split(n + 2, q, 0)
                    split(n + 2, q, 1)
                keep(n)

            loop(dve, chunk)


def tiles(w):
    k, n = w.shape
    return np.ascontiguousarray(w.reshape(k // P, P, n // P, P).transpose(2, 1, 0, 3)).reshape(n // P, P, k)


def layout(inputs):
    a = {k: np.asarray(v) for k, v in inputs.items()}
    o = {"consts": constants(), "distance": distances()}
    a["subln_g_2"] = np.tile(a["subln_g_2"], (1, 2))
    vec = lambda n: a[n].reshape(-1, P).T
    o["params"] = np.ascontiguousarray(np.concatenate([vec(n) for n, _ in PARAMS], 1))
    o["x"] = np.ascontiguousarray(a["x"][0].T.reshape(DC, P, T).transpose(1, 0, 2))
    lora = np.concatenate([a["a_w1"][0], a["a_a1"][0]], 1)
    o["lora1"] = np.ascontiguousarray(lora.reshape(DC, P, P).transpose(1, 0, 2))
    lora = np.concatenate([a["a_w2"][0], a["a_a2"][0]], 0)
    o["lora2"] = np.ascontiguousarray(lora.reshape(P, IC, P).transpose(1, 0, 2))
    for n, name in enumerate("rkvg"):
        o["w_" + name] = tiles(a["a_w_in"][0, n])
    o["w_out1"] = tiles(a["a_w_out"][0])
    cbug = tiles(a["b_w_in"][0]).reshape(4, IC, P, D)
    o["w_conv"] = np.ascontiguousarray(cbug[[2, 0, 3, 1]].transpose(1, 0, 2, 3))
    o["w_out2"] = tiles(a["b_w_out"][0])
    o["w_in2"] = tiles(a["w_in_2"][0][:, IN_ORDER])
    o["w_lru"] = np.ascontiguousarray(np.stack([a["w_rgate_2"][0], a["w_igate_2"][0]]).reshape(2, 4, 2, HD, HD)
                                      .transpose(2, 3, 0, 1, 4)).reshape(P, 2, 4, HD)
    o["lam"] = np.ascontiguousarray(np.stack([a[n][0] for n in ("lam_q1_2", "lam_k1_2", "lam_q2_2", "lam_k2_2")]))
    o["w_out3"] = tiles(a["w_out_2"][0])
    up = tiles(a["w_ff_up_2"][0]).reshape(2, FC, P, D)
    o["w_up"] = np.ascontiguousarray(up.transpose(1, 0, 2, 3))
    o["w_down"] = tiles(a["w_ff_down_2"][0])
    return o


def kernel(**inputs):
    import concourse.bacc as bacc
    from concourse.bass_utils import run_bass_kernel_spmd

    nc = bacc.Bacc("TRN2", target_bir_lowering=False, num_devices=1)
    arrays = layout(inputs)
    ins = {n: nc.dram_tensor(f"in_{n}", a.shape, F32, kind="ExternalInput").ap() for n, a in arrays.items()}
    out = nc.dram_tensor("out_y", (P, DC, T), F32, kind="ExternalOutput").ap()
    program(nc, ins, out)
    r = run_bass_kernel_spmd(nc, [{f"in_{n}": a for n, a in arrays.items()}], core_ids=[0])
    y = r.results[0]["out_y"]
    return np.ascontiguousarray(y.transpose(2, 1, 0).reshape(1, T, D))
```
